# Optimizing a Trainium2 kernel written in Bass

```python
import jax, jax.numpy as jnp
from jax import lax
import numpy as np

D_MODEL = 1024
BATCH = 1
SEQ = 256
DEPTH = 1
DEC_BATCH = 1
DEC_SEQ = 32
PAST_LEN = 256

CHUNK = 64
Q_BLOCK = 128
ATT_WIDTH = D_MODEL // 2
HEAD_DIM = 64
N_HEADS = ATT_WIDTH // HEAD_DIM
IDX_HEADS = 8
IDX_DIM = 64
TOPK_MAX = 256
POOL_WIDTH = D_MODEL - ATT_WIDTH
POOL_WINDOWS = (2, 4, 8, 16)
POOL_GROUPS = 4
POOL_GROUP_WIDTH = POOL_WIDTH // POOL_GROUPS
POOL_PAST = 15
N_EXPERTS = 32
TOP_K = 4
D_FF = D_MODEL
SWIGLU_LIMIT = 7.0
SWIGLU_ALPHA = 1.702
LN_EPS = 1e-5
DEEPNORM_ALPHA = (2 * DEPTH) ** 0.25
DEEPNORM_BETA = (8 * DEPTH) ** -0.25
Q_OFF = 0
K_OFF = Q_OFF + N_HEADS * HEAD_DIM
V_OFF = K_OFF + HEAD_DIM
QI_OFF = V_OFF + HEAD_DIM
KI_OFF = QI_OFF + IDX_HEADS * IDX_DIM
WI_OFF = KI_OFF + IDX_DIM
U_OFF = WI_OFF + IDX_HEADS
IN_COLS = U_OFF + POOL_WIDTH

kernel_name = "hymba_dsa_pool_moe_deepnorm_stream"

def _layer_norm(x, g, b):
    xf = x.astype(jnp.float32)
    mu = jnp.mean(xf, axis=-1, keepdims=True)
    xc = xf - mu
    var = jnp.mean(xc * xc, axis=-1, keepdims=True)
    y = xc * lax.rsqrt(var + LN_EPS)
    return (y * g.astype(jnp.float32) + b.astype(jnp.float32)).astype(x.dtype)

def _split_proj(h, w_in):
    B, T, _ = h.shape
    p = h @ w_in
    q = p[..., Q_OFF:K_OFF].reshape(B, T, N_HEADS, HEAD_DIM)
    k = p[..., K_OFF:V_OFF]
    v = p[..., V_OFF:QI_OFF]
    qi = p[..., QI_OFF:KI_OFF].reshape(B, T, IDX_HEADS, IDX_DIM)
    ki = p[..., KI_OFF:WI_OFF]
    wi = p[..., WI_OFF:U_OFF]
    u = p[..., U_OFF:IN_COLS]
    return q, k, v, qi, ki, wi, u

def _dsa_attend(q, wi, qi, q_pos, k_all, v_all, ki_all, k_pos, topk):
    idx_logits = jnp.einsum('bqhd,bld->bqhl', qi, ki_all).astype(jnp.float32) * (IDX_DIM ** -0.5)
    idx_w = wi.astype(jnp.float32) * (IDX_HEADS ** -0.5)
    score = jnp.einsum('bqh,bqhl->bql', idx_w, jax.nn.relu(idx_logits))
    visible = (k_pos[None, :] // CHUNK) <= (q_pos[:, None] // CHUNK)
    score = jnp.where(visible[None], score, -jnp.inf)
    _, sel = lax.top_k(score, topk)
    gather = jax.vmap(lambda rows, ids: rows[ids])
    k_sel = gather(k_all, sel)
    v_sel = gather(v_all, sel)
    sel_ok = (k_pos[sel] // CHUNK) <= (q_pos[None, :, None] // CHUNK)
    logits = jnp.einsum('bqhd,bqjd->bqhj', q, k_sel).astype(jnp.float32) * (HEAD_DIM ** -0.5)
    logits = jnp.where(sel_ok[:, :, None, :], logits, -jnp.inf)
    probs = jax.nn.softmax(logits, axis=-1).astype(v_sel.dtype)
    out = jnp.einsum('bqhj,bqjd->bqhd', probs, v_sel)
    return out.reshape(out.shape[0], out.shape[1], N_HEADS * HEAD_DIM)

def _dsa_prompt(q, wi, qi, k, v, ki, topk):
    B, S = q.shape[0], q.shape[1]
    nb = S // Q_BLOCK
    pos = jnp.arange(S, dtype=jnp.int32)

    def blocks(a):
        return jnp.moveaxis(a.reshape((B, nb, Q_BLOCK) + a.shape[2:]), 1, 0)

    def one_block(args):
        qb, wb, qib, pb = args
        return _dsa_attend(qb, wb, qib, pb, k, v, ki, pos, topk)

    out = lax.map(one_block, (blocks(q), blocks(wi), blocks(qi), pos.reshape(nb, Q_BLOCK)))
    return jnp.moveaxis(out, 0, 1).reshape(B, S, N_HEADS * HEAD_DIM)

def _pool_mix(u, prefix, pos, pool_w, pool_scale):
    B, T, C = u.shape
    P = prefix.shape[1]
    ext = jnp.concatenate([prefix, u], axis=1).astype(jnp.float32)
    cs = jnp.concatenate([jnp.zeros((B, 1, C), jnp.float32), jnp.cumsum(ext, axis=1)], axis=1)
    means = []
    for g, w in enumerate(POOL_WINDOWS):
        c0, c1 = g * POOL_GROUP_WIDTH, (g + 1) * POOL_GROUP_WIDTH
        wsum = cs[:, P + 1:P + 1 + T, c0:c1] - cs[:, P + 1 - w:P + 1 - w + T, c0:c1]
        count = jnp.minimum(w, pos + 1).astype(jnp.float32)
        means.append(wsum / count[None, :, None])
    diff = (jnp.concatenate(means, axis=-1) - u.astype(jnp.float32)).astype(u.dtype)
    diff = diff.reshape(B, T, POOL_GROUPS, POOL_GROUP_WIDTH)
    y = jnp.einsum('btgc,gcd->btgd', diff, pool_w).reshape(B, T, C)
    return y * pool_scale

def _moe(h, w_router, b_router, w1, b1, w2, b2):
    B, T, D = h.shape
    xt = h.reshape(B * T, D)
    logits = (xt @ w_router + b_router).astype(jnp.float32)
    top_val, top_idx = lax.top_k(logits, TOP_K)
    top_w = jax.nn.softmax(top_val, axis=-1)
    gates = jnp.einsum('nk,nke->ne', top_w, jax.nn.one_hot(top_idx, N_EXPERTS, dtype=jnp.float32)).astype(h.dtype)
    out = jnp.zeros_like(xt)
    for e in range(N_EXPERTS):
        gu = xt @ w1[e] + b1[e]
        gate = jnp.minimum(gu[:, :D_FF], SWIGLU_LIMIT)
        up = jnp.clip(gu[:, D_FF:], -SWIGLU_LIMIT, SWIGLU_LIMIT)
        act = (up + 1) * (gate * jax.nn.sigmoid(SWIGLU_ALPHA * gate))
        out = out + gates[:, e:e + 1] * (act @ w2[e] + b2[e])
    return out.reshape(B, T, D)

def _block_tail(h, att, pool, w_o, ln1_g, ln1_b, w_router, b_router, w1, b1, w2, b2, ln2_g, ln2_b):
    mix = jnp.concatenate([att, pool], axis=-1) @ w_o
    h1 = _layer_norm(DEEPNORM_ALPHA * h + mix, ln1_g, ln1_b)
    m = _moe(h1, w_router, b_router, w1, b1, w2, b2)
    return _layer_norm(DEEPNORM_ALPHA * h1 + m, ln2_g, ln2_b)

def setup_inputs(seed: int = 0) -> dict:
    key = jax.random.key(seed)
    ks = jax.random.split(key, 24)
    f32 = jnp.float32
    nrm = lambda k, shape: jax.random.normal(k, shape, f32)
    w_in = nrm(ks[7], (DEPTH, D_MODEL, IN_COLS)) * D_MODEL ** -0.5
    w_in = w_in.at[:, :, V_OFF:QI_OFF].multiply(DEEPNORM_BETA)
    return {
        'x_prompt': nrm(ks[0], (BATCH, SEQ, D_MODEL)),
        'x_sample': nrm(ks[1], (DEC_BATCH, DEC_SEQ, D_MODEL)),
        'cache_k': nrm(ks[2], (DEPTH, DEC_BATCH, PAST_LEN, HEAD_DIM)),
        'cache_v': nrm(ks[3], (DEPTH, DEC_BATCH, PAST_LEN, HEAD_DIM)),
        'cache_kidx': nrm(ks[4], (DEPTH, DEC_BATCH, PAST_LEN, IDX_DIM)),
        'state_pool': nrm(ks[5], (DEPTH, DEC_BATCH, POOL_PAST, POOL_WIDTH)),
        'ln0_g': 1.0 + 0.02 * nrm(ks[6], (D_MODEL,)),
        'ln0_b': 0.02 * nrm(ks[8], (D_MODEL,)),
        'w_in': w_in,
        'w_o': nrm(ks[9], (DEPTH, D_MODEL, D_MODEL)) * (D_MODEL ** -0.5) * DEEPNORM_BETA,
        'pool_w': nrm(ks[10], (DEPTH, POOL_GROUPS, POOL_GROUP_WIDTH, POOL_GROUP_WIDTH)) * POOL_GROUP_WIDTH ** -0.5,
        'pool_scale': 1.0 + 0.02 * nrm(ks[11], (DEPTH, POOL_WIDTH)),
        'ln1_g': 1.0 + 0.02 * nrm(ks[12], (DEPTH, D_MODEL)),
        'ln1_b': 0.02 * nrm(ks[13], (DEPTH, D_MODEL)),
        'w_router': nrm(ks[14], (DEPTH, D_MODEL, N_EXPERTS)) * D_MODEL ** -0.5,
        'b_router': 0.01 * nrm(ks[15], (DEPTH, N_EXPERTS)),
        'w1': nrm(ks[16], (DEPTH, N_EXPERTS, D_MODEL, 2 * D_FF)) * D_MODEL ** -0.5,
        'b1': 0.01 * nrm(ks[17], (DEPTH, N_EXPERTS, 2 * D_FF)),
        'w2': nrm(ks[18], (DEPTH, N_EXPERTS, D_FF, D_MODEL)) * (D_FF ** -0.5) * DEEPNORM_BETA,
        'b2': 0.01 * nrm(ks[19], (DEPTH, N_EXPERTS, D_MODEL)),
        'ln2_g': 1.0 + 0.02 * nrm(ks[20], (DEPTH, D_MODEL)),
        'ln2_b': 0.02 * nrm(ks[21], (DEPTH, D_MODEL)),
    }

def reference(x_prompt, x_sample, cache_k, cache_v, cache_kidx, state_pool, ln0_g, ln0_b, w_in, w_o,
              pool_w, pool_scale, ln1_g, ln1_b, w_router, b_router, w1, b1, w2, b2, ln2_g, ln2_b):
    hp = _layer_norm(x_prompt, ln0_g, ln0_b)
    hs = _layer_norm(x_sample, ln0_g, ln0_b)
    Bp, S = hp.shape[0], hp.shape[1]
    T = hs.shape[1]
    L_past = cache_k.shape[2]
    topk_p = min(TOPK_MAX, S // 4)
    topk_s = min(TOPK_MAX, (L_past + T) // 4)
    pos_p = jnp.arange(S, dtype=jnp.int32)
    pos_s = L_past + jnp.arange(T, dtype=jnp.int32)
    pos_all = jnp.arange(L_past + T, dtype=jnp.int32)
    kp_l, vp_l, kip_l, pp_l, ks_l, vs_l, kis_l, ps_l = [], [], [], [], [], [], [], []
    for l in range(DEPTH):
        tail = (w_o[l], ln1_g[l], ln1_b[l], w_router[l], b_router[l], w1[l], b1[l], w2[l], b2[l], ln2_g[l], ln2_b[l])
        qp, kp, vp, qip, kip, wip, up = _split_proj(hp, w_in[l])
        att_p = _dsa_prompt(qp, wip, qip, kp, vp, kip, topk_p)
        zero_prefix = jnp.zeros((Bp, POOL_PAST, POOL_WIDTH), up.dtype)
        pool_p = _pool_mix(up, zero_prefix, pos_p, pool_w[l], pool_scale[l])
        kp_l.append(kp)
        vp_l.append(vp)
        kip_l.append(kip)
        pp_l.append(jnp.concatenate([zero_prefix, up], axis=1)[:, -POOL_PAST:])
        hp = _block_tail(hp, att_p, pool_p, *tail)
        qs, kn, vn, qis, kin, wis, us = _split_proj(hs, w_in[l])
        k_all = jnp.concatenate([cache_k[l], kn], axis=1)
        v_all = jnp.concatenate([cache_v[l], vn], axis=1)
        ki_all = jnp.concatenate([cache_kidx[l], kin], axis=1)
        att_s = _dsa_attend(qs, wis, qis, pos_s, k_all, v_all, ki_all, pos_all, topk_s)
        pool_s = _pool_mix(us, state_pool[l], pos_s, pool_w[l], pool_scale[l])
        ks_l.append(kn)
        vs_l.append(vn)
        kis_l.append(kin)
        ps_l.append(jnp.concatenate([state_pool[l], us], axis=1)[:, -POOL_PAST:])
        hs = _block_tail(hs, att_s, pool_s, *tail)
    return (hp, hs, jnp.stack(kp_l), jnp.stack(vp_l), jnp.stack(kip_l), jnp.stack(pp_l),
            jnp.stack(ks_l), jnp.stack(vs_l), jnp.stack(kis_l), jnp.stack(ps_l))


_drawn_inputs = setup_inputs


def setup_inputs(seed=0):
    import zlib

    import numpy as np

    out = dict(_drawn_inputs(seed))
    spreads = {}
    factors = {'pool_scale': 3.45,
     'b_router': 3.426,
     'b1': 8.0,
     'b2': 8.0,
     'ln2_g': 2.946,
     'ln2_b': 2.749}
    for name, (base, spread) in spreads.items():
        noise = np.random.default_rng([zlib.crc32(name.encode()), seed]).standard_normal(out[name].shape)
        drawn = base * np.exp(spread * noise) if base else spread * noise
        out[name] = __import__('jax').numpy.asarray(drawn.astype(out[name].dtype))
    for name, factor in factors.items():
        out[name] = (out[name] * factor).astype(out[name].dtype)
    return out
```

```python
from contextlib import ExitStack

import concourse.bass as bass
from concourse import mybir

F32 = mybir.dt.float32
BF16 = mybir.dt.bfloat16
I32 = mybir.dt.int32
U32 = mybir.dt.uint32
ALU = mybir.AluOpType
ACT = mybir.ActivationFunctionType
AX = mybir.AxisListType.X

P = 128
CHUNK = 64
HEAD_DIM = 64
N_HEADS = 8
POOL_PAST = 15
WINDOWS = (2, 4, 8, 16)
TOP_K = 4
LIMIT = 7.0
SWIGLU_ALPHA = 1.702
LN_EPS = 1e-5
RESIDUAL = 2.0 ** 0.25
HIDDEN_KEY = -1.0e30
TAKEN = -3.0e38
BLK = 64


def encoder_kernel(nc, ins, outs):
    (x_prompt, x_sample, cache_k, cache_v, cache_kidx, state_pool, ln0_g, ln0_b, w_in, w_o, pool_w,
     pool_scale, ln1_g, ln1_b, w_router, b_router, w1, b1, w2, b2, ln2_g, ln2_b) = ins
    (y_prompt, y_sample, k_prompt, v_prompt, kidx_prompt, pool_prompt,
     k_sample, v_sample, kidx_sample, pool_sample) = outs

    S, D = x_prompt.shape[1:]
    TS = x_sample.shape[1]
    PAST = cache_k.shape[2]
    NE = w_router.shape[2]
    F = w2.shape[2]
    IN = w_in.shape[2]
    KT = D // P
    TOK = S + TS
    NT = 3
    TOKP = NT * P
    tiles = [(0, P, P), (P, P, 2 * P), (S, TS, PAST + TS)]
    topk = [min(256, S // 4)] * 2 + [min(256, (PAST + TS) // 4)]
    assert (S, TS, D, F, PAST, KT) == (2 * P, 32, 1024, 1024, 2 * P, 8)
    K_OFF = N_HEADS * HEAD_DIM
    QI_OFF = K_OFF + 2 * HEAD_DIM
    KI_OFF = QI_OFF + N_HEADS * HEAD_DIM
    U_OFF = KI_OFF + HEAD_DIM + N_HEADS
    KW = HEAD_DIM + N_HEADS
    LAST_BLK = -(-TOK // BLK)
    SLOT = 2 * 2 * F
    NSLOT = 6
    UW = POOL_PAST + S + POOL_PAST + TS
    U_S = POOL_PAST + S

    with ExitStack() as ctx:
        def sb(name, shape, dt=F32):
            return ctx.enter_context(nc.sbuf_tensor(name, shape, dt))

        def sem(name):
            return ctx.enter_context(nc.semaphore(name))

        ring = sb("ring", [P, NSLOT, SLOT])
        area = sb("area", [P, KT * IN])
        rows = sb("rows", [P, NT, D])
        tokT = sb("tokT", [P, KT, TOK])
        lnb = sb("lnb", [P, 2, D])
        uext = sb("uext", [P, 4, UW])
        diffT = sb("diffT", [P, 4, TOK])
        kv_rows = sb("kv_rows", [P, NT, P + KW])
        score = sb("score", [P, NT, 288])
        pool_w_sb = sb("pool_w_sb", [P, 4, P])
        w_router_sb = sb("w_router_sb", [P, KT, NE])
        b_router_sb = sb("b_router_sb", [P, NE])
        pool_scale_sb = sb("pool_scale_sb", [P, 4])
        narrow = sb("narrow", [P, D])
        b2_sb = narrow[0:NE, :]
        last_u = narrow[32:32 + POOL_PAST, :].rearrange("p (s c) -> p s c", s=2)
        state_rows = narrow[64:64 + POOL_PAST, 0:4 * P]
        ident_state = slice(64, 64 + POOL_PAST)
        ident = sb("ident", [P, P])
        iota_slot = sb("iota_slot", [P, LAST_BLK * BLK])
        iota_exp = sb("iota_exp", [P, NE])
        before = sb("before", [P, P], BF16)
        ones_b = sb("ones_b", [P, P], BF16)
        ones_row = sb("ones_row", [1, BLK])
        stats = sb("stats", [P, NT, 2, 6])
        moments = sb("moments", [P, NT, 2])
        veps = sb("veps", [P, NT])
        std = sb("std", [P, NT])
        rstd = sb("rstd", [P, NT])
        w_idx = sb("w_idx", [P, NT, N_HEADS])
        max8 = sb("max8", [P, NT, 8])
        row_max = sb("row_max", [P, NT, N_HEADS])
        neg_max = sb("neg_max", [P, NT, N_HEADS])
        row_sum = sb("row_sum", [P, NT, N_HEADS])
        row_inv = sb("row_inv", [P, NT, N_HEADS])
        logits = sb("logits", [P, NT, NE])
        top8 = sb("top8", [P, NT, 8])
        top_i = sb("top_i", [P, NT, 8], U32)
        top_f = sb("top_f", [P, NT, TOP_K])
        top_w = sb("top_w", [P, NT, TOP_K])
        top_s = sb("top_s", [P, NT])
        top_r = sb("top_r", [P, NT])
        flat = score[:, :, :].rearrange("p t n -> p (t n)")
        n_hot = NT * TOP_K * NE
        onehot = flat[:, 0:n_hot].rearrange("p (t k e) -> p t k e", t=NT, k=TOP_K)
        weighed = flat[:, n_hot:2 * n_hot].rearrange("p (t k e) -> p t k e", t=NT, k=TOP_K)
        chosen = sb("chosen", [P, NT, NE])
        chosen_b = sb("chosen_b", [P, NT, NE], BF16)
        gate_w = sb("gate_w", [P, NT, NE])
        place = sb("place", [P, NT, NE + 1])
        blocks_f = sb("blocks_f", [1, 3, NE])
        blocks_i = sb("blocks_i", [1, 2, NE], I32)

        w_in_sb = area[:, :].rearrange("p (j n) -> p j n", j=KT)
        w_o_sb = area[:, 0:KT * D].rearrange("p (k n) -> p k n", k=KT)
        out_acc = area[:, KT * D:KT * D + NT * D].rearrange("p (t n) -> p t n", t=NT)
        sums_a = area[:, KT * D:KT * D + 4 * UW].rearrange("p (g n) -> p g n", g=4)
        sums_b = area[:, KT * D + 4 * UW:KT * D + 8 * UW].rearrange("p (g n) -> p g n", g=4)
        PR = KT * D + NT * D
        probs = area[:, PR:PR + 8 * 288]

        spare = ring[:, 4:6, :].rearrange("p s n -> p (s n)")
        used = [0]

        def carve(base, n):
            at = used[0]
            used[0] += n
            return base[:, at:at + n]

        qT = carve(spare, 4 * TOK).rearrange("p (i t) -> p i t", i=4)
        qiT = carve(spare, 4 * TOK).rearrange("p (i t) -> p i t", i=4)
        kT2 = carve(spare, S + PAST + TS)
        kiT2 = carve(spare, S + PAST + TS)
        kvT = carve(spare, TOK)
        kwT = carve(spare, TOK)
        relu_sb = carve(spare, 4 * 288).rearrange("p (b h n) -> p b h n", b=2, h=2)
        probsT = carve(spare, 2 * 8 * P)
        att_rows = carve(spare, N_HEADS * HEAD_DIM)
        cache_rows = carve(spare, 2 * P).rearrange("p (c d) -> p c d", c=2)
        cache_vr = carve(spare, 2 * HEAD_DIM).rearrange("p (c d) -> p c d", c=2)
        rcount = carve(spare, 4 * 16).rearrange("p (g n) -> p g n", g=4)
        assert used[0] <= 2 * SLOT

        used[0] = 0
        b1_sb = carve(area, 2 * F)
        xT = carve(area, KT * BLK).rearrange("p (k s) -> p k s", k=KT)
        pick = carve(area, NT * BLK).rearrange("p (t s) -> p t s", t=NT)
        give = carve(area, NT * 2 * BLK).rearrange("p (t h s) -> p t h s", t=NT, h=2)
        giveT = carve(area, TOKP)
        g_sb = carve(area, F // 2)
        u_sb = carve(area, F // 2)
        sig_sb = carve(area, F // 2)
        h_sb = carve(area, F // 2)
        hT = carve(area, 4 * P).rearrange("p (c h s) -> p c h s", c=4, h=2)
        y_sb = carve(area, D // 2)
        assert used[0] <= KT * D
        used[0] = PR
        x_xT = carve(area, KT * BLK).rearrange("p (k s) -> p k s", k=KT)
        x_pick = carve(area, NT * BLK).rearrange("p (t s) -> p t s", t=NT)
        x_give = carve(area, NT * 2 * BLK).rearrange("p (t h s) -> p t h s", t=NT, h=2)
        x_giveT = carve(area, TOKP)
        x_y = carve(area, D // 2)
        gateT = carve(area, TOK)[0:NE, :]
        assert used[0] <= KT * IN

        ps = ctx.enter_context(nc.psum_tensor("ps", [P, 8, 512], F32))
        ps_gu = ps[:, 0:2, :]
        ps_x = ps[:, 2, :].rearrange("p (k s) -> p k s", k=KT)
        ps_hT = ps[:, 3, :]
        ps_y = ps[:, 4, :]
        ps_c = ps[:, 5:7, :]
        ps_g = ps[:, 7, 0:TOKP]

        zero_rows = sem("zero_rows")
        ident0 = sem("ident0")
        before0 = sem("before0")
        ident_ready = sem("ident_ready")
        const_ready = sem("const_ready")
        pool_step = sem("pool_step")
        x_in = [sem(f"x_in{t}") for t in range(2)]
        ln_in = [sem(f"ln_in{i}") for i in range(3)]
        w_in_in = [sem(f"w_in_in{i}") for i in range(3)]
        cache_in = sem("cache_in")
        small_in = sem("small_in")
        state_in = sem("state_in")
        w_o_in = sem("w_o_in")
        w_in_slot = [sem(f"w_slot{s}") for s in range(NSLOT)]
        b1_in = sem("b1_in")
        rows_out = sem("rows_out")
        final_out = sem("final_out")
        dve_step = sem("dve_step")
        var_ready = sem("var_ready")
        std_ready = sem("std_ready")
        ln_done = sem("ln_done")
        tokT_ps = sem("tokT_ps")
        tokT_sb = sem("tokT_sb")
        proj_ps = sem("proj_ps")
        proj_sb = sem("proj_sb")
        cacheT_ps = sem("cacheT_ps")
        cacheT_sb = sem("cacheT_sb")
        kvrow_ps = sem("kvrow_ps")
        kvrow_sb = sem("kvrow_sb")
        idx_ps = sem("idx_ps")
        idx_relu = sem("idx_relu")
        idx_used = sem("idx_used")
        pool_diff = sem("pool_diff")
        lastu_ps = sem("lastu_ps")
        lastu_sb = sem("lastu_sb")
        stateT_ps = sem("stateT_ps")
        stateT_sb = sem("stateT_sb")
        poolmm_ps = sem("poolmm_ps")
        poolT_sb = sem("poolT_sb")
        qk_ps = sem("qk_ps")
        qk_used = sem("qk_used")
        max_ready = sem("max_ready")
        exp_done = sem("exp_done")
        probsT_ps = sem("probsT_ps")
        probsT_sb = sem("probsT_sb")
        pv_ps = sem("pv_ps")
        att_ready = sem("att_ready")
        attT_ps = sem("attT_ps")
        attT_sb = sem("attT_sb")
        wo_ps = sem("wo_ps")
        h1T_ps = sem("h1T_ps")
        h1T_sb = sem("h1T_sb")
        router_ps = sem("router_ps")
        top_ready = sem("top_ready")
        top_exp = sem("top_exp")
        gates_ready = sem("gates_ready")
        prefix_ps = sem("prefix_ps")
        blocks_ready = sem("blocks_ready")
        gateT_ps = sem("gateT_ps")
        gateT_sb = sem("gateT_sb")
        b2_ps = sem("b2_ps")
        acc_init = sem("acc_init")
        slot_free = [sem(f"slot_free{s}") for s in range(NSLOT)]
        b1_free = sem("b1_free")
        pick_ready = sem("pick_ready")
        x_gathered = sem("x_gathered")
        xT_ready = sem("xT_ready")
        gu_done = sem("gu_done")
        gate_ready = sem("gate_ready")
        sig_ready = sem("sig_ready")
        up_ready = sem("up_ready")
        prod_ready = sem("prod_ready")
        h_ready = sem("h_ready")
        hT_done = sem("hT_done")
        hT_ready = sem("hT_ready")
        y_done = sem("y_done")
        y_ready = sem("y_ready")
        give_ready = sem("give_ready")
        giveT_done = sem("giveT_done")
        giveT_ready = sem("giveT_ready")
        comb_done = [sem(f"comb_done{t}") for t in range(NT)]
        acc_done = [sem(f"acc_done{t}") for t in range(NT)]
        x_pick_ready = sem("x_pick_ready")
        x_x_gathered = sem("x_x_gathered")
        x_xT_ready = sem("x_xT_ready")
        x_gu_done = sem("x_gu_done")
        x_gate_ready = sem("x_gate_ready")
        x_sig_ready = sem("x_sig_ready")
        x_up_ready = sem("x_up_ready")
        x_prod_ready = sem("x_prod_ready")
        x_h_ready = sem("x_h_ready")
        x_hT_done = sem("x_hT_done")
        x_hT_ready = sem("x_hT_ready")
        x_y_done = sem("x_y_done")
        x_y_ready = sem("x_y_ready")
        x_giveT_done = sem("x_giveT_done")
        x_giveT_ready = sem("x_giveT_ready")
        x_comb_done = [sem(f"x_comb_done{t}") for t in range(NT)]
        x_acc_done = [sem(f"x_acc_done{t}") for t in range(NT)]

        def broadcast_row(ap):
            return ap.rearrange("(a n) -> a n", a=1).partition_broadcast(P) if len(ap.shape) == 1 \
                else ap.partition_broadcast(P)

        w1_v = w1[0].rearrange("e (p k) n -> e p (k n)", k=KT)
        w2_v = w2[0].rearrange("e (h p c) n -> e h p (c n)", h=2, c=4)
        w1_t = ring[:, 0:4, :].rearrange("p s (k n) -> p (s k) n", k=2)
        w2_t = ring[:, 4:6, :].rearrange("p s (c n) -> p s c n", c=4)
        b1_v = b1[0]
        x_views = [x_prompt[0].rearrange("(t p) d -> p t d", p=P), x_sample[0]]
        order = [(KI_OFF, KW)] + [(QI_OFF + P * i, P) for i in range(4)] + [(K_OFF, P)] \
            + [(P * i, P) for i in range(4)] + [(U_OFF + P * i, P) for i in range(4)]
        chunk_of = [0] * 5 + [1] * 5 + [2] * 4
        chunks = [(QI_OFF, U_OFF), (0, QI_OFF), (U_OFF, IN)]
        PB = 4

        block = ctx.enter_context(nc.Block())

        @block.sync
        def _(sp):
            sp.dma_start(rows[:, 0:2, :], x_views[0]).then_inc(x_in[0], 16)
            sp.wait_ge(zero_rows, 1)
            sp.dma_start(rows[0:TS, 2, :], x_views[1]).then_inc(x_in[1], 16)
            sp.dma_start(lnb[:, 0, :], ln0_g.partition_broadcast(P)).then_inc(ln_in[0], 16)
            sp.dma_start(lnb[:, 1, :], ln0_b.partition_broadcast(P)).then_inc(ln_in[0], 16)
            w_in_v = w_in[0].rearrange("(p j) n -> p j n", j=KT)
            for i, (a, b) in enumerate(chunks):
                sp.dma_start(w_in_sb[:, :, a:b], w_in_v[:, :, a:b]).then_inc(w_in_in[i], 16)
                if i == 0:
                    sp.dma_start(cache_rows[:, :, 0:HEAD_DIM],
                                 cache_k[0, 0].rearrange("(c p) d -> p c d", p=P)).then_inc(cache_in, 16)
                    sp.dma_start(cache_rows[:, :, HEAD_DIM:P],
                                 cache_kidx[0, 0].rearrange("(c p) d -> p c d", p=P)).then_inc(cache_in, 16)
                    sp.dma_start(cache_vr[:, :, :],
                                 cache_v[0, 0].rearrange("(c p) d -> p c d", p=P)).then_inc(cache_in, 16)
                    sp.dma_start(state_rows[:, :], state_pool[0, 0]).then_inc(state_in, 16)
            sp.dma_start(pool_w_sb[:, :, :], pool_w[0].rearrange("g c d -> c g d")).then_inc(small_in, 16)
            sp.dma_start(pool_scale_sb[:, :], pool_scale[0].rearrange("(g p) -> p g", p=P),
                         allow_slow_non_contiguous=True).then_inc(small_in, 16)
            sp.dma_start(w_router_sb[:, :, :], w_router[0].rearrange("(p j) n -> p j n", j=KT)).then_inc(small_in, 16)
            sp.dma_start(b_router_sb[:, :], b_router[0].partition_broadcast(P)).then_inc(small_in, 16)
            sp.dma_start(b2_sb[:, :], b2[0]).then_inc(small_in, 16)
            for s in range(4):
                sp.dma_start(ring[:, s, :], w1_v[0, :, s * SLOT:(s + 1) * SLOT]).then_inc(w_in_slot[s], 16)
            sp.wait_ge(ln_done, NT)
            sp.dma_start(lnb[:, 0, :], ln1_g[0].partition_broadcast(P)).then_inc(ln_in[1], 16)
            sp.dma_start(lnb[:, 1, :], ln1_b[0].partition_broadcast(P)).then_inc(ln_in[1], 16)
            sp.wait_ge(proj_ps, len(order))
            sp.dma_start(w_o_sb, w_o[0].rearrange("(k p) n -> p k n", p=P)).then_inc(w_o_in, 16)
            sp.wait_ge(attT_ps, NT)
            sp.wait_ge(att_ready, NT)
            for h in range(2):
                sp.dma_start(ring[:, 4 + h, :], w2_v[0, h]).then_inc(w_in_slot[4 + h], 16)
            sp.wait_ge(wo_ps, NT)
            sp.dma_start(b1_sb[0:1, :], b1_v[0:1, :]).then_inc(b1_in, 16)
            sp.wait_ge(ln_done, 2 * NT)
            sp.dma_start(lnb[:, 0, :], ln2_g[0].partition_broadcast(P)).then_inc(ln_in[2], 16)
            sp.dma_start(lnb[:, 1, :], ln2_b[0].partition_broadcast(P)).then_inc(ln_in[2], 16)
            with sp.Fori(1, NE) as e:
                sp.wait_ge(b1_free, e)
                sp.dma_start(b1_sb[0:1, :], b1_v[bass.ds(e, 1), :]).then_inc(b1_in, 16)
                for s in range(4):
                    sp.wait_ge(slot_free[s], e)
                    sp.dma_start(ring[:, s, :], w1_v[bass.ds(e, 1), :, s * SLOT:(s + 1) * SLOT]
                                 .rearrange("e p n -> p (e n)")).then_inc(w_in_slot[s], 16)
                for h in range(2):
                    sp.wait_ge(slot_free[4 + h], e)
                    sp.dma_start(ring[:, 4 + h, :], w2_v[bass.ds(e, 1), h]
                                 .rearrange("e p n -> p (e n)")).then_inc(w_in_slot[4 + h], 16)

        @block.gpsimd
        def _(pool):
            nc.gpsimd.memset(rows[:, 2, :], 0.0).then_inc(zero_rows, 1)
            nc.gpsimd.memset(ident[:, :], 0.0).then_inc(ident0, 1)
            pool.wait_ge(ident0, 1)
            nc.gpsimd.affine_select(out=ident[:, :], in_=ident[:, :], compare_op=ALU.not_equal, fill=1.0, base=0,
                                    pattern=[[-1, P]], channel_multiplier=1).then_inc(ident_ready, 1)
            nc.gpsimd.memset(before[:, :], 0.0).then_inc(before0, 1)
            pool.wait_ge(before0, 1)
            nc.gpsimd.affine_select(out=before[:, :], in_=before[:, :], compare_op=ALU.is_ge, fill=1.0, base=0,
                                    pattern=[[-1, P]], channel_multiplier=1).then_inc(const_ready, 1)
            nc.gpsimd.memset(ones_b[:, :], 1.0).then_inc(const_ready, 1)
            nc.gpsimd.memset(ones_row[:, :], 1.0).then_inc(const_ready, 1)
            nc.gpsimd.memset(logits[:, :, :], 0.0).then_inc(const_ready, 1)
            nc.gpsimd.iota(iota_slot[:, :], [[1, LAST_BLK * BLK]], base=0, channel_multiplier=0,
                           allow_small_or_imprecise_dtypes=True).then_inc(const_ready, 1)
            nc.gpsimd.iota(iota_exp[:, :], [[1, NE]], base=0, channel_multiplier=0,
                           allow_small_or_imprecise_dtypes=True).then_inc(const_ready, 1)
            nc.gpsimd.iota(rcount[:, :, :], [[0, 4], [1, 16]], base=1, channel_multiplier=0,
                           allow_small_or_imprecise_dtypes=True).then_inc(const_ready, 1)
            nc.gpsimd.memset(uext[:, :, 0:POOL_PAST], 0.0).then_inc(const_ready, 1)
            pool.wait_ge(proj_sb, len(order))
            pool.wait_ge(stateT_sb, 1)
            pool.wait_ge(proj_ps, len(order))
            src, dst, step = uext, sums_a, 0
            for level in range(4):
                back = 1 << level
                a = 2 * back - 1
                nc.gpsimd.tensor_tensor(dst[:, level:4, a:UW], src[:, level:4, a:UW],
                                        src[:, level:4, a - back:UW - back], ALU.add).then_inc(pool_step, 1)
                step += 1
                pool.wait_ge(pool_step, step)
                src, dst = dst, (sums_b if dst is sums_a else sums_a)

            pool.wait_ge(kvrow_sb, 2)
            for t in range(2):
                for off, dram in ((0, k_prompt), (HEAD_DIM, v_prompt), (P, kidx_prompt)):
                    pool.dma_start(dram[0, 0, t * P:(t + 1) * P, :],
                                   kv_rows[:, t, off:off + HEAD_DIM]).then_inc(rows_out, 16)
            for off, dram in ((0, k_sample), (HEAD_DIM, v_sample), (P, kidx_sample)):
                pool.dma_start(dram[0, 0], kv_rows[0:TS, 2, off:off + HEAD_DIM]).then_inc(rows_out, 16)
            pool.wait_ge(lastu_sb, 1)
            pool.dma_start(pool_prompt[0, 0], last_u[:, 0, :]).then_inc(rows_out, 16)
            pool.dma_start(pool_sample[0, 0], last_u[:, 1, :]).then_inc(rows_out, 16)
            pool.wait_ge(rows_out, 16 * 11)

        @block.tensor
        def _(pe):
            mm = nc.tensor.matmul
            tr = nc.tensor.transpose

            def rows_to_tokT(done, ready, base):
                for t, (t0, n, _) in enumerate(tiles):
                    pe.wait_ge(done, base + t + 1)
                    for j in range(KT):
                        last = tr(ps[:, t * 2 + j // 4 if t < 2 else 4, (j % 4) * P:(j % 4) * P + n] if t < 2 else
                                  ps[:, 4, j * TS:(j + 1) * TS],
                                  rows[0:n, t, j:D:KT], ident[0:n, 0:n])
                        if t < 2 and j % 4 == 3:
                            last.then_inc(ready, 1)
                    if t == 2:
                        last.then_inc(ready, 1)

            pe.wait_ge(ident_ready, 1)
            rows_to_tokT(ln_done, tokT_ps, 0)

            def project(i):
                c0, w = order[i]
                pe.wait_ge(w_in_in[chunk_of[i]], 16)
                if i == 0:
                    pe.wait_ge(tokT_sb, 5)
                if i >= 4:
                    pe.wait_ge(proj_sb, i - 3)
                for j in range(KT):
                    last = mm(ps[0:w, PB + i % 4, 0:TOK], w_in_sb[:, j, c0:c0 + w], tokT[:, j, :],
                              start=(j == 0), stop=(j == KT - 1))
                last.then_inc(proj_ps, 1)

            for i in range(6):
                project(i)
            pe.wait_ge(cache_in, 48)
            for c in range(2):
                last = tr(ps[:, 0, c * P:(c + 1) * P], cache_rows[:, c, :], ident[:, :])
            last.then_inc(cacheT_ps, 1)
            pe.wait_ge(proj_sb, 6)
            for t, (t0, n, _) in enumerate(tiles):
                bank, at = (1, t * (P + KW)) if t < 2 else (2, 0)
                tr(ps[0:n, bank, at:at + P], kvT[:, t0:t0 + n], ident[:, :])
                last = tr(ps[0:n, bank, at + P:at + P + KW], kwT[0:KW, t0:t0 + n], ident[0:KW, 0:KW])
                if t >= 1:
                    last.then_inc(kvrow_ps, 1)
            pe.wait_ge(cacheT_sb, 1)
            pe.wait_ge(kvrow_sb, 2)
            n_pair = 0
            for t, (t0, n, nk) in enumerate(tiles):
                k0 = 0 if t < 2 else S
                for pair in range(4):
                    if n_pair >= 2:
                        pe.wait_ge(idx_relu, n_pair - 1)
                    for half in range(2):
                        r = slice(half * HEAD_DIM, (half + 1) * HEAD_DIM)
                        last = mm(ps[0:n, 2 * (n_pair % 2) + half, 0:nk], qiT[r, pair, t0:t0 + n],
                                  kiT2[r, k0:k0 + nk], start=True, stop=True)
                    last.then_inc(idx_ps, 1)
                    n_pair += 1
            for i in range(6, 14):
                project(i)
            pe.wait_ge(state_in, 16)
            pe.wait_ge(idx_relu, 12)
            for g in range(4):
                last = tr(ps[:, 3, g * POOL_PAST:(g + 1) * POOL_PAST], state_rows[:, g * P:(g + 1) * P],
                          ident[ident_state, ident_state])
            last.then_inc(stateT_ps, 1)

            n_qk = 0
            pe.wait_ge(proj_sb, 10)

            def logits_of(t, n_qk):
                t0, n, nk = tiles[t]
                k0 = 0 if t < 2 else S
                for pair in range(4):
                    if n_qk >= 2:
                        pe.wait_ge(qk_used, n_qk - 1)
                    elif n_qk == 1:
                        pe.wait_ge(stateT_sb, 1)
                    for half in range(2):
                        r = slice(half * HEAD_DIM, (half + 1) * HEAD_DIM)
                        last = mm(ps[0:n, 2 * (n_qk % 2) + half, 0:nk], qT[r, pair, t0:t0 + n],
                                  kT2[r, k0:k0 + nk], start=True, stop=True)
                    last.then_inc(qk_ps, 1)
                    n_qk += 1
                return n_qk

            pe_groups = [0]

            def attend(t):
                t0, n, nk = tiles[t]
                nl = -(-nk // P)
                if t == 0:
                    pe.wait_ge(proj_sb, 14)
                pe.wait_ge(exp_done, t + 1)
                for c in range(nl):
                    lw = min(P, nk - c * P)
                    for hg in range(2):
                        g = pe_groups[0]
                        if g >= 2:
                            pe.wait_ge(probsT_sb, g - 1)
                        for q in range(4):
                            h = 4 * hg + q
                            last = tr(ps[0:lw, 4 + g % 2, q * n:(q + 1) * n],
                                      probs[0:n, h * nk + c * P:h * nk + c * P + lw], ident[0:n, 0:n])
                        last.then_inc(probsT_ps, 1)
                        pe_groups[0] += 1
                pe.wait_ge(probsT_sb, pe_groups[0])
                if t >= 1:
                    pe.wait_ge(att_ready, t)
                for h in range(N_HEADS):
                    for c in range(nl):
                        lw = min(P, nk - c * P)
                        if t < 2:
                            v = kv_rows[0:lw, c, HEAD_DIM:P]
                        else:
                            v = cache_vr[0:lw, c, :] if c < 2 else kv_rows[0:lw, 2, HEAD_DIM:P]
                        at = (c * N_HEADS + h) * n
                        last = mm(ps[0:n, 6, h * HEAD_DIM:(h + 1) * HEAD_DIM], probsT[0:lw, at:at + n], v,
                                  start=(c == 0), stop=(c == nl - 1))
                last.then_inc(pv_ps, 1)

            def turn_att(t):
                t0, n, _ = tiles[t]
                pe.wait_ge(att_ready, t + 1)
                if t >= 1:
                    pe.wait_ge(attT_sb, t)
                for k in range(4):
                    last = tr(ps[:, 7, k * n:(k + 1) * n], att_rows[0:n, k * P:(k + 1) * P], ident[0:n, 0:n])
                last.then_inc(attT_ps, 1)

            for t in range(NT):
                n_qk = logits_of(t, n_qk)
                attend(t)
                if t == 0:
                    pe.wait_ge(proj_sb, len(order))
                    pe.wait_ge(qk_used, n_qk)
                    for part, at in ((0, U_S - POOL_PAST), (1, UW - POOL_PAST)):
                        for g in range(4):
                            last = tr(ps[0:POOL_PAST, part, g * P:(g + 1) * P], uext[:, g, at:at + POOL_PAST],
                                      ident[:, :])
                    last.then_inc(lastu_ps, 1)
                    pe.wait_ge(lastu_sb, 1)
                turn_att(t)
            pe.wait_ge(small_in, 80)
            pe.wait_ge(pool_diff, 1)
            pe.wait_ge(qk_used, n_qk)
            for g in range(4):
                mm(ps[:, g, 0:TOK], pool_w_sb[:, g, :], diffT[:, g, :], start=True, stop=True).then_inc(poolmm_ps, 1)
            pe.wait_ge(w_o_in, 16)
            pe.wait_ge(attT_sb, NT)
            pe.wait_ge(poolT_sb, 4)
            for t, (t0, n, _) in enumerate(tiles):
                for k in range(KT):
                    for half in range(2):
                        dst = ps[0:n, 2 * t + half, :] if t < 2 else ps[half * TS:(half + 1) * TS, 4, :]
                        last = mm(dst, tokT[:, k, t0:t0 + n], w_o_sb[:, k, half * 512:(half + 1) * 512],
                                  start=(k == 0), stop=(k == KT - 1))
                last.then_inc(wo_ps, 1)
            rows_to_tokT(ln_done, h1T_ps, NT)
            pe.wait_ge(h1T_sb, 5)
            for t, (t0, n, _) in enumerate(tiles):
                for j in range(KT):
                    last = mm(ps[0:n, 6, t * NE:(t + 1) * NE], tokT[:, j, t0:t0 + n], w_router_sb[:, j, :],
                              start=(j == 0), stop=(j == KT - 1))
            last.then_inc(router_ps, 1)
            pe.wait_ge(const_ready, 8)
            pe.wait_ge(gates_ready, 1)
            for t in range(NT):
                for s in range(t + 1):
                    mm(ps[:, 7, t * NE:(t + 1) * NE], ones_b[:, :] if s < t else before[:, :], chosen_b[:, s, :],
                       start=(s == 0), stop=(s == t))
            for s in range(NT):
                last = mm(ps[:, 7, NT * NE:(NT + 1) * NE], ones_b[:, :], chosen_b[:, s, :],
                          start=(s == 0), stop=(s == NT - 1))
            last.then_inc(prefix_ps, 1)
            pe.wait_ge(gates_ready, 2)
            for t, (t0, n, _) in enumerate(tiles):
                last = tr(ps[0:NE, 3, t0:t0 + n], gate_w[0:n, t, :], ident[0:n, 0:n])
            last.then_inc(gateT_ps, 1)

            def gather(sel, ready, want, done):
                pe.wait_ge(ready, want)
                for k in range(KT):
                    for t in range(NT):
                        last = mm(ps_x[:, k, :], rows[:, t, k:D:KT], sel[:, t, :],
                                  start=(t == 0), stop=(t == NT - 1))
                last.then_inc(done, 1)

            def up_products(x, e, free):
                pe.wait_ge(b1_in, 16 * (e + 1))
                for c in range(2):
                    for g in range(2):
                        a = c * F + g * 512
                        last = mm(ps_gu[g * BLK:(g + 1) * BLK, c, :], ones_row[0:1, :], b1_sb[0:1, a:a + 512],
                                  start=True, stop=False)
                if free:
                    last.then_inc(b1_free, 1)
                for k in range(KT):
                    if k % 2 == 0:
                        pe.wait_ge(w_in_slot[k // 2], 16 * (e + 1))
                    for c in range(2):
                        for g in range(2):
                            a = c * F + g * 512
                            last = mm(ps_gu[g * BLK:(g + 1) * BLK, c, :], x[:, k, :], w1_t[:, k, a:a + 512],
                                      start=False, stop=(k == KT - 1))
                    if free and k % 2 == 1 and k < KT - 1:
                        last.then_inc(slot_free[k // 2], 1)
                return last

            def turn_h():
                for c in range(4):
                    last = tr(ps_hT[:, c * P:(c + 1) * P], h_sb[:, c:512:4], ident[:, :])
                return last

            def down_products(e, free):
                for h in range(2):
                    pe.wait_ge(w_in_slot[4 + h], 16 * (e + 1))
                    for c in range(4):
                        for g in range(2):
                            last = mm(ps_y[g * BLK:(g + 1) * BLK, :], hT[:, c, h, :],
                                      w2_t[:, h, c, g * 512:(g + 1) * 512],
                                      start=(h == 0 and c == 0), stop=(h == 1 and c == 3))
                    if free and h == 0:
                        last.then_inc(slot_free[4], 1)
                return last

            def turn_give(src, done):
                for t in range(NT):
                    last = tr(ps_g[:, t * P:(t + 1) * P], src[:, t].rearrange("p h s -> p (h s)"), ident[:, :])
                last.then_inc(done, 1)

            def combine(t, gT, y, done):
                for g in range(2):
                    last = mm(ps_c[:, g, :], gT[g * BLK:(g + 1) * BLK, t * P:(t + 1) * P], y[g * BLK:(g + 1) * BLK, :],
                              start=True, stop=True)
                last.then_inc(done, 1)

            gather(pick, pick_ready, 1, x_gathered)
            pe.wait_ge(gateT_sb, 1)
            for t, (t0, n, _) in enumerate(tiles):
                if t >= 1:
                    pe.wait_ge(acc_init, t)
                for g in range(2):
                    last = mm(ps_c[0:n, g, :], gateT[:, t0:t0 + n], b2_sb[:, g * 512:(g + 1) * 512],
                              start=True, stop=True)
                last.then_inc(b2_ps, 1)

            pe.wait_ge(blocks_ready, 1)
            with pe.Fori(0, NE) as e:
                more = pe.value_load(blocks_i[0:1, 0, bass.ds(e, 1)], min_val=0, max_val=LAST_BLK - 1)
                with pe.If(more > 0):
                    base = pe.value_load(blocks_i[0:1, 1, bass.ds(e, 1)], min_val=0, max_val=NE * LAST_BLK)
                    with pe.Fori(0, more) as i:
                        b = base + i
                        pe.wait_ge(acc_done[2], e + 1)
                        pe.wait_ge(xT_ready, e + 1)
                        pe.wait_ge(y_ready, e + 1)
                        pe.wait_ge(giveT_ready, e + 1)
                        gather(x_pick, x_pick_ready, b + 1, x_x_gathered)
                        turn_give(x_give, x_giveT_done)
                        pe.wait_ge(x_xT_ready, b + 1)
                        up_products(x_xT, e, False).then_inc(x_gu_done, 1)
                        pe.wait_ge(x_h_ready, b + 1)
                        turn_h().then_inc(x_hT_done, 1)
                        pe.wait_ge(x_hT_ready, b + 1)
                        down_products(e, False).then_inc(x_y_done, 1)
                        pe.wait_ge(x_y_ready, b + 1)
                        pe.wait_ge(x_giveT_ready, b + 1)
                        for t in range(NT):
                            combine(t, x_giveT, x_y, x_comb_done[t])
                            pe.wait_ge(x_acc_done[t], b + 1)
                pe.wait_ge(xT_ready, e + 1)
                last = up_products(xT, e, True)
                last.then_inc(slot_free[3], 1)
                pe.wait_ge(y_ready, e + 1)
                pe.wait_ge(giveT_ready, e + 1)
                pe.wait_ge(acc_done[2], e + 1)
                combine(0, giveT, y_sb, comb_done[0])
                gather(pick, pick_ready, e + 2, x_gathered)
                pe.wait_ge(h_ready, e + 1)
                turn_h().then_inc(hT_done, 1)
                pe.wait_ge(acc_done[0], e + 1)
                combine(1, giveT, y_sb, comb_done[1])
                pe.wait_ge(hT_ready, e + 1)
                down_products(e, True).then_inc(slot_free[5], 1)
                pe.wait_ge(acc_done[1], e + 1)
                combine(2, giveT, y_sb, comb_done[2])
                pe.wait_ge(give_ready, e + 1)
                turn_give(give, giveT_done)
            pe.wait_ge(y_ready, NE + 1)
            pe.wait_ge(giveT_ready, NE + 1)
            for t in range(NT):
                pe.wait_ge(acc_done[(t + 2) % 3], NE + 1)
                combine(t, giveT, y_sb, comb_done[t])

        @block.scalar
        def _(act):
            copy = nc.scalar.copy

            def sqrt_of(base):
                for t, (_, n, _) in enumerate(tiles):
                    act.wait_ge(var_ready, base + t + 1)
                    nc.scalar.activation(std[0:n, t:t + 1], veps[0:n, t:t + 1], ACT.Sqrt).then_inc(std_ready, 1)

            def tokT_copies(src, done):
                for i in range(5):
                    act.wait_ge(src, i + 1)
                    if i < 4:
                        t, q = i // 2, i % 2
                        copy(tokT[:, 4 * q:4 * q + 4, t * P:(t + 1) * P],
                             ps[:, i, :].rearrange("p (j t) -> p j t", j=4)).then_inc(done, 1)
                    else:
                        copy(tokT[:, :, S:TOK],
                             ps[:, 4, 0:KT * TS].rearrange("p (j t) -> p j t", j=KT)).then_inc(done, 1)

            sqrt_of(0)
            tokT_copies(tokT_ps, tokT_sb)

            def take(i):
                c0, w = order[i]
                bank = ps[:, PB + i % 4, :]
                act.wait_ge(proj_ps, i + 1)
                if i in (0, 5):
                    lo, raw = (kiT2, kwT) if i == 0 else (kT2, kvT)
                    for half in range(2):
                        r = slice(half * HEAD_DIM, (half + 1) * HEAD_DIM)
                        copy(lo[r, 0:S], bank[0:HEAD_DIM, 0:S])
                        copy(lo[r, S + PAST:S + PAST + TS], bank[0:HEAD_DIM, S:TOK])
                    copy(raw[0:w, :], bank[0:w, 0:TOK]).then_inc(proj_sb, 1)
                elif i < 5:
                    copy(qiT[:, i - 1, :], bank[:, 0:TOK]).then_inc(proj_sb, 1)
                elif i < 10:
                    copy(qT[:, i - 6, :], bank[:, 0:TOK]).then_inc(proj_sb, 1)
                else:
                    g = i - 10
                    copy(uext[:, g, POOL_PAST:U_S], bank[:, 0:S])
                    copy(uext[:, g, U_S + POOL_PAST:UW], bank[:, S:TOK]).then_inc(proj_sb, 1)

            for i in range(6):
                take(i)
            act.wait_ge(cacheT_ps, 1)
            for half in range(2):
                r = slice(half * HEAD_DIM, (half + 1) * HEAD_DIM)
                copy(kT2[r, S:S + PAST], ps[0:HEAD_DIM, 0, 0:PAST])
                last = copy(kiT2[r, S:S + PAST], ps[HEAD_DIM:P, 0, 0:PAST])
            last.then_inc(cacheT_sb, 1)
            act.wait_ge(kvrow_ps, 1)
            copy(kv_rows[:, 0:2, :], ps[:, 1, 0:2 * (P + KW)].rearrange("p (t n) -> p t n", t=2)).then_inc(kvrow_sb, 1)
            act.wait_ge(kvrow_ps, 2)
            copy(kv_rows[0:TS, 2, :], ps[0:TS, 2, 0:P + KW]).then_inc(kvrow_sb, 1)
            n_pair = 0
            for t, (t0, n, nk) in enumerate(tiles):
                for pair in range(4):
                    act.wait_ge(idx_ps, n_pair + 1)
                    if n_pair >= 2:
                        act.wait_ge(idx_used, n_pair - 1)
                    b = n_pair % 2
                    nc.scalar.activation(relu_sb[0:n, b, :, 0:nk], ps[0:n, 2 * b:2 * b + 2, 0:nk],
                                         ACT.Relu).then_inc(idx_relu, 1)
                    n_pair += 1
            for i in range(6, 14):
                take(i)
            act.wait_ge(stateT_ps, 1)
            copy(uext[:, :, U_S:U_S + POOL_PAST],
                 ps[:, 3, 0:4 * POOL_PAST].rearrange("p (g n) -> p g n", g=4)).then_inc(stateT_sb, 1)

            groups = 0
            for t, (t0, n, nk) in enumerate(tiles):
                act.wait_ge(max_ready, t + 1)
                for h in range(N_HEADS):
                    p = probs[0:n, h * nk:(h + 1) * nk]
                    last = nc.scalar.activation(p, p, ACT.Exp, bias=neg_max[0:n, t, h:h + 1],
                                                accum_out=row_sum[0:n, t, h:h + 1])
                last.then_inc(exp_done, 1)
                for c in range(-(-nk // P)):
                    lw = min(P, nk - c * P)
                    for hg in range(2):
                        act.wait_ge(probsT_ps, groups + 1)
                        if t >= 1 and c == 0 and hg == 0:
                            act.wait_ge(pv_ps, t)
                        at = (c * N_HEADS + 4 * hg) * n
                        copy(probsT[0:lw, at:at + 4 * n], ps[0:lw, 4 + groups % 2, 0:4 * n]).then_inc(probsT_sb, 1)
                        groups += 1
                if t == 0:
                    act.wait_ge(lastu_ps, 1)
                    copy(last_u[:, :, :], ps[0:POOL_PAST, 0:2, :]).then_inc(lastu_sb, 1)
                act.wait_ge(attT_ps, t + 1)
                copy(tokT[:, 0:4, t0:t0 + n],
                     ps[:, 7, 0:4 * n].rearrange("p (k t) -> p k t", k=4)).then_inc(attT_sb, 1)
            sqrt_of(NT)
            tokT_copies(h1T_ps, h1T_sb)
            act.wait_ge(top_ready, 1)
            nc.scalar.activation(top_w[:, :, :], top_w[:, :, :], ACT.Exp).then_inc(top_exp, 1)
            act.wait_ge(gateT_ps, 1)
            copy(gateT[:, :], ps[0:NE, 3, 0:TOK]).then_inc(gateT_sb, 1)

            act.wait_ge(x_gathered, 1)
            copy(xT, ps_x).then_inc(xT_ready, 1)
            act.wait_ge(blocks_ready, 1)
            with act.Fori(0, NE) as e:
                more = act.value_load(blocks_i[0:1, 0, bass.ds(e, 1)], min_val=0, max_val=LAST_BLK - 1)
                with act.If(more > 0):
                    base = act.value_load(blocks_i[0:1, 1, bass.ds(e, 1)], min_val=0, max_val=NE * LAST_BLK)
                    with act.Fori(0, more) as i:
                        b = base + i
                        act.wait_ge(x_x_gathered, b + 1)
                        copy(x_xT, ps_x).then_inc(x_xT_ready, 1)
                        act.wait_ge(x_giveT_done, b + 1)
                        copy(x_giveT, ps_g).then_inc(x_giveT_ready, 1)
                        act.wait_ge(x_gate_ready, b + 1)
                        nc.scalar.activation(sig_sb, g_sb, ACT.Sigmoid, scale=SWIGLU_ALPHA).then_inc(x_sig_ready, 1)
                        act.wait_ge(x_hT_done, b + 1)
                        copy(hT, ps_hT.rearrange("p (c h s) -> p c h s", c=4, h=2)).then_inc(x_hT_ready, 1)
                        act.wait_ge(x_y_done, b + 1)
                        copy(x_y, ps_y).then_inc(x_y_ready, 1)
                act.wait_ge(gate_ready, e + 1)
                nc.scalar.activation(sig_sb, g_sb, ACT.Sigmoid, scale=SWIGLU_ALPHA).then_inc(sig_ready, 1)
                act.wait_ge(x_gathered, e + 2)
                copy(xT, ps_x).then_inc(xT_ready, 1)
                act.wait_ge(hT_done, e + 1)
                copy(hT, ps_hT.rearrange("p (c h s) -> p c h s", c=4, h=2)).then_inc(hT_ready, 1)
                act.wait_ge(slot_free[5], e + 1)
                act.wait_ge(comb_done[2], e + 1)
                copy(y_sb, ps_y).then_inc(y_ready, 1)
                act.wait_ge(giveT_done, e + 1)
                copy(giveT, ps_g).then_inc(giveT_ready, 1)
            sqrt_of(2 * NT)
            for t in range(2):
                act.wait_ge(ln_done, 2 * NT + t + 1)
                act.dma_start(y_prompt[0, t * P:(t + 1) * P, :], out_acc[:, t, :]).then_inc(final_out, 16)
            act.wait_ge(ln_done, 3 * NT)
            act.dma_start(y_sample[0], out_acc[0:TS, 2, :]).then_inc(final_out, 16)
            act.wait_ge(final_out, 48)

        @block.vector
        def _(dve):
            v = nc.vector
            step = [0]

            def link(ins):
                step[0] += 1
                ins.then_inc(dve_step, 1)
                dve.wait_ge(dve_step, step[0])

            def layer_norm(t, n, src, base):
                for q in range(2):
                    ins = v.bn_stats(stats[0:n, t, q, :], src[:, q * 512:(q + 1) * 512])
                link(ins)
                link(v.bn_aggr(moments[0:n, t, :], stats[0:n, t, :, :]))
                v.tensor_scalar(veps[0:n, t:t + 1], moments[0:n, t, 1:2], LN_EPS, None, ALU.add).then_inc(var_ready, 1)
                link(v.scalar_tensor_tensor(src, src, moments[0:n, t, 0:1], lnb[0:n, 0, :], ALU.subtract, ALU.mult))
                dve.wait_ge(std_ready, base + t + 1)
                link(v.reciprocal(rstd[0:n, t:t + 1], std[0:n, t:t + 1]))
                v.scalar_tensor_tensor(src, src, rstd[0:n, t:t + 1], lnb[0:n, 1, :], ALU.mult, ALU.add)\
                    .then_inc(ln_done, 1)

            dve.wait_ge(ln_in[0], 32)
            for t, (_, n, _) in enumerate(tiles):
                dve.wait_ge(x_in[t // 2], 16)
                layer_norm(t, n, rows[0:n, t, :], 0)

            dve.wait_ge(const_ready, 8)
            for g, w in enumerate(WINDOWS):
                ins = v.tensor_scalar(rcount[:, g, :], rcount[:, g, :], float(w), None, ALU.min)
            link(ins)
            link(v.reciprocal(rcount[:, :, :], rcount[:, :, :]))

            dve.wait_ge(kvrow_sb, 2)
            for t, (_, n, _) in enumerate(tiles):
                ins = v.tensor_scalar(w_idx[0:n, t, :], kv_rows[0:n, t, P + HEAD_DIM:P + KW],
                                      N_HEADS ** -0.5 * HEAD_DIM ** -0.5, None, ALU.mult)
            link(ins)
            n_pair = 0
            for t, (_, n, nk) in enumerate(tiles):
                sc = score[0:n, t, 0:nk]
                for pair in range(4):
                    dve.wait_ge(idx_relu, n_pair + 1)
                    for half in range(2):
                        r, w = relu_sb[0:n, n_pair % 2, half, 0:nk], w_idx[0:n, t, 2 * pair + half:2 * pair + half + 1]
                        if pair == 0 and half == 0:
                            link(v.tensor_scalar(sc, r, w, None, ALU.mult))
                        elif half == 0:
                            link(v.scalar_tensor_tensor(sc, r, w, sc, ALU.mult, ALU.add))
                        else:
                            v.scalar_tensor_tensor(sc, r, w, sc, ALU.mult, ALU.add).then_inc(idx_used, 1)
                            dve.wait_ge(idx_used, n_pair + 1)
                    n_pair += 1
                if t < 2:
                    link(v.memset(score[0:CHUNK, t, nk - CHUNK:nk], HIDDEN_KEY))
            for t, (_, n, nk) in enumerate(tiles):
                sc = score[0:n, t, 0:nk]
                assert topk[t] % 8 == 0
                for _ in range(topk[t] // 8):
                    link(v.max(max8[0:n, t, :], sc))
                    link(v.match_replace(sc, max8[0:n, t, :], sc, TAKEN))
                link(v.tensor_scalar(sc, sc, TAKEN / 2, HIDDEN_KEY, ALU.is_gt, ALU.mult))

            n_qk = 0
            for t, (_, n, nk) in enumerate(tiles):
                if t == 0:
                    dve.wait_ge(proj_ps, len(order))
                else:
                    dve.wait_ge(probsT_ps, [2, 6][t - 1])
                for pair in range(4):
                    dve.wait_ge(qk_ps, n_qk + 1)
                    for half in range(2):
                        h = 2 * pair + half
                        ins = v.tensor_tensor_reduce(
                            out=probs[0:n, h * nk:(h + 1) * nk], in0=ps[0:n, 2 * (n_qk % 2) + half, 0:nk],
                            in1=score[0:n, t, 0:nk], scale=HEAD_DIM ** -0.5, scalar=TAKEN, op0=ALU.add, op1=ALU.max,
                            accum_out=row_max[0:n, t, h:h + 1])
                    ins.then_inc(qk_used, 1)
                    n_qk += 1
                dve.wait_ge(qk_used, n_qk)
                v.tensor_scalar(neg_max[0:n, t, :], row_max[0:n, t, :], -1.0, None, ALU.mult).then_inc(max_ready, 1)
                dve.wait_ge(exp_done, t + 1)
                link(v.reciprocal(row_inv[0:n, t, :], row_sum[0:n, t, :]))
                dve.wait_ge(pv_ps, t + 1)
                if t >= 1:
                    dve.wait_ge(attT_ps, t)
                v.tensor_tensor(att_rows[0:n, :].rearrange("p (h d) -> p h d", h=N_HEADS),
                                ps[0:n, 6, :].rearrange("p (h d) -> p h d", h=N_HEADS),
                                row_inv[0:n, t, :].unsqueeze(2).broadcast_to([n, N_HEADS, HEAD_DIM]),
                                ALU.mult).then_inc(att_ready, 1)
                if t == 0:
                    dve.wait_ge(pool_step, 4)
                    dve.wait_ge(small_in, 80)
                    for g, w in enumerate(WINDOWS):
                        s = sums_a if g % 2 == 0 else sums_b
                        link(v.tensor_tensor(s[:, g, POOL_PAST:POOL_PAST + 16], s[:, g, POOL_PAST:POOL_PAST + 16],
                                             rcount[:, g, :], ALU.mult))
                        v.tensor_tensor(diffT[:, g, 0:16], s[:, g, POOL_PAST:POOL_PAST + 16],
                                        uext[:, g, POOL_PAST:POOL_PAST + 16], ALU.subtract)
                        v.scalar_tensor_tensor(diffT[:, g, 16:S], s[:, g, POOL_PAST + 16:U_S], 1.0 / w,
                                               uext[:, g, POOL_PAST + 16:U_S], ALU.mult, ALU.subtract)
                        ins = v.scalar_tensor_tensor(diffT[:, g, S:TOK], s[:, g, U_S + POOL_PAST:UW], 1.0 / w,
                                                     uext[:, g, U_S + POOL_PAST:UW], ALU.mult, ALU.subtract)
                    ins.then_inc(pool_diff, 1)
            for g in range(4):
                dve.wait_ge(poolmm_ps, g + 1)
                v.tensor_scalar(tokT[:, 4 + g, :], ps[:, g, 0:TOK], pool_scale_sb[:, g:g + 1], None,
                                ALU.mult).then_inc(poolT_sb, 1)

            dve.wait_ge(ln_in[1], 32)
            for t, (_, n, _) in enumerate(tiles):
                dve.wait_ge(wo_ps, t + 1)
                if t < 2:
                    link(v.scalar_tensor_tensor(rows[:, t, :].rearrange("p (h n) -> p h n", h=2),
                                                rows[:, t, :].rearrange("p (h n) -> p h n", h=2), RESIDUAL,
                                                ps[:, 2 * t:2 * t + 2, :], ALU.mult, ALU.add))
                else:
                    for half in range(2):
                        r = rows[0:TS, 2, half * 512:(half + 1) * 512]
                        ins = v.scalar_tensor_tensor(r, r, RESIDUAL, ps[half * TS:(half + 1) * TS, 4, :],
                                                     ALU.mult, ALU.add)
                        link(ins)
                layer_norm(t, n, rows[0:n, t, :], NT)

            dve.wait_ge(router_ps, 1)
            for t, (_, n, _) in enumerate(tiles):
                ins = v.tensor_tensor(logits[0:n, t, :], ps[0:n, 6, t * NE:(t + 1) * NE], b_router_sb[0:n, :], ALU.add)
            link(ins)
            for t in range(NT):
                ins = v.max(top8[:, t, :], logits[:, t, :])
            link(ins)
            v.tensor_tensor(top_w[:, :, :], top8[:, :, 0:TOP_K],
                            top8[:, :, 0:1].broadcast_to([P, NT, TOP_K]), ALU.subtract).then_inc(top_ready, 1)
            for t in range(NT):
                ins = v.max_index(top_i[:, t, :], top8[:, t, :], logits[:, t, :])
            link(ins)
            link(v.tensor_copy(top_f[:, :, :], top_i[:, :, 0:TOP_K]))
            for t in range(NT):
                ins = v.tensor_tensor(onehot[:, t], iota_exp[:, :].unsqueeze(1).broadcast_to([P, TOP_K, NE]),
                                      top_f[:, t, :].unsqueeze(2).broadcast_to([P, TOP_K, NE]), ALU.is_equal)
            link(ins)
            for t in range(NT):
                ins = v.tensor_reduce(chosen[:, t, :], onehot[:, t].rearrange("p k e -> p e k"), AX, ALU.add)
            link(ins)
            v.memset(chosen[32:64, 2, :], 0.0)
            link(v.memset(chosen[64:P, 2, :], 0.0))
            v.tensor_copy(chosen_b[:, :, :], chosen[:, :, :]).then_inc(gates_ready, 1)
            dve.wait_ge(top_exp, 1)
            link(v.tensor_reduce(top_s[:, :], top_w[:, :, :], AX, ALU.add))
            link(v.reciprocal(top_r[:, :], top_s[:, :]))
            link(v.tensor_tensor(top_w[:, :, :], top_w[:, :, :],
                                 top_r[:, :].unsqueeze(2).broadcast_to([P, NT, TOP_K]), ALU.mult))
            for t in range(NT):
                ins = v.tensor_tensor(weighed[:, t], onehot[:, t],
                                      top_w[:, t, :].unsqueeze(2).broadcast_to([P, TOP_K, NE]), ALU.mult)
            link(ins)
            for t in range(NT):
                ins = v.tensor_reduce(gate_w[:, t, :], weighed[:, t].rearrange("p k e -> p e k"), AX, ALU.add)
            ins.then_inc(gates_ready, 1)
            dve.wait_ge(gates_ready, 2)
            dve.wait_ge(prefix_ps, 1)
            link(v.scalar_tensor_tensor(place[:, :, 0:NE], ps[:, 7, 0:NT * NE].rearrange("p (t e) -> p t e", t=NT), 1.0,
                                        chosen[:, :, :], ALU.add, ALU.mult))
            link(v.memset(place[:, :, NE:NE + 1], -1.0))
            link(v.tensor_scalar(place[:, :, 0:NE], place[:, :, 0:NE], -1.0, None, ALU.add))

            first_slots = iota_slot[:, 0:BLK]

            def one_hot(dst, at, slots):
                return v.tensor_tensor(dst, slots.unsqueeze(1).broadcast_to([P, NT, BLK]),
                                       at.broadcast_to([P, NT, BLK]), ALU.is_equal)

            def gated_one_hot(dst, e, slots):
                for t in range(NT):
                    ins = v.tensor_scalar(dst[:, t], slots.unsqueeze(1).broadcast_to([P, 2, BLK]),
                                          place[:, t, bass.ds(e, 1)], gate_w[:, t, bass.ds(e, 1)],
                                          ALU.is_equal, ALU.mult)
                return ins

            one_hot(pick, place[:, :, 0:1], first_slots).then_inc(pick_ready, 1)
            count = ps[0:1, 7, NT * NE:(NT + 1) * NE]
            n_more, n_incl, n_excl = (blocks_f[:, i, :] for i in range(3))
            link(v.tensor_scalar(n_more, count, float(BLK), None, ALU.is_gt))
            for b in range(2, LAST_BLK):
                link(v.scalar_tensor_tensor(n_more, count, float(b * BLK), n_more, ALU.is_gt, ALU.add))
            link(v.tensor_tensor_scan(n_incl, n_more, n_more, 0.0, ALU.add, ALU.bypass))
            link(v.tensor_tensor(n_excl, n_incl, n_more, ALU.subtract))
            v.tensor_copy(blocks_i[:, 0, :], n_more)
            v.tensor_copy(blocks_i[:, 1, :], n_excl).then_inc(blocks_ready, 1)
            for t, (_, n, _) in enumerate(tiles):
                dve.wait_ge(b2_ps, t + 1)
                v.scalar_tensor_tensor(out_acc[0:n, t, :].rearrange("p (h n) -> p h n", h=2),
                                       rows[0:n, t, :].rearrange("p (h n) -> p h n", h=2), RESIDUAL,
                                       ps_c[0:n, :, :], ALU.mult, ALU.add).then_inc(acc_init, 1)
            dve.wait_ge(acc_init, NT)
            v.memset(giveT, 0.0).then_inc(giveT_ready, 1)
            v.memset(y_sb, 0.0).then_inc(y_ready, 1)
            for s in (acc_done[2],):
                v.memset(max8[:, 0, :], 0.0).then_inc(s, 1)

            def swiglu(gu, gate, sig, up, prod, want, h_out):
                dve.wait_ge(gu, want)
                v.tensor_scalar(g_sb, ps_gu[:, 0, :], LIMIT, None, ALU.min).then_inc(gate, 1)
                v.tensor_scalar(u_sb, ps_gu[:, 1, :], LIMIT, -LIMIT, ALU.min, ALU.max).then_inc(up, 1)
                dve.wait_ge(gate, want)
                dve.wait_ge(up, want)
                v.scalar_tensor_tensor(u_sb, u_sb, 1.0, g_sb, ALU.add, ALU.mult).then_inc(prod, 1)
                dve.wait_ge(prod, want)
                dve.wait_ge(sig, want)
                v.tensor_tensor(h_sb, u_sb, sig_sb, ALU.mult).then_inc(h_out, 1)

            def accumulate(t, comb, want, done):
                _, n, _ = tiles[t]
                dve.wait_ge(comb, want)
                acc = out_acc[0:n, t, :].rearrange("p (h n) -> p h n", h=2)
                v.tensor_tensor(acc, acc, ps_c[0:n, :, :], ALU.add).then_inc(done, 1)

            dve.wait_ge(blocks_ready, 1)
            with dve.Fori(0, NE) as e:
                more = dve.value_load(blocks_i[0:1, 0, bass.ds(e, 1)], min_val=0, max_val=LAST_BLK - 1)
                with dve.If(more > 0):
                    base = dve.value_load(blocks_i[0:1, 1, bass.ds(e, 1)], min_val=0, max_val=NE * LAST_BLK)
                    with dve.Fori(0, more) as i:
                        b = base + i
                        slots = iota_slot[:, bass.ds((i + 1) * BLK, BLK)]
                        gated_one_hot(x_give, e, slots)
                        one_hot(x_pick, place[:, :, bass.ds(e, 1)], slots).then_inc(x_pick_ready, 1)
                        swiglu(x_gu_done, x_gate_ready, x_sig_ready, x_up_ready, x_prod_ready, b + 1, x_h_ready)
                        for t in range(NT):
                            accumulate(t, x_comb_done[t], b + 1, x_acc_done[t])
                dve.wait_ge(x_gathered, e + 1)
                one_hot(pick, place[:, :, bass.ds(e + 1, 1)], first_slots).then_inc(pick_ready, 1)
                swiglu(slot_free[3], gate_ready, sig_ready, up_ready, prod_ready, e + 1, h_ready)
                gated_one_hot(give, e, first_slots).then_inc(give_ready, 1)
                for t in range(NT):
                    accumulate(t, comb_done[t], e + 1, acc_done[t])
            for t, (_, n, _) in enumerate(tiles):
                accumulate(t, comb_done[t], NE + 1, acc_done[t])
            dve.wait_ge(ln_in[2], 32)
            for t, (_, n, _) in enumerate(tiles):
                dve.wait_ge(acc_done[t], NE + (2 if t == 2 else 1))
                layer_norm(t, n, out_acc[0:n, t, :], 2 * NT)


_INS = ['x_prompt', 'x_sample', 'cache_k', 'cache_v', 'cache_kidx', 'state_pool', 'ln0_g', 'ln0_b', 'w_in', 'w_o',
        'pool_w', 'pool_scale', 'ln1_g', 'ln1_b', 'w_router', 'b_router', 'w1', 'b1', 'w2', 'b2', 'ln2_g', 'ln2_b']
_OUTS = [(1, 256, 1024), (1, 32, 1024), (1, 1, 256, 64), (1, 1, 256, 64), (1, 1, 256, 64), (1, 1, 15, 512),
         (1, 1, 32, 64), (1, 1, 32, 64), (1, 1, 32, 64), (1, 1, 15, 512)]


def kernel(**inputs):
    import numpy as _np
    import concourse.bacc as _bacc
    from concourse import mybir as _mybir
    from concourse.bass_utils import run_bass_kernel_spmd as _run

    nc = _bacc.Bacc("TRN2", target_bir_lowering=False, num_devices=1)
    arrays, ins, outs = {}, [], []
    for name in _INS:
        a = _np.ascontiguousarray(inputs[name])
        arrays[f"in_{name}_dram"] = a
        ins.append(nc.dram_tensor(f"in_{name}_dram", a.shape, _mybir.dt.from_np(a.dtype), kind="ExternalInput").ap())
    for i, shape in enumerate(_OUTS):
        outs.append(nc.dram_tensor(f"out_{i}_dram", shape, _mybir.dt.float32, kind="ExternalOutput").ap())
    encoder_kernel(nc, ins, outs)
    r = _run(nc, [arrays], core_ids=[0])
    return tuple(r.results[0][f"out_{i}_dram"] for i in range(len(_OUTS)))
```

```python
from contextlib import ExitStack

import concourse.bass as bass
from concourse import mybir

F32 = mybir.dt.float32
F32R = mybir.dt.float32r
BF16 = mybir.dt.bfloat16
I32 = mybir.dt.int32
U32 = mybir.dt.uint32
ALU = mybir.AluOpType
ACT = mybir.ActivationFunctionType
AX = mybir.AxisListType.X

P = 128
CHUNK = 64
HEAD_DIM = 64
N_HEADS = 8
POOL_PAST = 15
WINDOWS = (2, 4, 8, 16)
TOP_K = 4
LIMIT = 7.0
SWIGLU_ALPHA = 1.702
LN_EPS = 1e-5
RESIDUAL = 2.0 ** 0.25
HIDDEN_KEY = -1.0e30
TAKEN = -3.0e38
BLK = 64


def encoder_kernel(nc, ins, outs):
    (x_prompt, x_sample, cache_k, cache_v, cache_kidx, state_pool, ln0_g, ln0_b, w_in, w_o, pool_w,
     pool_scale, ln1_g, ln1_b, w_router, b_router, w1, b1, w2, b2, ln2_g, ln2_b) = ins
    (y_prompt, y_sample, k_prompt, v_prompt, kidx_prompt, pool_prompt,
     k_sample, v_sample, kidx_sample, pool_sample) = outs

    S, D = x_prompt.shape[1:]
    TS = x_sample.shape[1]
    PAST = cache_k.shape[2]
    NE = w_router.shape[2]
    F = w2.shape[2]
    IN = w_in.shape[2]
    KT = D // P
    TOK = S + TS
    NT = 3
    TOKP = NT * P
    tiles = [(0, P, P), (P, P, 2 * P), (S, TS, PAST + TS)]
    topk = [min(256, S // 4)] * 2 + [min(256, (PAST + TS) // 4)]
    assert (S, TS, D, F, PAST, KT) == (2 * P, 32, 1024, 1024, 2 * P, 8)
    K_OFF = N_HEADS * HEAD_DIM
    QI_OFF = K_OFF + 2 * HEAD_DIM
    KI_OFF = QI_OFF + N_HEADS * HEAD_DIM
    U_OFF = KI_OFF + HEAD_DIM + N_HEADS
    KW = HEAD_DIM + N_HEADS
    LAST_BLK = -(-TOK // BLK)
    SLOT = 2 * 2 * F
    NSLOT = 6
    UW = POOL_PAST + S + POOL_PAST + TS
    U_S = POOL_PAST + S

    with ExitStack() as ctx:
        def sb(name, shape, dt=F32):
            return ctx.enter_context(nc.sbuf_tensor(name, shape, dt))

        def sem(name):
            return ctx.enter_context(nc.semaphore(name))

        ring = sb("ring", [P, NSLOT, SLOT])
        area = sb("area", [P, KT * IN])
        rows = sb("rows", [P, NT, D])
        tokT = sb("tokT", [P, KT, TOK])
        lnb = sb("lnb", [P, 2, D])
        uext = sb("uext", [P, 4, UW])
        kv_rows = sb("kv_rows", [P, NT, P + KW])
        score = sb("score", [P, NT, 288])
        w_router_sb = sb("w_router_sb", [P, KT, NE])
        b_router_sb = sb("b_router_sb", [P, NE])
        pool_scale_sb = sb("pool_scale_sb", [P, 4])
        giveT = sb("giveT", [P, TOKP], F32R)
        y_sb = sb("y_sb", [P, D], F32R)
        ident = sb("ident", [P, P])
        iota_slot = sb("iota_slot", [P, LAST_BLK * BLK])
        iota_exp = sb("iota_exp", [P, NE])
        before = sb("before", [P, P], BF16)
        ones_b = sb("ones_b", [P, P], BF16)
        same_exp = sb("same_exp", [3 * NE, NE + 1])
        sel = sb("sel", [3 * NE, BLK], BF16)
        gcol = sb("gcol", [P, 1])
        x_gcol = sb("x_gcol", [P, 1])
        stats = sb("stats", [P, NT, 2, 6])
        moments = sb("moments", [P, NT, 2])
        veps = sb("veps", [P, NT])
        std = sb("std", [P, NT])
        rstd = sb("rstd", [P, NT])
        w_idx = sb("w_idx", [P, NT, N_HEADS])
        max8 = sb("max8", [P, NT, 8])
        row_max = sb("row_max", [P, NT, N_HEADS])
        neg_max = sb("neg_max", [P, NT, N_HEADS])
        row_sum = sb("row_sum", [P, NT, N_HEADS])
        row_inv = sb("row_inv", [P, NT, N_HEADS])
        logits = sb("logits", [P, NT, NE])
        top8 = sb("top8", [P, NT, 8])
        top_i = sb("top_i", [P, NT, 8], U32)
        top_f = sb("top_f", [P, NT, TOP_K])
        top_w = sb("top_w", [P, NT, TOP_K])
        top_s = sb("top_s", [P, NT])
        top_r = sb("top_r", [P, NT])
        flat = score[:, :, :].rearrange("p t n -> p (t n)")
        n_hot = NT * TOP_K * NE
        onehot = flat[:, 0:n_hot].rearrange("p (t k e) -> p t k e", t=NT, k=TOP_K)
        weighed = flat[:, n_hot:2 * n_hot].rearrange("p (t k e) -> p t k e", t=NT, k=TOP_K)
        chosen = sb("chosen", [P, NT, NE])
        chosen_b = sb("chosen_b", [P, NT, NE], BF16)
        gate_w = sb("gate_w", [P, NT, NE + 1])
        place = sb("place", [P, NT, NE + 1])
        blocks_f = sb("blocks_f", [1, 3, NE])
        blocks_i = sb("blocks_i", [1, 2, NE], I32)

        w_in_sb = area[:, :].rearrange("p (j n) -> p j n", j=KT)
        w_o_sb = area[:, 0:KT * D].rearrange("p (k n) -> p k n", k=KT)
        out_acc = area[:, KT * D:KT * D + NT * D].rearrange("p (t n) -> p t n", t=NT)
        sums_a = area[:, KT * D:KT * D + 4 * UW].rearrange("p (g n) -> p g n", g=4)
        sums_b = area[:, KT * D + 4 * UW:KT * D + 8 * UW].rearrange("p (g n) -> p g n", g=4)
        BP = KT * D + NT * D
        bias_parts = area[0:3 * NE, BP:BP + 3 * F // 2].bitcast(BF16)
        assert BP + 3 * F // 2 <= KT * IN

        spare = ring[:, 2:6, :].rearrange("p s n -> p (s n)")
        used = [0]

        def carve(base, n):
            at = used[0]
            used[0] += n
            return base[:, at:at + n]

        qT = carve(spare, 4 * TOK).rearrange("p (i t) -> p i t", i=4)
        qiT = carve(spare, 4 * TOK).rearrange("p (i t) -> p i t", i=4)
        kT2 = carve(spare, S + PAST + TS)
        kiT2 = carve(spare, S + PAST + TS)
        kvT = carve(spare, TOK)
        kwT = carve(spare, TOK)
        relu_sb = carve(spare, 4 * 288).rearrange("p (b h n) -> p b h n", b=2, h=2)
        probsT = carve(spare, 2 * 8 * P)
        att_rows = carve(spare, N_HEADS * HEAD_DIM)
        cache_rows = carve(spare, 2 * P).rearrange("p (c d) -> p c d", c=2)
        cache_vr = carve(spare, 2 * HEAD_DIM).rearrange("p (c d) -> p c d", c=2)
        diffT = carve(spare, 4 * TOK).rearrange("p (g t) -> p g t", g=4)
        pool_w_sb = carve(spare, 4 * P).rearrange("p (g c) -> p g c", g=4)
        narrow = carve(spare, D)
        last_u = narrow[32:32 + POOL_PAST, :].rearrange("p (s c) -> p s c", s=2)
        state_rows = narrow[64:64 + POOL_PAST, 0:4 * P]
        ident_state = slice(64, 64 + POOL_PAST)
        rcount = carve(spare, 4 * 16).rearrange("p (g n) -> p g n", g=4)
        probs = carve(spare, 8 * 288)
        bias_f = carve(spare, 3 * F)[0:3 * NE, :]
        assert used[0] <= 4 * SLOT

        used[0] = 0
        xT = carve(area, KT * BLK).rearrange("p (k s) -> p k s", k=KT)
        pick = carve(area, NT * 2 * BLK).rearrange("p (t h s) -> p t h s", t=NT, h=2)
        g_sb = carve(area, F // 2)
        u_sb = carve(area, F // 2)
        sig_sb = carve(area, F // 2)
        h_sb = carve(area, F // 2)
        hT = carve(area, 4 * P).rearrange("p (c h s) -> p c h s", c=4, h=2)
        x_xT = carve(area, KT * BLK).rearrange("p (k s) -> p k s", k=KT)
        x_pick = carve(area, NT * 2 * BLK).rearrange("p (t h s) -> p t h s", t=NT, h=2)
        x_giveT = carve(area, TOKP)
        x_y = carve(area, D // 2)
        assert used[0] <= KT * D

        ps = ctx.enter_context(nc.psum_tensor("ps", [P, 8, 512], F32))
        ps_gu = ps[:, 0:2, :]
        ps_x = ps[:, 2, :].rearrange("p (k s) -> p k s", k=KT)
        ps_hT = ps[:, 3, :]
        ps_y = ps[:, 4, :]
        ps_c = ps[:, 5:7, :]
        ps_g = ps[:, 7, 0:TOKP + 1]
        x_ps_g = ps[:, 3, 0:TOKP + 1]

        zero_rows = sem("zero_rows")
        ident0 = sem("ident0")
        before0 = sem("before0")
        same0 = sem("same0")
        ident_ready = sem("ident_ready")
        const_ready = sem("const_ready")
        pool_step = sem("pool_step")
        x_in = [sem(f"x_in{t}") for t in range(2)]
        ln_in = [sem(f"ln_in{i}") for i in range(3)]
        w_in_in = [sem(f"w_in_in{i}") for i in range(3)]
        cache_in = sem("cache_in")
        small_in = sem("small_in")
        state_in = sem("state_in")
        w_o_in = sem("w_o_in")
        w_in_slot = [sem(f"w_slot{s}") for s in range(NSLOT)]
        bias_in = sem("bias_in")
        bias_step = sem("bias_step")
        bias_ready = sem("bias_ready")
        rows_out = sem("rows_out")
        final_out = sem("final_out")
        dve_step = sem("dve_step")
        var_ready = sem("var_ready")
        std_ready = sem("std_ready")
        ln_done = sem("ln_done")
        tokT_ps = sem("tokT_ps")
        tokT_sb = sem("tokT_sb")
        proj_ps = sem("proj_ps")
        proj_sb = sem("proj_sb")
        cacheT_ps = sem("cacheT_ps")
        cacheT_sb = sem("cacheT_sb")
        kvrow_ps = sem("kvrow_ps")
        kvrow_sb = sem("kvrow_sb")
        idx_ps = sem("idx_ps")
        idx_relu = sem("idx_relu")
        idx_used = sem("idx_used")
        pool_diff = sem("pool_diff")
        lastu_ps = sem("lastu_ps")
        lastu_sb = sem("lastu_sb")
        stateT_ps = sem("stateT_ps")
        stateT_sb = sem("stateT_sb")
        poolmm_ps = sem("poolmm_ps")
        poolT_sb = sem("poolT_sb")
        qk_ps = sem("qk_ps")
        qk_used = sem("qk_used")
        max_ready = sem("max_ready")
        exp_done = sem("exp_done")
        probsT_ps = sem("probsT_ps")
        probsT_sb = sem("probsT_sb")
        pv_ps = sem("pv_ps")
        att_ready = sem("att_ready")
        attT_ps = sem("attT_ps")
        attT_sb = sem("attT_sb")
        wo_ps = sem("wo_ps")
        h1T_ps = sem("h1T_ps")
        h1T_sb = sem("h1T_sb")
        router_ps = sem("router_ps")
        top_ready = sem("top_ready")
        top_exp = sem("top_exp")
        gates_ready = sem("gates_ready")
        prefix_ps = sem("prefix_ps")
        blocks_ready = sem("blocks_ready")
        acc_init = sem("acc_init")
        slot_free = [sem(f"slot_free{s}") for s in range(NSLOT)]
        sel_ready = sem("sel_ready")
        pick_ready = sem("pick_ready")
        x_gathered = sem("x_gathered")
        xT_ready = sem("xT_ready")
        gate_ready = sem("gate_ready")
        sig_ready = sem("sig_ready")
        up_ready = sem("up_ready")
        prod_ready = sem("prod_ready")
        h_ready = sem("h_ready")
        hT_done = sem("hT_done")
        hT_ready = sem("hT_ready")
        y_high = sem("y_high")
        y_ready = sem("y_ready")
        giveT_done = sem("giveT_done")
        giveT_ready = sem("giveT_ready")
        comb_done = [sem(f"comb_done{t}") for t in range(NT)]
        acc_done = [sem(f"acc_done{t}") for t in range(NT)]
        x_pick_ready = sem("x_pick_ready")
        x_x_gathered = sem("x_x_gathered")
        x_xT_ready = sem("x_xT_ready")
        x_gu_done = sem("x_gu_done")
        x_gate_ready = sem("x_gate_ready")
        x_sig_ready = sem("x_sig_ready")
        x_up_ready = sem("x_up_ready")
        x_prod_ready = sem("x_prod_ready")
        x_h_ready = sem("x_h_ready")
        x_hT_done = sem("x_hT_done")
        x_hT_ready = sem("x_hT_ready")
        x_y_done = sem("x_y_done")
        x_y_ready = sem("x_y_ready")
        x_giveT_done = sem("x_giveT_done")
        x_giveT_ready = sem("x_giveT_ready")
        x_comb_done = [sem(f"x_comb_done{t}") for t in range(NT)]
        x_acc_done = [sem(f"x_acc_done{t}") for t in range(NT)]

        def broadcast_row(ap):
            return ap.rearrange("(a n) -> a n", a=1).partition_broadcast(P) if len(ap.shape) == 1 \
                else ap.partition_broadcast(P)

        w1_v = w1[0].rearrange("e (p k) n -> e p (k n)", k=KT)
        w2_v = w2[0].rearrange("e (h p c) n -> e h p (c n)", h=2, c=4)
        w1_t = ring[:, 0:4, :].rearrange("p s (k n) -> p (s k) n", k=2)
        w2_t = ring[:, 4:6, :].rearrange("p s (c n) -> p s c n", c=4)
        x_views = [x_prompt[0].rearrange("(t p) d -> p t d", p=P), x_sample[0]]
        order = [(KI_OFF, KW)] + [(QI_OFF + P * i, P) for i in range(4)] + [(K_OFF, P)] \
            + [(P * i, P) for i in range(4)] + [(U_OFF + P * i, P) for i in range(4)]
        chunk_of = [0] * 5 + [1] * 5 + [2] * 4
        chunks = [(QI_OFF, U_OFF), (0, QI_OFF), (U_OFF, IN)]
        PB = 4

        block = ctx.enter_context(nc.Block())

        @block.sync
        def _(sp):
            sp.dma_start(rows[:, 0:2, :], x_views[0]).then_inc(x_in[0], 16)
            sp.wait_ge(zero_rows, 1)
            sp.dma_start(rows[0:TS, 2, :], x_views[1]).then_inc(x_in[1], 16)
            sp.dma_start(lnb[:, 0, :], ln0_g.partition_broadcast(P)).then_inc(ln_in[0], 16)
            sp.dma_start(lnb[:, 1, :], ln0_b.partition_broadcast(P)).then_inc(ln_in[0], 16)
            w_in_v = w_in[0].rearrange("(p j) n -> p j n", j=KT)
            for i, (a, b) in enumerate(chunks):
                sp.dma_start(w_in_sb[:, :, a:b], w_in_v[:, :, a:b]).then_inc(w_in_in[i], 16)
                if i == 0:
                    sp.dma_start(cache_rows[:, :, 0:HEAD_DIM],
                                 cache_k[0, 0].rearrange("(c p) d -> p c d", p=P)).then_inc(cache_in, 16)
                    sp.dma_start(cache_rows[:, :, HEAD_DIM:P],
                                 cache_kidx[0, 0].rearrange("(c p) d -> p c d", p=P)).then_inc(cache_in, 16)
                    sp.dma_start(cache_vr[:, :, :],
                                 cache_v[0, 0].rearrange("(c p) d -> p c d", p=P)).then_inc(cache_in, 16)
                    sp.dma_start(state_rows[:, :], state_pool[0, 0]).then_inc(state_in, 16)
            sp.dma_start(pool_w_sb[:, :, :], pool_w[0].rearrange("g c d -> c g d")).then_inc(small_in, 16)
            sp.dma_start(pool_scale_sb[:, :], pool_scale[0].rearrange("(g p) -> p g", p=P),
                         allow_slow_non_contiguous=True).then_inc(small_in, 16)
            sp.dma_start(w_router_sb[:, :, :], w_router[0].rearrange("(p j) n -> p j n", j=KT)).then_inc(small_in, 16)
            sp.dma_start(b_router_sb[:, :], b_router[0].partition_broadcast(P)).then_inc(small_in, 16)
            for part in range(3):
                r = slice(part * NE, (part + 1) * NE)
                sp.dma_start(bias_f[r, 0:2 * F], b1[0]).then_inc(bias_in, 16)
                sp.dma_start(bias_f[r, 2 * F:3 * F], b2[0]).then_inc(bias_in, 16)
            for s in range(2):
                sp.dma_start(ring[:, s, :], w1_v[0, :, s * SLOT:(s + 1) * SLOT]).then_inc(w_in_slot[s], 16)
            sp.wait_ge(ln_done, NT)
            sp.dma_start(lnb[:, 0, :], ln1_g[0].partition_broadcast(P)).then_inc(ln_in[1], 16)
            sp.dma_start(lnb[:, 1, :], ln1_b[0].partition_broadcast(P)).then_inc(ln_in[1], 16)
            sp.wait_ge(proj_ps, len(order))
            sp.dma_start(w_o_sb, w_o[0].rearrange("(k p) n -> p k n", p=P)).then_inc(w_o_in, 16)
            sp.wait_ge(attT_ps, NT)
            sp.wait_ge(att_ready, NT)
            sp.wait_ge(poolmm_ps, 4)
            sp.wait_ge(rows_out, 16 * 11)
            sp.wait_ge(bias_ready, 1)
            for s in range(2, 4):
                sp.dma_start(ring[:, s, :], w1_v[0, :, s * SLOT:(s + 1) * SLOT]).then_inc(w_in_slot[s], 16)
            for h in range(2):
                sp.dma_start(ring[:, 4 + h, :], w2_v[0, h]).then_inc(w_in_slot[4 + h], 16)
            sp.wait_ge(ln_done, 2 * NT)
            sp.dma_start(lnb[:, 0, :], ln2_g[0].partition_broadcast(P)).then_inc(ln_in[2], 16)
            sp.dma_start(lnb[:, 1, :], ln2_b[0].partition_broadcast(P)).then_inc(ln_in[2], 16)
            with sp.Fori(1, NE) as e:
                for s in range(4):
                    sp.wait_ge(slot_free[s], e)
                    sp.dma_start(ring[:, s, :], w1_v[bass.ds(e, 1), :, s * SLOT:(s + 1) * SLOT]
                                 .rearrange("e p n -> p (e n)")).then_inc(w_in_slot[s], 16)
                for h in range(2):
                    sp.wait_ge(slot_free[4 + h], e)
                    sp.dma_start(ring[:, 4 + h, :], w2_v[bass.ds(e, 1), h]
                                 .rearrange("e p n -> p (e n)")).then_inc(w_in_slot[4 + h], 16)

        @block.gpsimd
        def _(pool):
            nc.gpsimd.memset(rows[:, 2, :], 0.0).then_inc(zero_rows, 1)
            nc.gpsimd.memset(ident[:, :], 0.0).then_inc(ident0, 1)
            pool.wait_ge(ident0, 1)
            nc.gpsimd.affine_select(out=ident[:, :], in_=ident[:, :], compare_op=ALU.not_equal, fill=1.0, base=0,
                                    pattern=[[-1, P]], channel_multiplier=1).then_inc(ident_ready, 1)
            nc.gpsimd.memset(before[:, :], 0.0).then_inc(before0, 1)
            pool.wait_ge(before0, 1)
            nc.gpsimd.affine_select(out=before[:, :], in_=before[:, :], compare_op=ALU.is_ge, fill=1.0, base=0,
                                    pattern=[[-1, P]], channel_multiplier=1).then_inc(const_ready, 1)
            nc.gpsimd.memset(ones_b[:, :], 1.0).then_inc(const_ready, 1)
            pool.wait_ge(ident_ready, 1)
            nc.gpsimd.memset(same_exp[:, NE:NE + 1], 0.0)
            nc.gpsimd.tensor_tensor(same_exp[:, 0:NE], ident[0:3 * NE, 0:NE], ident[0:3 * NE, NE:2 * NE],
                                    ALU.add).then_inc(same0, 1)
            pool.wait_ge(same0, 1)
            nc.gpsimd.tensor_tensor(same_exp[:, 0:NE], same_exp[:, 0:NE], ident[0:3 * NE, 2 * NE:3 * NE],
                                    ALU.add).then_inc(const_ready, 1)
            nc.gpsimd.memset(logits[:, :, :], 0.0).then_inc(const_ready, 1)
            nc.gpsimd.iota(iota_slot[:, :], [[1, LAST_BLK * BLK]], base=0, channel_multiplier=0,
                           allow_small_or_imprecise_dtypes=True).then_inc(const_ready, 1)
            nc.gpsimd.iota(iota_exp[:, :], [[1, NE]], base=0, channel_multiplier=0,
                           allow_small_or_imprecise_dtypes=True).then_inc(const_ready, 1)
            nc.gpsimd.iota(rcount[:, :, :], [[0, 4], [1, 16]], base=1, channel_multiplier=0,
                           allow_small_or_imprecise_dtypes=True).then_inc(const_ready, 1)
            nc.gpsimd.memset(uext[:, :, 0:POOL_PAST], 0.0).then_inc(const_ready, 1)
            pool.wait_ge(proj_sb, len(order))
            pool.wait_ge(stateT_sb, 1)
            pool.wait_ge(proj_ps, len(order))
            src, dst, step = uext, sums_a, 0
            for level in range(4):
                back = 1 << level
                a = 2 * back - 1
                nc.gpsimd.tensor_tensor(dst[:, level:4, a:UW], src[:, level:4, a:UW],
                                        src[:, level:4, a - back:UW - back], ALU.add).then_inc(pool_step, 1)
                step += 1
                pool.wait_ge(pool_step, step)
                src, dst = dst, (sums_b if dst is sums_a else sums_a)

            pool.wait_ge(bias_in, 6 * 16)
            nc.gpsimd.tensor_copy(bias_parts, bias_f).then_inc(bias_step, 1)
            for part in (1, 2):
                r = slice(part * NE, 3 * NE)
                pool.wait_ge(bias_step, 2 * part - 1)
                for a in range(part, 3):
                    q = slice(a * NE, (a + 1) * NE)
                    last = nc.gpsimd.tensor_tensor(bias_f[q, :], bias_f[q, :], bias_parts[q, :], ALU.subtract)
                last.then_inc(bias_step, 1)
                pool.wait_ge(bias_step, 2 * part)
                for a in range(part, 3):
                    q = slice(a * NE, (a + 1) * NE)
                    last = nc.gpsimd.tensor_copy(bias_parts[q, :], bias_f[q, :])
                last.then_inc(bias_step if part == 1 else bias_ready, 1)

            pool.wait_ge(kvrow_sb, 2)
            for t in range(2):
                for off, dram in ((0, k_prompt), (HEAD_DIM, v_prompt), (P, kidx_prompt)):
                    pool.dma_start(dram[0, 0, t * P:(t + 1) * P, :],
                                   kv_rows[:, t, off:off + HEAD_DIM]).then_inc(rows_out, 16)
            for off, dram in ((0, k_sample), (HEAD_DIM, v_sample), (P, kidx_sample)):
                pool.dma_start(dram[0, 0], kv_rows[0:TS, 2, off:off + HEAD_DIM]).then_inc(rows_out, 16)
            pool.wait_ge(lastu_sb, 1)
            pool.dma_start(pool_prompt[0, 0], last_u[:, 0, :]).then_inc(rows_out, 16)
            pool.dma_start(pool_sample[0, 0], last_u[:, 1, :]).then_inc(rows_out, 16)
            pool.wait_ge(rows_out, 16 * 11)

        @block.tensor
        def _(pe):
            mm = nc.tensor.matmul
            tr = nc.tensor.transpose

            def rows_to_tokT(done, ready, base):
                for t, (t0, n, _) in enumerate(tiles):
                    pe.wait_ge(done, base + t + 1)
                    for j in range(KT):
                        last = tr(ps[:, t * 2 + j // 4 if t < 2 else 4, (j % 4) * P:(j % 4) * P + n] if t < 2 else
                                  ps[:, 4, j * TS:(j + 1) * TS],
                                  rows[0:n, t, j:D:KT], ident[0:n, 0:n])
                        if t < 2 and j % 4 == 3:
                            last.then_inc(ready, 1)
                    if t == 2:
                        last.then_inc(ready, 1)

            pe.wait_ge(ident_ready, 1)
            rows_to_tokT(ln_done, tokT_ps, 0)

            def project(i):
                c0, w = order[i]
                pe.wait_ge(w_in_in[chunk_of[i]], 16)
                if i == 0:
                    pe.wait_ge(tokT_sb, 5)
                if i >= 4:
                    pe.wait_ge(proj_sb, i - 3)
                for j in range(KT):
                    last = mm(ps[0:w, PB + i % 4, 0:TOK], w_in_sb[:, j, c0:c0 + w], tokT[:, j, :],
                              start=(j == 0), stop=(j == KT - 1))
                last.then_inc(proj_ps, 1)

            for i in range(6):
                project(i)
            pe.wait_ge(cache_in, 48)
            for c in range(2):
                last = tr(ps[:, 0, c * P:(c + 1) * P], cache_rows[:, c, :], ident[:, :])
            last.then_inc(cacheT_ps, 1)
            pe.wait_ge(proj_sb, 6)
            for t, (t0, n, _) in enumerate(tiles):
                bank, at = (1, t * (P + KW)) if t < 2 else (2, 0)
                tr(ps[0:n, bank, at:at + P], kvT[:, t0:t0 + n], ident[:, :])
                last = tr(ps[0:n, bank, at + P:at + P + KW], kwT[0:KW, t0:t0 + n], ident[0:KW, 0:KW])
                if t >= 1:
                    last.then_inc(kvrow_ps, 1)
            pe.wait_ge(cacheT_sb, 1)
            pe.wait_ge(kvrow_sb, 2)
            n_pair = 0
            for t, (t0, n, nk) in enumerate(tiles):
                k0 = 0 if t < 2 else S
                for pair in range(4):
                    if n_pair >= 2:
                        pe.wait_ge(idx_relu, n_pair - 1)
                    for half in range(2):
                        r = slice(half * HEAD_DIM, (half + 1) * HEAD_DIM)
                        last = mm(ps[0:n, 2 * (n_pair % 2) + half, 0:nk], qiT[r, pair, t0:t0 + n],
                                  kiT2[r, k0:k0 + nk], start=True, stop=True)
                    last.then_inc(idx_ps, 1)
                    n_pair += 1
            for i in range(6, 14):
                project(i)
            pe.wait_ge(state_in, 16)
            pe.wait_ge(idx_relu, 12)
            for g in range(4):
                last = tr(ps[:, 3, g * POOL_PAST:(g + 1) * POOL_PAST], state_rows[:, g * P:(g + 1) * P],
                          ident[ident_state, ident_state])
            last.then_inc(stateT_ps, 1)

            n_qk = 0
            pe.wait_ge(proj_sb, 10)

            def logits_of(t, n_qk):
                t0, n, nk = tiles[t]
                k0 = 0 if t < 2 else S
                for pair in range(4):
                    if n_qk >= 2:
                        pe.wait_ge(qk_used, n_qk - 1)
                    elif n_qk == 1:
                        pe.wait_ge(stateT_sb, 1)
                    for half in range(2):
                        r = slice(half * HEAD_DIM, (half + 1) * HEAD_DIM)
                        last = mm(ps[0:n, 2 * (n_qk % 2) + half, 0:nk], qT[r, pair, t0:t0 + n],
                                  kT2[r, k0:k0 + nk], start=True, stop=True)
                    last.then_inc(qk_ps, 1)
                    n_qk += 1
                return n_qk

            pe_groups = [0]

            def attend(t):
                t0, n, nk = tiles[t]
                nl = -(-nk // P)
                if t == 0:
                    pe.wait_ge(proj_sb, 14)
                pe.wait_ge(exp_done, t + 1)
                for c in range(nl):
                    lw = min(P, nk - c * P)
                    for hg in range(2):
                        g = pe_groups[0]
                        if g >= 2:
                            pe.wait_ge(probsT_sb, g - 1)
                        for q in range(4):
                            h = 4 * hg + q
                            last = tr(ps[0:lw, 4 + g % 2, q * n:(q + 1) * n],
                                      probs[0:n, h * nk + c * P:h * nk + c * P + lw], ident[0:n, 0:n])
                        last.then_inc(probsT_ps, 1)
                        pe_groups[0] += 1
                pe.wait_ge(probsT_sb, pe_groups[0])
                if t >= 1:
                    pe.wait_ge(att_ready, t)
                for h in range(N_HEADS):
                    for c in range(nl):
                        lw = min(P, nk - c * P)
                        if t < 2:
                            v = kv_rows[0:lw, c, HEAD_DIM:P]
                        else:
                            v = cache_vr[0:lw, c, :] if c < 2 else kv_rows[0:lw, 2, HEAD_DIM:P]
                        at = (c * N_HEADS + h) * n
                        last = mm(ps[0:n, 6, h * HEAD_DIM:(h + 1) * HEAD_DIM], probsT[0:lw, at:at + n], v,
                                  start=(c == 0), stop=(c == nl - 1))
                last.then_inc(pv_ps, 1)

            def turn_att(t):
                t0, n, _ = tiles[t]
                pe.wait_ge(att_ready, t + 1)
                if t >= 1:
                    pe.wait_ge(attT_sb, t)
                for k in range(4):
                    last = tr(ps[:, 7, k * n:(k + 1) * n], att_rows[0:n, k * P:(k + 1) * P], ident[0:n, 0:n])
                last.then_inc(attT_ps, 1)

            for t in range(NT):
                n_qk = logits_of(t, n_qk)
                attend(t)
                if t == 0:
                    pe.wait_ge(proj_sb, len(order))
                    pe.wait_ge(qk_used, n_qk)
                    for part, at in ((0, U_S - POOL_PAST), (1, UW - POOL_PAST)):
                        for g in range(4):
                            last = tr(ps[0:POOL_PAST, part, g * P:(g + 1) * P], uext[:, g, at:at + POOL_PAST],
                                      ident[:, :])
                    last.then_inc(lastu_ps, 1)
                    pe.wait_ge(lastu_sb, 1)
                turn_att(t)
            pe.wait_ge(small_in, 64)
            pe.wait_ge(pool_diff, 1)
            pe.wait_ge(qk_used, n_qk)
            for g in range(4):
                mm(ps[:, g, 0:TOK], pool_w_sb[:, g, :], diffT[:, g, :], start=True, stop=True).then_inc(poolmm_ps, 1)
            pe.wait_ge(w_o_in, 16)
            pe.wait_ge(attT_sb, NT)
            pe.wait_ge(poolT_sb, 4)
            for t, (t0, n, _) in enumerate(tiles):
                for k in range(KT):
                    for half in range(2):
                        dst = ps[0:n, 2 * t + half, :] if t < 2 else ps[half * TS:(half + 1) * TS, 4, :]
                        last = mm(dst, tokT[:, k, t0:t0 + n], w_o_sb[:, k, half * 512:(half + 1) * 512],
                                  start=(k == 0), stop=(k == KT - 1))
                last.then_inc(wo_ps, 1)
            rows_to_tokT(ln_done, h1T_ps, NT)
            pe.wait_ge(h1T_sb, 5)
            for t, (t0, n, _) in enumerate(tiles):
                for j in range(KT):
                    last = mm(ps[0:n, 6, t * NE:(t + 1) * NE], tokT[:, j, t0:t0 + n], w_router_sb[:, j, :],
                              start=(j == 0), stop=(j == KT - 1))
            last.then_inc(router_ps, 1)
            pe.wait_ge(const_ready, 8)
            pe.wait_ge(gates_ready, 1)
            for t in range(NT):
                for s in range(t + 1):
                    mm(ps[:, 4, t * NE:(t + 1) * NE], ones_b[:, :] if s < t else before[:, :], chosen_b[:, s, :],
                       start=(s == 0), stop=(s == t))
            for s in range(NT):
                last = mm(ps[:, 4, NT * NE:(NT + 1) * NE], ones_b[:, :], chosen_b[:, s, :],
                          start=(s == 0), stop=(s == NT - 1))
            last.then_inc(prefix_ps, 1)
            def gather(one, ready, want, done):
                pe.wait_ge(ready, want)
                for k in range(KT):
                    for t in range(NT):
                        last = mm(ps_x[:, k, :], rows[:, t, k:D:KT], one[:, t, 0, :],
                                  start=(t == 0), stop=(t == NT - 1))
                last.then_inc(done, 1)

            def up_products(x, e, free):
                for c in range(2):
                    for g in range(2):
                        a = c * F + g * 512
                        mm(ps_gu[g * BLK:(g + 1) * BLK, c, :], sel[:, :], bias_parts[:, a:a + 512],
                           start=True, stop=False)
                for k in range(KT):
                    if k % 2 == 0:
                        pe.wait_ge(w_in_slot[k // 2], 16 * (e + 1))
                    for c in range(2):
                        for g in range(2):
                            a = c * F + g * 512
                            last = mm(ps_gu[g * BLK:(g + 1) * BLK, c, :], x[:, k, :], w1_t[:, k, a:a + 512],
                                      start=False, stop=(k == KT - 1))
                    if free and k % 2 == 1 and k < KT - 1:
                        last.then_inc(slot_free[k // 2], 1)
                return last

            def turn_h():
                for c in range(4):
                    last = tr(ps_hT[:, c * P:(c + 1) * P], h_sb[:, c:512:4], ident[:, :])
                return last

            def down_products(e, h, free):
                if h == 0:
                    for g in range(2):
                        a = 2 * F + g * 512
                        mm(ps_y[g * BLK:(g + 1) * BLK, :], sel[:, :], bias_parts[:, a:a + 512],
                           start=True, stop=False)
                pe.wait_ge(w_in_slot[4 + h], 16 * (e + 1))
                for c in range(4):
                    for g in range(2):
                        last = mm(ps_y[g * BLK:(g + 1) * BLK, :], hT[:, c, h, :],
                                  w2_t[:, h, c, g * 512:(g + 1) * 512],
                                  start=False, stop=(h == 1 and c == 3))
                if free:
                    last.then_inc(slot_free[4 + h], 1)
                return last

            def turn_pick(src, dst, gates_of, done):
                for t in range(NT):
                    tr(dst[:, t * P:(t + 1) * P], src[:, t].rearrange("p h s -> p (h s)"), ident[:, :])
                for t in range(NT):
                    last = mm(dst[:, TOKP:TOKP + 1], src[:, t].rearrange("p h s -> p (h s)"),
                              gate_w[:, t, gates_of], start=(t == 0), stop=(t == NT - 1))
                last.then_inc(done, 1)

            def combine(t, done, dst=ps_c):
                for g in range(2):
                    last = mm(dst[:, g, :], giveT[:, t * P:(t + 1) * P], y_sb[:, g * 512:(g + 1) * 512],
                              start=True, stop=True)
                last.then_inc(done, 1)

            def x_combine(t, done):
                for g in range(2):
                    r = slice(g * BLK, (g + 1) * BLK)
                    last = mm(ps_c[:, g, :], x_giveT[r, t * P:(t + 1) * P], x_y[r, :], start=True, stop=True)
                last.then_inc(done, 1)

            gather(pick, pick_ready, 1, x_gathered)
            pe.wait_ge(gates_ready, 2)
            turn_pick(pick, ps_g, slice(0, 1), giveT_done)
            pe.wait_ge(bias_ready, 1)
            pe.wait_ge(blocks_ready, 1)
            with pe.Fori(0, NE) as e:
                more = pe.value_load(blocks_i[0:1, 0, bass.ds(e, 1)], min_val=0, max_val=LAST_BLK - 1)
                with pe.If(more > 0):
                    base = pe.value_load(blocks_i[0:1, 1, bass.ds(e, 1)], min_val=0, max_val=NE * LAST_BLK)
                    with pe.Fori(0, more) as i:
                        b = base + i
                        pe.wait_ge(xT_ready, e + 1)
                        pe.wait_ge(y_ready, e + 1)
                        gather(x_pick, x_pick_ready, b + 1, x_x_gathered)
                        turn_pick(x_pick, x_ps_g, bass.ds(e, 1), x_giveT_done)
                        pe.wait_ge(x_xT_ready, b + 1)
                        pe.wait_ge(sel_ready, e + 1)
                        up_products(x_xT, e, False).then_inc(x_gu_done, 1)
                        pe.wait_ge(x_giveT_ready, b + 1)
                        pe.wait_ge(x_h_ready, b + 1)
                        turn_h().then_inc(x_hT_done, 1)
                        pe.wait_ge(x_hT_ready, b + 1)
                        down_products(e, 0, False)
                        down_products(e, 1, False).then_inc(x_y_done, 1)
                        pe.wait_ge(x_y_ready, b + 1)
                        for t in range(NT):
                            x_combine(t, x_comb_done[t])
                            pe.wait_ge(x_acc_done[t], b + 1)
                pe.wait_ge(xT_ready, e + 1)
                pe.wait_ge(sel_ready, e + 1)
                up_products(xT, e, True).then_inc(slot_free[3], 1)
                pe.wait_ge(y_ready, e + 1)
                pe.wait_ge(giveT_ready, e + 1)
                combine(0, comb_done[0])
                gather(pick, pick_ready, e + 2, x_gathered)
                pe.wait_ge(h_ready, e + 1)
                turn_h().then_inc(hT_done, 1)
                pe.wait_ge(acc_done[0], e + 1)
                combine(1, comb_done[1])
                pe.wait_ge(hT_ready, e + 1)
                down_products(e, 0, True)
                pe.wait_ge(acc_done[1], e + 1)
                combine(2, comb_done[2])
                down_products(e, 1, True)
                pe.wait_ge(giveT_ready, e + 2)
                turn_pick(pick, ps_g, bass.ds(e + 1, 1), giveT_done)
            pe.wait_ge(y_ready, NE + 1)
            pe.wait_ge(giveT_ready, NE + 1)
            for t in range(NT):
                combine(t, comb_done[t], dst=(ps_c, ps[:, 0:2, :], ps[:, 2:4, :])[t])

        @block.scalar
        def _(act):
            copy = nc.scalar.copy

            def sqrt_of(base):
                for t, (_, n, _) in enumerate(tiles):
                    act.wait_ge(var_ready, base + t + 1)
                    nc.scalar.activation(std[0:n, t:t + 1], veps[0:n, t:t + 1], ACT.Sqrt).then_inc(std_ready, 1)

            def tokT_copies(src, done):
                for i in range(5):
                    act.wait_ge(src, i + 1)
                    if i < 4:
                        t, q = i // 2, i % 2
                        copy(tokT[:, 4 * q:4 * q + 4, t * P:(t + 1) * P],
                             ps[:, i, :].rearrange("p (j t) -> p j t", j=4)).then_inc(done, 1)
                    else:
                        copy(tokT[:, :, S:TOK],
                             ps[:, 4, 0:KT * TS].rearrange("p (j t) -> p j t", j=KT)).then_inc(done, 1)

            sqrt_of(0)
            tokT_copies(tokT_ps, tokT_sb)

            def take(i):
                c0, w = order[i]
                bank = ps[:, PB + i % 4, :]
                act.wait_ge(proj_ps, i + 1)
                if i in (0, 5):
                    lo, raw = (kiT2, kwT) if i == 0 else (kT2, kvT)
                    for half in range(2):
                        r = slice(half * HEAD_DIM, (half + 1) * HEAD_DIM)
                        copy(lo[r, 0:S], bank[0:HEAD_DIM, 0:S])
                        copy(lo[r, S + PAST:S + PAST + TS], bank[0:HEAD_DIM, S:TOK])
                    copy(raw[0:w, :], bank[0:w, 0:TOK]).then_inc(proj_sb, 1)
                elif i < 5:
                    copy(qiT[:, i - 1, :], bank[:, 0:TOK]).then_inc(proj_sb, 1)
                elif i < 10:
                    copy(qT[:, i - 6, :], bank[:, 0:TOK]).then_inc(proj_sb, 1)
                else:
                    g = i - 10
                    copy(uext[:, g, POOL_PAST:U_S], bank[:, 0:S])
                    copy(uext[:, g, U_S + POOL_PAST:UW], bank[:, S:TOK]).then_inc(proj_sb, 1)

            for i in range(6):
                take(i)
            act.wait_ge(cacheT_ps, 1)
            for half in range(2):
                r = slice(half * HEAD_DIM, (half + 1) * HEAD_DIM)
                copy(kT2[r, S:S + PAST], ps[0:HEAD_DIM, 0, 0:PAST])
                last = copy(kiT2[r, S:S + PAST], ps[HEAD_DIM:P, 0, 0:PAST])
            last.then_inc(cacheT_sb, 1)
            act.wait_ge(kvrow_ps, 1)
            copy(kv_rows[:, 0:2, :], ps[:, 1, 0:2 * (P + KW)].rearrange("p (t n) -> p t n", t=2)).then_inc(kvrow_sb, 1)
            act.wait_ge(kvrow_ps, 2)
            copy(kv_rows[0:TS, 2, :], ps[0:TS, 2, 0:P + KW]).then_inc(kvrow_sb, 1)
            n_pair = 0
            for t, (t0, n, nk) in enumerate(tiles):
                for pair in range(4):
                    act.wait_ge(idx_ps, n_pair + 1)
                    if n_pair >= 2:
                        act.wait_ge(idx_used, n_pair - 1)
                    b = n_pair % 2
                    nc.scalar.activation(relu_sb[0:n, b, :, 0:nk], ps[0:n, 2 * b:2 * b + 2, 0:nk],
                                         ACT.Relu).then_inc(idx_relu, 1)
                    n_pair += 1
            for i in range(6, 14):
                take(i)
            act.wait_ge(stateT_ps, 1)
            copy(uext[:, :, U_S:U_S + POOL_PAST],
                 ps[:, 3, 0:4 * POOL_PAST].rearrange("p (g n) -> p g n", g=4)).then_inc(stateT_sb, 1)

            groups = 0
            for t, (t0, n, nk) in enumerate(tiles):
                act.wait_ge(max_ready, t + 1)
                for h in range(N_HEADS):
                    p = probs[0:n, h * nk:(h + 1) * nk]
                    last = nc.scalar.activation(p, p, ACT.Exp, bias=neg_max[0:n, t, h:h + 1],
                                                accum_out=row_sum[0:n, t, h:h + 1])
                last.then_inc(exp_done, 1)
                for c in range(-(-nk // P)):
                    lw = min(P, nk - c * P)
                    for hg in range(2):
                        act.wait_ge(probsT_ps, groups + 1)
                        if t >= 1 and c == 0 and hg == 0:
                            act.wait_ge(pv_ps, t)
                        at = (c * N_HEADS + 4 * hg) * n
                        copy(probsT[0:lw, at:at + 4 * n], ps[0:lw, 4 + groups % 2, 0:4 * n]).then_inc(probsT_sb, 1)
                        groups += 1
                if t == 0:
                    act.wait_ge(lastu_ps, 1)
                    copy(last_u[:, :, :], ps[0:POOL_PAST, 0:2, :]).then_inc(lastu_sb, 1)
                act.wait_ge(attT_ps, t + 1)
                copy(tokT[:, 0:4, t0:t0 + n],
                     ps[:, 7, 0:4 * n].rearrange("p (k t) -> p k t", k=4)).then_inc(attT_sb, 1)
            sqrt_of(NT)
            tokT_copies(h1T_ps, h1T_sb)
            act.wait_ge(top_ready, 1)
            nc.scalar.activation(top_w[:, :, :], top_w[:, :, :], ACT.Exp).then_inc(top_exp, 1)

            def gated_high(done):
                for g in range(2):
                    r = slice(g * BLK, (g + 1) * BLK)
                    nc.scalar.activation(y_sb[0:BLK, g * 512:(g + 1) * 512], ps_y[r, :], ACT.Copy,
                                         scale=gcol[r, :]).then_inc(done, 1)

            act.wait_ge(x_gathered, 1)
            copy(xT, ps_x).then_inc(xT_ready, 1)
            act.wait_ge(blocks_ready, 1)
            with act.Fori(0, NE) as e:
                more = act.value_load(blocks_i[0:1, 0, bass.ds(e, 1)], min_val=0, max_val=LAST_BLK - 1)
                with act.If(more > 0):
                    base = act.value_load(blocks_i[0:1, 1, bass.ds(e, 1)], min_val=0, max_val=NE * LAST_BLK)
                    with act.Fori(0, more) as i:
                        b = base + i
                        act.wait_ge(x_x_gathered, b + 1)
                        copy(x_xT, ps_x).then_inc(x_xT_ready, 1)
                        act.wait_ge(x_giveT_done, b + 1)
                        copy(x_giveT, x_ps_g[:, 0:TOKP])
                        copy(x_gcol[:, :], x_ps_g[:, TOKP:TOKP + 1]).then_inc(x_giveT_ready, 1)
                        act.wait_ge(x_gate_ready, b + 1)
                        nc.scalar.activation(sig_sb, g_sb, ACT.Sigmoid, scale=SWIGLU_ALPHA).then_inc(x_sig_ready, 1)
                        act.wait_ge(x_hT_done, b + 1)
                        copy(hT, ps_hT.rearrange("p (c h s) -> p c h s", c=4, h=2)).then_inc(x_hT_ready, 1)
                        act.wait_ge(x_y_done, b + 1)
                        act.wait_ge(x_giveT_ready, b + 1)
                        nc.scalar.activation(x_y, ps_y, ACT.Copy, scale=x_gcol[:, :]).then_inc(x_y_ready, 1)
                act.wait_ge(gate_ready, e + 1)
                nc.scalar.activation(sig_sb, g_sb, ACT.Sigmoid, scale=SWIGLU_ALPHA).then_inc(sig_ready, 1)
                act.wait_ge(x_gathered, e + 2)
                copy(xT, ps_x).then_inc(xT_ready, 1)
                act.wait_ge(hT_done, e + 1)
                copy(hT, ps_hT.rearrange("p (c h s) -> p c h s", c=4, h=2)).then_inc(hT_ready, 1)
                act.wait_ge(giveT_done, e + 1)
                act.wait_ge(comb_done[2], e + 1)
                copy(giveT[:, :], ps_g[:, 0:TOKP])
                copy(gcol[:, :], ps_g[:, TOKP:TOKP + 1]).then_inc(giveT_ready, 1)
                act.wait_ge(giveT_ready, e + 2)
                act.wait_ge(slot_free[5], e + 1)
                gated_high(y_high)
            sqrt_of(2 * NT)
            for t in range(2):
                act.wait_ge(ln_done, 2 * NT + t + 1)
                act.dma_start(y_prompt[0, t * P:(t + 1) * P, :], out_acc[:, t, :]).then_inc(final_out, 16)
            act.wait_ge(ln_done, 3 * NT)
            act.dma_start(y_sample[0], out_acc[0:TS, 2, :]).then_inc(final_out, 16)
            act.wait_ge(final_out, 48)

        @block.vector
        def _(dve):
            v = nc.vector
            step = [0]

            def link(ins):
                step[0] += 1
                ins.then_inc(dve_step, 1)
                dve.wait_ge(dve_step, step[0])

            def layer_norm(t, n, src, base):
                for q in range(2):
                    ins = v.bn_stats(stats[0:n, t, q, :], src[:, q * 512:(q + 1) * 512])
                link(ins)
                link(v.bn_aggr(moments[0:n, t, :], stats[0:n, t, :, :]))
                v.tensor_scalar(veps[0:n, t:t + 1], moments[0:n, t, 1:2], LN_EPS, None, ALU.add).then_inc(var_ready, 1)
                link(v.scalar_tensor_tensor(src, src, moments[0:n, t, 0:1], lnb[0:n, 0, :], ALU.subtract, ALU.mult))
                dve.wait_ge(std_ready, base + t + 1)
                link(v.reciprocal(rstd[0:n, t:t + 1], std[0:n, t:t + 1]))
                v.scalar_tensor_tensor(src, src, rstd[0:n, t:t + 1], lnb[0:n, 1, :], ALU.mult, ALU.add)\
                    .then_inc(ln_done, 1)

            dve.wait_ge(ln_in[0], 32)
            for t, (_, n, _) in enumerate(tiles):
                dve.wait_ge(x_in[t // 2], 16)
                layer_norm(t, n, rows[0:n, t, :], 0)

            dve.wait_ge(const_ready, 8)
            for g, w in enumerate(WINDOWS):
                ins = v.tensor_scalar(rcount[:, g, :], rcount[:, g, :], float(w), None, ALU.min)
            link(ins)
            link(v.reciprocal(rcount[:, :, :], rcount[:, :, :]))

            dve.wait_ge(kvrow_sb, 2)
            for t, (_, n, _) in enumerate(tiles):
                ins = v.tensor_scalar(w_idx[0:n, t, :], kv_rows[0:n, t, P + HEAD_DIM:P + KW],
                                      N_HEADS ** -0.5 * HEAD_DIM ** -0.5, None, ALU.mult)
            link(ins)
            n_pair = 0
            for t, (_, n, nk) in enumerate(tiles):
                sc = score[0:n, t, 0:nk]
                for pair in range(4):
                    dve.wait_ge(idx_relu, n_pair + 1)
                    for half in range(2):
                        r, w = relu_sb[0:n, n_pair % 2, half, 0:nk], w_idx[0:n, t, 2 * pair + half:2 * pair + half + 1]
                        if pair == 0 and half == 0:
                            link(v.tensor_scalar(sc, r, w, None, ALU.mult))
                        elif half == 0:
                            link(v.scalar_tensor_tensor(sc, r, w, sc, ALU.mult, ALU.add))
                        else:
                            v.scalar_tensor_tensor(sc, r, w, sc, ALU.mult, ALU.add).then_inc(idx_used, 1)
                            dve.wait_ge(idx_used, n_pair + 1)
                    n_pair += 1
                if t < 2:
                    link(v.memset(score[0:CHUNK, t, nk - CHUNK:nk], HIDDEN_KEY))
            for t, (_, n, nk) in enumerate(tiles):
                sc = score[0:n, t, 0:nk]
                assert topk[t] % 8 == 0
                for _ in range(topk[t] // 8):
                    link(v.max(max8[0:n, t, :], sc))
                    link(v.match_replace(sc, max8[0:n, t, :], sc, TAKEN))
                link(v.tensor_scalar(sc, sc, TAKEN / 2, HIDDEN_KEY, ALU.is_gt, ALU.mult))

            n_qk = 0
            for t, (_, n, nk) in enumerate(tiles):
                if t >= 1:
                    dve.wait_ge(probsT_ps, [2, 6][t - 1])
                for pair in range(4):
                    dve.wait_ge(qk_ps, n_qk + 1)
                    for half in range(2):
                        h = 2 * pair + half
                        ins = v.tensor_tensor_reduce(
                            out=probs[0:n, h * nk:(h + 1) * nk], in0=ps[0:n, 2 * (n_qk % 2) + half, 0:nk],
                            in1=score[0:n, t, 0:nk], scale=HEAD_DIM ** -0.5, scalar=TAKEN, op0=ALU.add, op1=ALU.max,
                            accum_out=row_max[0:n, t, h:h + 1])
                    ins.then_inc(qk_used, 1)
                    n_qk += 1
                dve.wait_ge(qk_used, n_qk)
                v.tensor_scalar(neg_max[0:n, t, :], row_max[0:n, t, :], -1.0, None, ALU.mult).then_inc(max_ready, 1)
                dve.wait_ge(exp_done, t + 1)
                link(v.reciprocal(row_inv[0:n, t, :], row_sum[0:n, t, :]))
                dve.wait_ge(pv_ps, t + 1)
                if t >= 1:
                    dve.wait_ge(attT_ps, t)
                v.tensor_tensor(att_rows[0:n, :].rearrange("p (h d) -> p h d", h=N_HEADS),
                                ps[0:n, 6, :].rearrange("p (h d) -> p h d", h=N_HEADS),
                                row_inv[0:n, t, :].unsqueeze(2).broadcast_to([n, N_HEADS, HEAD_DIM]),
                                ALU.mult).then_inc(att_ready, 1)
                if t == 0:
                    dve.wait_ge(pool_step, 4)
                    dve.wait_ge(small_in, 64)
                    for g, w in enumerate(WINDOWS):
                        s = sums_a if g % 2 == 0 else sums_b
                        link(v.tensor_tensor(s[:, g, POOL_PAST:POOL_PAST + 16], s[:, g, POOL_PAST:POOL_PAST + 16],
                                             rcount[:, g, :], ALU.mult))
                        v.tensor_tensor(diffT[:, g, 0:16], s[:, g, POOL_PAST:POOL_PAST + 16],
                                        uext[:, g, POOL_PAST:POOL_PAST + 16], ALU.subtract)
                        v.scalar_tensor_tensor(diffT[:, g, 16:S], s[:, g, POOL_PAST + 16:U_S], 1.0 / w,
                                               uext[:, g, POOL_PAST + 16:U_S], ALU.mult, ALU.subtract)
                        ins = v.scalar_tensor_tensor(diffT[:, g, S:TOK], s[:, g, U_S + POOL_PAST:UW], 1.0 / w,
                                                     uext[:, g, U_S + POOL_PAST:UW], ALU.mult, ALU.subtract)
                    ins.then_inc(pool_diff, 1)
            for g in range(4):
                dve.wait_ge(poolmm_ps, g + 1)
                v.tensor_scalar(tokT[:, 4 + g, :], ps[:, g, 0:TOK], pool_scale_sb[:, g:g + 1], None,
                                ALU.mult).then_inc(poolT_sb, 1)

            dve.wait_ge(ln_in[1], 32)
            for t, (_, n, _) in enumerate(tiles):
                dve.wait_ge(wo_ps, t + 1)
                if t < 2:
                    link(v.scalar_tensor_tensor(rows[:, t, :].rearrange("p (h n) -> p h n", h=2),
                                                rows[:, t, :].rearrange("p (h n) -> p h n", h=2), RESIDUAL,
                                                ps[:, 2 * t:2 * t + 2, :], ALU.mult, ALU.add))
                else:
                    for half in range(2):
                        r = rows[0:TS, 2, half * 512:(half + 1) * 512]
                        ins = v.scalar_tensor_tensor(r, r, RESIDUAL, ps[half * TS:(half + 1) * TS, 4, :],
                                                     ALU.mult, ALU.add)
                        link(ins)
                layer_norm(t, n, rows[0:n, t, :], NT)

            dve.wait_ge(router_ps, 1)
            for t, (_, n, _) in enumerate(tiles):
                ins = v.tensor_tensor(logits[0:n, t, :], ps[0:n, 6, t * NE:(t + 1) * NE], b_router_sb[0:n, :], ALU.add)
            link(ins)
            for t in range(NT):
                ins = v.max(top8[:, t, :], logits[:, t, :])
            link(ins)
            v.tensor_tensor(top_w[:, :, :], top8[:, :, 0:TOP_K],
                            top8[:, :, 0:1].broadcast_to([P, NT, TOP_K]), ALU.subtract).then_inc(top_ready, 1)
            for t in range(NT):
                ins = v.max_index(top_i[:, t, :], top8[:, t, :], logits[:, t, :])
            link(ins)
            link(v.tensor_copy(top_f[:, :, :], top_i[:, :, 0:TOP_K]))
            for t in range(NT):
                ins = v.tensor_tensor(onehot[:, t], iota_exp[:, :].unsqueeze(1).broadcast_to([P, TOP_K, NE]),
                                      top_f[:, t, :].unsqueeze(2).broadcast_to([P, TOP_K, NE]), ALU.is_equal)
            link(ins)
            for t in range(NT):
                ins = v.tensor_reduce(chosen[:, t, :], onehot[:, t].rearrange("p k e -> p e k"), AX, ALU.add)
            link(ins)
            v.memset(chosen[32:64, 2, :], 0.0)
            link(v.memset(chosen[64:P, 2, :], 0.0))
            v.tensor_copy(chosen_b[:, :, :], chosen[:, :, :]).then_inc(gates_ready, 1)
            dve.wait_ge(top_exp, 1)
            link(v.tensor_reduce(top_s[:, :], top_w[:, :, :], AX, ALU.add))
            link(v.reciprocal(top_r[:, :], top_s[:, :]))
            link(v.tensor_tensor(top_w[:, :, :], top_w[:, :, :],
                                 top_r[:, :].unsqueeze(2).broadcast_to([P, NT, TOP_K]), ALU.mult))
            for t in range(NT):
                ins = v.tensor_tensor(weighed[:, t], onehot[:, t],
                                      top_w[:, t, :].unsqueeze(2).broadcast_to([P, TOP_K, NE]), ALU.mult)
            link(ins)
            for t in range(NT):
                ins = v.tensor_reduce(gate_w[:, t, 0:NE], weighed[:, t].rearrange("p k e -> p e k"), AX, ALU.add)
            v.memset(gate_w[:, :, NE:NE + 1], 0.0).then_inc(gates_ready, 1)
            dve.wait_ge(gates_ready, 2)
            dve.wait_ge(prefix_ps, 1)
            link(v.scalar_tensor_tensor(place[:, :, 0:NE], ps[:, 4, 0:NT * NE].rearrange("p (t e) -> p t e", t=NT), 1.0,
                                        chosen[:, :, :], ALU.add, ALU.mult))
            link(v.memset(place[:, :, NE:NE + 1], -1.0))
            link(v.tensor_scalar(place[:, :, 0:NE], place[:, :, 0:NE], -1.0, None, ALU.add))

            first_slots = iota_slot[:, 0:BLK]

            def one_hot(dst, at, slots):
                return v.tensor_tensor(dst,
                                       slots.unsqueeze(1).unsqueeze(1).broadcast_to([P, NT, 2, BLK]),
                                       at.unsqueeze(3).broadcast_to([P, NT, 2, BLK]), ALU.is_equal)

            one_hot(pick, place[:, :, 0:1], first_slots).then_inc(pick_ready, 1)
            count = ps[0:1, 4, NT * NE:(NT + 1) * NE]
            n_more, n_incl, n_excl = (blocks_f[:, i, :] for i in range(3))
            link(v.tensor_scalar(n_more, count, float(BLK), None, ALU.is_gt))
            for b in range(2, LAST_BLK):
                link(v.scalar_tensor_tensor(n_more, count, float(b * BLK), n_more, ALU.is_gt, ALU.add))
            link(v.tensor_tensor_scan(n_incl, n_more, n_more, 0.0, ALU.add, ALU.bypass))
            link(v.tensor_tensor(n_excl, n_incl, n_more, ALU.subtract))
            v.tensor_copy(blocks_i[:, 0, :], n_more)
            v.tensor_copy(blocks_i[:, 1, :], n_excl).then_inc(blocks_ready, 1)
            for t, (_, n, _) in enumerate(tiles):
                v.tensor_scalar(out_acc[0:n, t, :], rows[0:n, t, :], RESIDUAL, None, ALU.mult).then_inc(acc_init, 1)
            dve.wait_ge(acc_init, NT)
            v.tensor_scalar(giveT[:, :], rows[:, 0, 0:TOKP], 0.0, None, ALU.mult).then_inc(giveT_ready, 1)
            v.tensor_scalar(y_sb[:, :], rows[:, 0, :], 0.0, None, ALU.mult).then_inc(y_ready, 1)

            def select(e):
                v.tensor_copy(sel[:, :], same_exp[:, e].broadcast_to([3 * NE, BLK])).then_inc(sel_ready, 1)

            def gated_low(e):
                for g in range(2):
                    r = slice(g * BLK, (g + 1) * BLK)
                    dve.wait_ge(y_high, 2 * e + 1 + g)
                    ins = v.scalar_tensor_tensor(y_sb[BLK:P, g * 512:(g + 1) * 512], ps_y[r, :], gcol[r, :],
                                                 y_sb[0:BLK, g * 512:(g + 1) * 512].bitcast(F32),
                                                 ALU.mult, ALU.subtract)
                ins.then_inc(y_ready, 1)

            select(slice(0, 1))

            def swiglu(gu, gate, sig, up, prod, want, h_out):
                dve.wait_ge(gu, want)
                v.tensor_scalar(g_sb, ps_gu[:, 0, :], LIMIT, None, ALU.min).then_inc(gate, 1)
                v.tensor_scalar(u_sb, ps_gu[:, 1, :], LIMIT, -LIMIT, ALU.min, ALU.max).then_inc(up, 1)
                dve.wait_ge(gate, want)
                dve.wait_ge(up, want)
                v.scalar_tensor_tensor(u_sb, u_sb, 1.0, g_sb, ALU.add, ALU.mult).then_inc(prod, 1)
                dve.wait_ge(prod, want)
                dve.wait_ge(sig, want)
                v.tensor_tensor(h_sb, u_sb, sig_sb, ALU.mult).then_inc(h_out, 1)

            def accumulate(t, comb, want, done, src=ps_c):
                _, n, _ = tiles[t]
                dve.wait_ge(comb, want)
                acc = out_acc[0:n, t, :].rearrange("p (h n) -> p h n", h=2)
                v.tensor_tensor(acc, acc, src[0:n, :, :], ALU.add).then_inc(done, 1)

            dve.wait_ge(blocks_ready, 1)
            with dve.Fori(0, NE) as e:
                more = dve.value_load(blocks_i[0:1, 0, bass.ds(e, 1)], min_val=0, max_val=LAST_BLK - 1)
                with dve.If(more > 0):
                    base = dve.value_load(blocks_i[0:1, 1, bass.ds(e, 1)], min_val=0, max_val=NE * LAST_BLK)
                    with dve.Fori(0, more) as i:
                        b = base + i
                        slots = iota_slot[:, bass.ds((i + 1) * BLK, BLK)]
                        one_hot(x_pick, place[:, :, bass.ds(e, 1)], slots).then_inc(x_pick_ready, 1)
                        swiglu(x_gu_done, x_gate_ready, x_sig_ready, x_up_ready, x_prod_ready, b + 1, x_h_ready)
                        for t in range(NT):
                            accumulate(t, x_comb_done[t], b + 1, x_acc_done[t])
                dve.wait_ge(giveT_done, e + 1)
                one_hot(pick, place[:, :, bass.ds(e + 1, 1)], first_slots).then_inc(pick_ready, 1)
                swiglu(slot_free[3], gate_ready, sig_ready, up_ready, prod_ready, e + 1, h_ready)
                accumulate(0, comb_done[0], e + 1, acc_done[0])
                accumulate(1, comb_done[1], e + 1, acc_done[1])
                dve.wait_ge(slot_free[4], e + 1)
                select(bass.ds(e + 1, 1))
                accumulate(2, comb_done[2], e + 1, acc_done[2])
                gated_low(e)
            for t, (_, n, _) in enumerate(tiles):
                accumulate(t, comb_done[t], NE + 1, acc_done[t], src=(ps_c, ps[:, 0:2, :], ps[:, 2:4, :])[t])
            dve.wait_ge(ln_in[2], 32)
            for t, (_, n, _) in enumerate(tiles):
                dve.wait_ge(acc_done[t], NE + 1)
                layer_norm(t, n, out_acc[0:n, t, :], 2 * NT)


_INS = ['x_prompt', 'x_sample', 'cache_k', 'cache_v', 'cache_kidx', 'state_pool', 'ln0_g', 'ln0_b', 'w_in', 'w_o',
        'pool_w', 'pool_scale', 'ln1_g', 'ln1_b', 'w_router', 'b_router', 'w1', 'b1', 'w2', 'b2', 'ln2_g', 'ln2_b']
_OUTS = [(1, 256, 1024), (1, 32, 1024), (1, 1, 256, 64), (1, 1, 256, 64), (1, 1, 256, 64), (1, 1, 15, 512),
         (1, 1, 32, 64), (1, 1, 32, 64), (1, 1, 32, 64), (1, 1, 15, 512)]


def kernel(**inputs):
    import numpy as _np
    import concourse.bacc as _bacc
    from concourse import mybir as _mybir
    from concourse.bass_utils import run_bass_kernel_spmd as _run

    nc = _bacc.Bacc("TRN2", target_bir_lowering=False, num_devices=1)
    arrays, ins, outs = {}, [], []
    for name in _INS:
        a = _np.ascontiguousarray(inputs[name])
        arrays[f"in_{name}_dram"] = a
        ins.append(nc.dram_tensor(f"in_{name}_dram", a.shape, _mybir.dt.from_np(a.dtype), kind="ExternalInput").ap())
    for i, shape in enumerate(_OUTS):
        outs.append(nc.dram_tensor(f"out_{i}_dram", shape, _mybir.dt.float32, kind="ExternalOutput").ap())
    encoder_kernel(nc, ins, outs)
    r = _run(nc, [arrays], core_ids=[0])
    return tuple(r.results[0][f"out_{i}_dram"] for i in range(len(_OUTS)))
```

```python
from contextlib import ExitStack

import concourse.bass as bass
from concourse import mybir

F32 = mybir.dt.float32
F32R = mybir.dt.float32r
BF16 = mybir.dt.bfloat16
I32 = mybir.dt.int32
ALU = mybir.AluOpType
ACT = mybir.ActivationFunctionType
AX = mybir.AxisListType.X

P = 128
CHUNK = 64
HEAD_DIM = 64
N_HEADS = 8
POOL_PAST = 15
WINDOWS = (2, 4, 8, 16)
TOP_K = 4
LIMIT = 7.0
SWIGLU_ALPHA = 1.702
LN_EPS = 1e-5
RESIDUAL = 2.0 ** 0.25
HIDDEN_KEY = -1.0e30
TAKEN = -3.0e38
BLK = 64


def encoder_kernel(nc, ins, outs):
    (x_prompt, x_sample, cache_k, cache_v, cache_kidx, state_pool, ln0_g, ln0_b, w_in, w_o, pool_w,
     pool_scale, ln1_g, ln1_b, w_router, b_router, w1, b1, w2, b2, ln2_g, ln2_b) = ins
    (y_prompt, y_sample, k_prompt, v_prompt, kidx_prompt, pool_prompt,
     k_sample, v_sample, kidx_sample, pool_sample) = outs

    S, D = x_prompt.shape[1:]
    TS = x_sample.shape[1]
    PAST = cache_k.shape[2]
    NE = w_router.shape[2]
    F = w2.shape[2]
    IN = w_in.shape[2]
    KT = D // P
    TOK = S + TS
    NT = 3
    TOKP = NT * P
    tiles = [(0, P, P), (P, P, 2 * P), (S, TS, PAST + TS)]
    topk = [min(256, S // 4)] * 2 + [min(256, (PAST + TS) // 4)]
    assert (S, TS, D, F, PAST, KT) == (2 * P, 32, 1024, 1024, 2 * P, 8)
    K_OFF = N_HEADS * HEAD_DIM
    QI_OFF = K_OFF + 2 * HEAD_DIM
    KI_OFF = QI_OFF + N_HEADS * HEAD_DIM
    U_OFF = KI_OFF + HEAD_DIM + N_HEADS
    KW = HEAD_DIM + N_HEADS
    LAST_BLK = -(-TOK // BLK)
    SLOT = 2 * 2 * F
    NSLOT = 6
    UW = POOL_PAST + S + POOL_PAST + TS
    U_S = POOL_PAST + S

    with ExitStack() as ctx:
        def sb(name, shape, dt=F32):
            return ctx.enter_context(nc.sbuf_tensor(name, shape, dt))

        def sem(name):
            return ctx.enter_context(nc.semaphore(name))

        ring = sb("ring", [P, NSLOT, SLOT])
        area = sb("area", [P, KT * IN])
        rows = sb("rows", [P, NT, D])
        tokT = sb("tokT", [P, KT, TOK])
        lnb = sb("lnb", [P, 2, D])
        uext = sb("uext", [P, 4, UW])
        kv_rows = sb("kv_rows", [P, NT, P + KW])
        score = sb("score", [P, NT, 288])
        w_router_sb = sb("w_router_sb", [P, KT, NE])
        b_router_sb = sb("b_router_sb", [P, NE])
        pool_scale_sb = sb("pool_scale_sb", [P, 4])
        giveT = sb("giveT", [P, TOKP], F32R)
        y_sb = sb("y_sb", [P, D], F32R)
        ident = sb("ident", [P, P])
        iota_slot = sb("iota_slot", [P, LAST_BLK * BLK])
        before = sb("before", [P, P], BF16)
        ones_b = sb("ones_b", [P, P], BF16)
        same_exp = sb("same_exp", [3 * NE, NE + 1])
        sel = sb("sel", [3 * NE, BLK], BF16)
        gcol = sb("gcol", [P, 1])
        x_gcol = sb("x_gcol", [P, 1])
        ln0T = sb("ln0T", [P, 2, KT])
        shift = sb("shift", [P, NT])
        stats = sb("stats", [P, NT, 2, 6])
        moments = sb("moments", [P, NT, 2])
        veps = sb("veps", [P, NT])
        std = sb("std", [P, NT])
        rstd = sb("rstd", [P, NT])
        w_idx = sb("w_idx", [P, NT, N_HEADS])
        max8 = sb("max8", [P, NT, 8])
        row_max = sb("row_max", [P, NT, N_HEADS])
        neg_max = sb("neg_max", [P, NT, N_HEADS])
        row_sum = sb("row_sum", [P, NT, N_HEADS])
        row_inv = sb("row_inv", [P, NT, N_HEADS])
        logits = sb("logits", [P, NT, NE])
        top8 = sb("top8", [P, NT, 8])
        top_s = sb("top_s", [P, NT])
        top_r = sb("top_r", [P, NT])
        flat = score[:, :, :].rearrange("p t n -> p (t n)")
        shifted, kept, expo, weighed = (flat[:, i * NT * NE:(i + 1) * NT * NE].rearrange("p (t e) -> p t e", t=NT)
                                        for i in range(4))
        chosen = sb("chosen", [P, NT, NE])
        chosen_b = sb("chosen_b", [P, NT, NE], BF16)
        gate_w = sb("gate_w", [P, NT, NE + 1])
        place = sb("place", [P, NT, NE + 1])
        blocks_f = sb("blocks_f", [1, 3, NE])
        blocks_i = sb("blocks_i", [1, 2, NE], I32)

        w_o_sb = area[:, 0:KT * D].rearrange("p (k n) -> p k n", k=KT)
        out_acc = area[:, KT * D:KT * D + NT * D].rearrange("p (t n) -> p t n", t=NT)
        sums_a = area[:, KT * D:KT * D + 4 * UW].rearrange("p (g n) -> p g n", g=4)
        sums_b = area[:, KT * D + 4 * UW:KT * D + 8 * UW].rearrange("p (g n) -> p g n", g=4)
        BP = KT * D + NT * D
        bias_parts = area[0:3 * NE, BP:BP + 3 * F // 2].bitcast(BF16)
        last_u = area[0:POOL_PAST, BP + 3 * F // 2:BP + 3 * F // 2 + D].rearrange("p (s c) -> p s c", s=2)
        assert BP + 3 * F // 2 + D <= KT * IN

        used = [0]

        def carve(base, n):
            at = used[0]
            used[0] += n
            return base[:, at:at + n]

        spare = ring[:, 2:6, :].rearrange("p s n -> p (s n)")
        qiT = carve(spare, 4 * TOK).rearrange("p (i t) -> p i t", i=4)
        kiT2 = carve(spare, S + PAST + TS)
        kvT = carve(spare, TOK)
        kwT = carve(spare, TOK)
        relu_sb = carve(spare, 4 * 288).rearrange("p (b h n) -> p b h n", b=2, h=2)
        cache_rows = carve(spare, 2 * P).rearrange("p (c d) -> p c d", c=2)
        assert used[0] <= SLOT
        used[0] = SLOT
        bias_f = carve(spare, 3 * F)[0:3 * NE, :]
        state_rows = carve(spare, 4 * P)[0:POOL_PAST, :]
        pool_w_sb = carve(spare, 4 * P).rearrange("p (g c) -> p g c", g=4)
        assert used[0] == 2 * SLOT
        qT = carve(spare, 4 * TOK).rearrange("p (i t) -> p i t", i=4)
        kT2 = carve(spare, S + PAST + TS)
        probsT = carve(spare, 2 * 8 * P)
        bias_round = probsT.bitcast(BF16)[0:2 * NE, 0:3 * F]
        att_rows = carve(spare, N_HEADS * HEAD_DIM)
        cache_vr = carve(spare, 2 * HEAD_DIM).rearrange("p (c d) -> p c d", c=2)
        diffT = carve(spare, 4 * TOK).rearrange("p (g t) -> p g t", g=4)
        rcount = carve(spare, 4 * 16).rearrange("p (g n) -> p g n", g=4)
        probs = carve(spare, 8 * 288)
        assert used[0] <= 4 * SLOT

        used[0] = 0
        xT = carve(area, KT * BLK).rearrange("p (k s) -> p k s", k=KT)
        pick = carve(area, NT * 2 * BLK).rearrange("p (t h s) -> p t h s", t=NT, h=2)
        g_sb = carve(area, F // 2)
        u_sb = carve(area, F // 2)
        sig_sb = carve(area, F // 2)
        h_sb = carve(area, F // 2)
        hT = carve(area, 4 * P).rearrange("p (c h s) -> p c h s", c=4, h=2)
        early_w1 = carve(area, SLOT)
        assert used[0] <= KT * D
        used[0] = 0
        tok_flat = tokT[:, :, :].rearrange("p k t -> p (k t)")
        x_xT = carve(tok_flat, KT * BLK).rearrange("p (k s) -> p k s", k=KT)
        x_pick = carve(tok_flat, NT * 2 * BLK).rearrange("p (t h s) -> p t h s", t=NT, h=2)
        x_giveT = carve(tok_flat, TOKP)
        x_y = carve(tok_flat, D // 2)
        assert used[0] <= KT * TOK

        ps = ctx.enter_context(nc.psum_tensor("ps", [P, 8, 512], F32))
        ps_gu = ps[:, 0:2, :]
        ps_x = ps[:, 2, :].rearrange("p (k s) -> p k s", k=KT)
        ps_hT = ps[:, 3, :]
        ps_y = ps[:, 4, :]
        ps_c = ps[:, 5:7, :]
        ps_g = ps[:, 7, 0:TOKP + 1]
        x_ps_g = ps[:, 3, 0:TOKP + 1]

        zero_rows = sem("zero_rows")
        ident0 = sem("ident0")
        before0 = sem("before0")
        same0 = sem("same0")
        ident_ready = sem("ident_ready")
        const_ready = sem("const_ready")
        pool_step = sem("pool_step")
        x_in = [sem(f"x_in{t}") for t in range(NT)]
        ln0T_in = sem("ln0T_in")
        norm_ready = sem("norm_ready")
        normed = sem("normed")
        gained = sem("gained")
        gained_last = sem("gained_last")
        result = [sem(f"result{t}") for t in range(NT)]
        tokT_sb_v = sem("tokT_sb_v")
        ln_in = [sem(f"ln_in{i}") for i in range(3)]
        w_in_in = [sem(f"w_in_in{i}") for i in range(3)]
        cache_in = sem("cache_in")
        small_in = sem("small_in")
        state_in = sem("state_in")
        w_o_in = sem("w_o_in")
        w_in_slot = [sem(f"w_slot{s}") for s in range(NSLOT)]
        bias_in = sem("bias_in")
        early_in = sem("early_in")
        bias_left = sem("bias_left")
        bias_ready = sem("bias_ready")
        rows_out = sem("rows_out")
        final_out = sem("final_out")
        dve_step = sem("dve_step")
        var_ready = sem("var_ready")
        std_ready = sem("std_ready")
        ln_done = sem("ln_done")
        tokT_ps = sem("tokT_ps")
        tokT_sb = sem("tokT_sb")
        proj_ps = sem("proj_ps")
        proj_sb = sem("proj_sb")
        cacheT_ps = sem("cacheT_ps")
        cacheT_sb = sem("cacheT_sb")
        kvrow_ps = sem("kvrow_ps")
        kvrow_sb = sem("kvrow_sb")
        idx_ps = sem("idx_ps")
        idx_relu = sem("idx_relu")
        idx_used = sem("idx_used")
        pool_diff = sem("pool_diff")
        lastu_ps = sem("lastu_ps")
        lastu_sb = sem("lastu_sb")
        stateT_ps = sem("stateT_ps")
        stateT_sb = sem("stateT_sb")
        poolmm_ps = sem("poolmm_ps")
        poolT_sb = sem("poolT_sb")
        qk_ps = sem("qk_ps")
        qk_used = sem("qk_used")
        max_ready = sem("max_ready")
        exp_done = sem("exp_done")
        probsT_ps = sem("probsT_ps")
        probsT_sb = sem("probsT_sb")
        pv_ps = sem("pv_ps")
        att_ready = sem("att_ready")
        attT_ps = sem("attT_ps")
        attT_sb = sem("attT_sb")
        wo_ps = sem("wo_ps")
        h1T_ps = sem("h1T_ps")
        h1T_sb = sem("h1T_sb")
        router_ps = sem("router_ps")
        top_ready = sem("top_ready")
        top_exp = sem("top_exp")
        gates_ready = sem("gates_ready")
        prefix_ps = sem("prefix_ps")
        blocks_ready = sem("blocks_ready")
        acc_init = sem("acc_init")
        slot_free = [sem(f"slot_free{s}") for s in range(NSLOT)]
        sel_ready = sem("sel_ready")
        pick_first = sem("pick_first")
        x_first = sem("x_first")
        x_first_sb = sem("x_first_sb")
        pick_ready = sem("pick_ready")
        x_gathered = sem("x_gathered")
        xT_ready = sem("xT_ready")
        gate_ready = sem("gate_ready")
        sig_ready = sem("sig_ready")
        up_ready = sem("up_ready")
        prod_ready = sem("prod_ready")
        h_ready = sem("h_ready")
        hT_done = sem("hT_done")
        hT_ready = sem("hT_ready")
        y_high = sem("y_high")
        y_ready = sem("y_ready")
        giveT_done = sem("giveT_done")
        giveT_ready = sem("giveT_ready")
        comb_done = [sem(f"comb_done{t}") for t in range(NT)]
        acc_done = [sem(f"acc_done{t}") for t in range(NT)]
        x_pick_ready = sem("x_pick_ready")
        x_x_gathered = sem("x_x_gathered")
        x_xT_ready = sem("x_xT_ready")
        x_gu_done = sem("x_gu_done")
        x_gate_ready = sem("x_gate_ready")
        x_sig_ready = sem("x_sig_ready")
        x_up_ready = sem("x_up_ready")
        x_prod_ready = sem("x_prod_ready")
        x_h_ready = sem("x_h_ready")
        x_hT_done = sem("x_hT_done")
        x_hT_ready = sem("x_hT_ready")
        x_y_done = sem("x_y_done")
        x_y_ready = sem("x_y_ready")
        x_giveT_done = sem("x_giveT_done")
        x_giveT_ready = sem("x_giveT_ready")
        x_comb_done = [sem(f"x_comb_done{t}") for t in range(NT)]
        x_acc_done = [sem(f"x_acc_done{t}") for t in range(NT)]

        def col(e):
            return slice(e, e + 1) if isinstance(e, int) else bass.ds(e, 1)

        w1_v = w1[0].rearrange("e (p k) n -> e p (k n)", k=KT)
        w2_v = w2[0].rearrange("e (h p c) n -> e h p (c n)", h=2, c=4)
        w1_t = ring[:, 0:4, :].rearrange("p s (k n) -> p (s k) n", k=2)
        w2_t = ring[:, 4:6, :].rearrange("p s (c n) -> p s c n", c=4)
        x_views = [x_prompt[0].rearrange("(t p) d -> p t d", p=P), x_sample[0]]
        order = [(KI_OFF, KW)] + [(QI_OFF + P * i, P) for i in range(4)] + [(K_OFF, P)] \
            + [(P * i, P) for i in range(4)] + [(U_OFF + P * i, P) for i in range(4)]
        chunk_of = [0] * 5 + [1] * 5 + [2] * 4
        chunks = [(QI_OFF, U_OFF), (0, QI_OFF), (U_OFF, IN)]
        w_in_sb, at = [], 0
        for a, b in chunks:
            w_in_sb.append(area[:, at:at + KT * (b - a)].rearrange("p (j n) -> p j n", j=KT))
            at += KT * (b - a)
        assert KT * U_OFF >= KT * D

        def proj_bank(i):
            return 4 + (i % 4 if i < 10 else i % 2)

        def qk_bank(h):
            return ps[:, h % 3, :]

        block = ctx.enter_context(nc.Block())

        @block.sync
        def _(sp):
            for t in range(2):
                sp.dma_start(rows[:, t, :], x_views[0][:, t, :]).then_inc(x_in[t], 16)
            sp.wait_ge(zero_rows, 1)
            sp.dma_start(rows[0:TS, 2, :], x_views[1]).then_inc(x_in[2], 16)
            sp.dma_start(ln0T[:, 0, :], ln0_g.rearrange("(p j) -> p j", j=KT)).then_inc(ln0T_in, 16)
            sp.dma_start(ln0T[:, 1, :], ln0_b.rearrange("(p j) -> p j", j=KT)).then_inc(ln0T_in, 16)
            w_in_v = w_in[0].rearrange("(p j) n -> p j n", j=KT)
            for i, (a, b) in enumerate(chunks):
                if i == 1:
                    for part in range(3):
                        r = slice(part * NE, (part + 1) * NE)
                        sp.dma_start(bias_f[r, 0:2 * F], b1[0]).then_inc(bias_in, 16)
                        sp.dma_start(bias_f[r, 2 * F:3 * F], b2[0]).then_inc(bias_in, 16)
                elif i == 2:
                    sp.dma_start(lnb[:, 0, :], ln0_g.partition_broadcast(P)).then_inc(ln_in[0], 16)
                    sp.dma_start(lnb[:, 1, :], ln0_b.partition_broadcast(P)).then_inc(ln_in[0], 16)
                sp.dma_start(w_in_sb[i], w_in_v[:, :, a:b]).then_inc(w_in_in[i], 16)
                if i == 0:
                    sp.dma_start(cache_rows[:, :, 0:HEAD_DIM],
                                 cache_k[0, 0].rearrange("(c p) d -> p c d", p=P)).then_inc(cache_in, 16)
                    sp.dma_start(cache_rows[:, :, HEAD_DIM:P],
                                 cache_kidx[0, 0].rearrange("(c p) d -> p c d", p=P)).then_inc(cache_in, 16)
                    sp.dma_start(cache_vr[:, :, :],
                                 cache_v[0, 0].rearrange("(c p) d -> p c d", p=P)).then_inc(cache_in, 16)
                    sp.dma_start(state_rows[:, :], state_pool[0, 0]).then_inc(state_in, 16)
            sp.dma_start(pool_w_sb[:, :, :], pool_w[0].rearrange("g c d -> c g d")).then_inc(small_in, 16)
            sp.dma_start(pool_scale_sb[:, :], pool_scale[0].rearrange("(g p) -> p g", p=P),
                         allow_slow_non_contiguous=True).then_inc(small_in, 16)
            sp.dma_start(w_router_sb[:, :, :], w_router[0].rearrange("(p j) n -> p j n", j=KT)).then_inc(small_in, 16)
            sp.dma_start(b_router_sb[:, :], b_router[0].partition_broadcast(P)).then_inc(small_in, 16)
            for s in range(2):
                sp.dma_start(ring[:, s, :], w1_v[0, :, s * SLOT:(s + 1) * SLOT]).then_inc(w_in_slot[s], 16)
            sp.wait_ge(ln_done, NT)
            sp.dma_start(lnb[:, 0, :], ln1_g[0].partition_broadcast(P)).then_inc(ln_in[1], 16)
            sp.dma_start(lnb[:, 1, :], ln1_b[0].partition_broadcast(P)).then_inc(ln_in[1], 16)
            sp.wait_ge(kvrow_sb, 2)
            for t in range(2):
                for off, dram in ((0, k_prompt), (HEAD_DIM, v_prompt), (P, kidx_prompt)):
                    sp.dma_start(dram[0, 0, t * P:(t + 1) * P, :],
                                 kv_rows[:, t, off:off + HEAD_DIM]).then_inc(rows_out, 16)
            for off, dram in ((0, k_sample), (HEAD_DIM, v_sample), (P, kidx_sample)):
                sp.dma_start(dram[0, 0], kv_rows[0:TS, 2, off:off + HEAD_DIM]).then_inc(rows_out, 16)
            sp.wait_ge(proj_ps, 10)
            sp.dma_start(w_o_sb, w_o[0].rearrange("(k p) n -> p k n", p=P)).then_inc(w_o_in, 16)
            sp.wait_ge(idx_ps, 4 * NT)
            sp.wait_ge(idx_used, 4 * NT)
            sp.dma_start(ring[:, 2, :], w1_v[0, :, 2 * SLOT:3 * SLOT]).then_inc(w_in_slot[2], 16)
            sp.wait_ge(lastu_sb, 1)
            sp.dma_start(pool_prompt[0, 0], last_u[:, 0, :]).then_inc(rows_out, 16)
            sp.dma_start(pool_sample[0, 0], last_u[:, 1, :]).then_inc(rows_out, 16)
            sp.wait_ge(bias_ready, 1)
            sp.wait_ge(stateT_ps, 1)
            sp.wait_ge(poolmm_ps, 4)
            sp.dma_start(ring[:, 3, :], w1_v[0, :, 3 * SLOT:4 * SLOT]).then_inc(w_in_slot[3], 16)
            sp.wait_ge(attT_ps, NT)
            sp.wait_ge(att_ready, NT)
            sp.wait_ge(rows_out, 16 * 11)
            for h in range(2):
                sp.dma_start(ring[:, 4 + h, :], w2_v[0, h]).then_inc(w_in_slot[4 + h], 16)
            sp.wait_ge(wo_ps, NT)
            sp.dma_start(early_w1, w1_v[1, :, 0:SLOT]).then_inc(early_in, 16)
            sp.wait_ge(ln_done, 2 * NT)
            sp.dma_start(lnb[:, 0, :], ln2_g[0].partition_broadcast(P)).then_inc(ln_in[2], 16)
            sp.dma_start(lnb[:, 1, :], ln2_b[0].partition_broadcast(P)).then_inc(ln_in[2], 16)

            def load(e, s):
                src = w1_v[col(e), :, s * SLOT:(s + 1) * SLOT] if s < 4 else w2_v[col(e), s - 4]
                sp.wait_ge(slot_free[s], 1 if s == 0 and isinstance(e, int) else e)
                sp.dma_start(ring[:, s, :], src.rearrange("e p n -> p (e n)")).then_inc(w_in_slot[s], 16)

            load(2, 0)
            for s in range(1, NSLOT):
                load(1, s)
            for s in range(1, NSLOT):
                load(2, s)
            with sp.Fori(3, NE) as e:
                for s in range(NSLOT):
                    load(e, s)

        @block.gpsimd
        def _(pool):
            nc.gpsimd.memset(rows[:, 2, :], 0.0).then_inc(zero_rows, 1)
            nc.gpsimd.memset(ident[:, :], 0.0).then_inc(ident0, 1)
            pool.wait_ge(ident0, 1)
            nc.gpsimd.affine_select(out=ident[:, :], in_=ident[:, :], compare_op=ALU.not_equal, fill=1.0, base=0,
                                    pattern=[[-1, P]], channel_multiplier=1).then_inc(ident_ready, 1)
            nc.gpsimd.memset(before[:, :], 0.0).then_inc(before0, 1)
            pool.wait_ge(before0, 1)
            nc.gpsimd.affine_select(out=before[:, :], in_=before[:, :], compare_op=ALU.is_ge, fill=1.0, base=0,
                                    pattern=[[-1, P]], channel_multiplier=1).then_inc(const_ready, 1)
            nc.gpsimd.memset(ones_b[:, :], 1.0).then_inc(const_ready, 1)
            pool.wait_ge(ident_ready, 1)
            nc.gpsimd.memset(same_exp[:, NE:NE + 1], 0.0)
            nc.gpsimd.tensor_tensor(same_exp[:, 0:NE], ident[0:3 * NE, 0:NE], ident[0:3 * NE, NE:2 * NE],
                                    ALU.add).then_inc(same0, 1)
            pool.wait_ge(same0, 1)
            nc.gpsimd.tensor_tensor(same_exp[:, 0:NE], same_exp[:, 0:NE], ident[0:3 * NE, 2 * NE:3 * NE],
                                    ALU.add).then_inc(const_ready, 1)
            nc.gpsimd.memset(logits[:, :, :], 0.0).then_inc(const_ready, 1)
            nc.gpsimd.iota(iota_slot[:, :], [[1, LAST_BLK * BLK]], base=0, channel_multiplier=0,
                           allow_small_or_imprecise_dtypes=True).then_inc(const_ready, 1)
            nc.gpsimd.iota(rcount[:, :, :], [[0, 4], [1, 16]], base=1, channel_multiplier=0,
                           allow_small_or_imprecise_dtypes=True).then_inc(const_ready, 1)
            nc.gpsimd.memset(uext[:, :, 0:POOL_PAST], 0.0).then_inc(const_ready, 1)
            pool.wait_ge(proj_sb, len(order))
            pool.wait_ge(stateT_sb, 1)
            pool.wait_ge(proj_ps, len(order))
            src, dst, step = uext, sums_a, 0
            for level in range(4):
                back = 1 << level
                a = 2 * back - 1
                nc.gpsimd.tensor_tensor(dst[:, level:4, a:UW], src[:, level:4, a:UW],
                                        src[:, level:4, a - back:UW - back], ALU.add).then_inc(pool_step, 1)
                step += 1
                pool.wait_ge(pool_step, step)
                src, dst = dst, (sums_b if dst is sums_a else sums_a)

            pool.wait_ge(bias_left, 1)
            pool.wait_ge(proj_ps, len(order))
            nc.gpsimd.tensor_copy(bias_parts, bias_f).then_inc(bias_ready, 1)

            pool.wait_ge(ln_in[2], 32)
            for t in range(2):
                pool.wait_ge(gained, t + 1)
                nc.gpsimd.tensor_tensor(out_acc[:, t, :], out_acc[:, t, :], lnb[:, 1, :],
                                        ALU.add).then_inc(result[t], 1)

        @block.tensor
        def _(pe):
            mm = nc.tensor.matmul
            tr = nc.tensor.transpose

            def rows_to_tokT(ready):
                for t, (t0, n, _) in enumerate(tiles):
                    if t >= 1:
                        keep_warm(3)
                    pe.wait_ge(normed, t + 1)
                    for j in range(KT):
                        last = tr(ps[:, t * 2 + j // 4 if t < 2 else 4, (j % 4) * P:(j % 4) * P + n] if t < 2 else
                                  ps[:, 4, j * TS:(j + 1) * TS],
                                  rows[0:n, t, j:D:KT], ident[0:n, 0:n])
                        if t < 2 and j % 4 == 3:
                            last.then_inc(ready, 1)
                    if t == 2:
                        last.then_inc(ready, 1)

            def keep_warm(n, bank=7):
                for _ in range(n):
                    mm(ps[:, bank, 0:P], ident[:, :], ident[:, :], start=True, stop=True)

            pe.wait_ge(ident_ready, 1)
            keep_warm(12)
            rows_to_tokT(tokT_ps)

            def project(i):
                c0, w = order[i]
                chunk = chunk_of[i]
                c0 -= chunks[chunk][0]
                pe.wait_ge(w_in_in[chunk], 16)
                if i == 0:
                    pe.wait_ge(tokT_sb_v, 4)
                    pe.wait_ge(tokT_sb, 1)
                if i >= 4:
                    pe.wait_ge(proj_sb, max(k for k in range(i) if proj_bank(k) == proj_bank(i)) + 1)
                for j in range(KT):
                    last = mm(ps[0:w, proj_bank(i), 0:TOK], w_in_sb[chunk][:, j, c0:c0 + w], tokT[:, j, :],
                              start=(j == 0), stop=(j == KT - 1))
                last.then_inc(proj_ps, 1)

            keep_warm(12)
            for i in range(6):
                project(i)
            pe.wait_ge(cache_in, 48)
            for c in range(2):
                last = tr(ps[:, 0, c * P:(c + 1) * P], cache_rows[:, c, :], ident[:, :])
            last.then_inc(cacheT_ps, 1)
            keep_warm(3, bank=3)
            pe.wait_ge(proj_sb, 6)
            for t, (t0, n, _) in enumerate(tiles):
                bank, at = (1, t * (P + KW)) if t < 2 else (2, 0)
                tr(ps[0:n, bank, at:at + P], kvT[:, t0:t0 + n], ident[:, :])
                last = tr(ps[0:n, bank, at + P:at + P + KW], kwT[0:KW, t0:t0 + n], ident[0:KW, 0:KW])
                if t >= 1:
                    last.then_inc(kvrow_ps, 1)
            keep_warm(5, bank=3)
            pe.wait_ge(cacheT_sb, 1)
            pe.wait_ge(kvrow_sb, 2)

            def index_logits(t):
                t0, n, nk = tiles[t]
                k0 = 0 if t < 2 else S
                for pair in range(4):
                    n_pair = 4 * t + pair
                    if n_pair >= 2:
                        pe.wait_ge(idx_relu, n_pair - 1)
                    for half in range(2):
                        r = slice(half * HEAD_DIM, (half + 1) * HEAD_DIM)
                        last = mm(ps[0:n, 2 * (n_pair % 2) + half, 0:nk], qiT[r, pair, t0:t0 + n],
                                  kiT2[r, k0:k0 + nk], start=True, stop=True)
                    last.then_inc(idx_ps, 1)

            index_logits(0)
            project(6)
            project(7)
            index_logits(1)
            project(8)
            project(9)
            index_logits(2)

            pe.wait_ge(proj_sb, 8)
            keep_warm(6)
            pe.wait_ge(proj_sb, 10)
            pe.wait_ge(idx_relu, 12)

            def logits_of(t):
                t0, n, nk = tiles[t]
                k0 = 0 if t < 2 else S
                for h in range(N_HEADS):
                    done = N_HEADS * t + h
                    if h >= 3:
                        pe.wait_ge(qk_used, done - 2)
                    elif h == 0 and t >= 1:
                        pe.wait_ge(qk_used, done)
                    r = slice(h % 2 * HEAD_DIM, (h % 2 + 1) * HEAD_DIM)
                    mm(qk_bank(h)[0:n, 0:nk], qT[r, h // 2, t0:t0 + n], kT2[r, k0:k0 + nk],
                       start=True, stop=True).then_inc(qk_ps, 1)

            pe_groups = [0]

            def attend(t):
                t0, n, nk = tiles[t]
                nl = -(-nk // P)
                pe.wait_ge(exp_done, t + 1)
                for c in range(nl):
                    lw = min(P, nk - c * P)
                    for hg in range(2):
                        g = pe_groups[0]
                        if g >= 2:
                            pe.wait_ge(probsT_sb, g - 1)
                        for q in range(4):
                            h = 4 * hg + q
                            last = tr(ps[0:lw, 6 + g % 2, q * n:(q + 1) * n],
                                      probs[0:n, h * nk + c * P:h * nk + c * P + lw], ident[0:n, 0:n])
                        last.then_inc(probsT_ps, 1)
                        pe_groups[0] += 1
                keep_warm(3, bank=2)
                pe.wait_ge(probsT_sb, pe_groups[0])
                if t >= 1:
                    pe.wait_ge(attT_sb, t)
                for h in range(N_HEADS):
                    for c in range(nl):
                        lw = min(P, nk - c * P)
                        if t < 2:
                            v = kv_rows[0:lw, c, HEAD_DIM:P]
                        else:
                            v = cache_vr[0:lw, c, :] if c < 2 else kv_rows[0:lw, 2, HEAD_DIM:P]
                        at = (c * N_HEADS + h) * n
                        last = mm(ps[0:n, 3, h * HEAD_DIM:(h + 1) * HEAD_DIM], probsT[0:lw, at:at + n], v,
                                  start=(c == 0), stop=(c == nl - 1))
                last.then_inc(pv_ps, 1)

            def turn_att(t):
                t0, n, _ = tiles[t]
                pe.wait_ge(att_ready, t + 1)
                for k in range(4):
                    last = tr(ps[:, 3, k * n:(k + 1) * n], att_rows[0:n, k * P:(k + 1) * P], ident[0:n, 0:n])
                last.then_inc(attT_ps, 1)

            def mix(t, ks, start, stop):
                t0, n, _ = tiles[t]
                for k in ks:
                    for half in range(2):
                        dst = ps[0:n, 4 * t + half, :] if t < 2 else ps[half * TS:(half + 1) * TS, 2, :]
                        last = mm(dst, tokT[:, k, t0:t0 + n], w_o_sb[:, k, half * 512:(half + 1) * 512],
                                  start=(start and k == ks[0]), stop=(stop and k == ks[-1]))
                if stop:
                    last.then_inc(wo_ps, 1)

            logits_of(0)
            project(10)
            project(11)
            attend(0)
            logits_of(1)
            project(12)
            project(13)
            pe.wait_ge(state_in, 16)
            pe.wait_ge(proj_sb, 13)
            for g in range(4):
                last = tr(ps[:, 4, g * POOL_PAST:(g + 1) * POOL_PAST], state_rows[:, g * P:(g + 1) * P],
                          ident[0:POOL_PAST, 0:POOL_PAST])
            last.then_inc(stateT_ps, 1)
            turn_att(0)
            attend(1)
            logits_of(2)
            turn_att(1)
            pe.wait_ge(proj_sb, len(order))
            pe.wait_ge(stateT_sb, 1)
            for part, at in ((0, U_S - POOL_PAST), (1, UW - POOL_PAST)):
                for g in range(4):
                    last = tr(ps[0:POOL_PAST, 4 + part, g * P:(g + 1) * P], uext[:, g, at:at + POOL_PAST],
                              ident[:, :])
            last.then_inc(lastu_ps, 1)
            att_ks, pool_ks = (0, 1, 2, 3), (4, 5, 6, 7)
            pe.wait_ge(w_o_in, 16)
            pe.wait_ge(attT_sb, 1)
            pe.wait_ge(qk_used, NT * N_HEADS)
            mix(0, att_ks, True, False)
            pe.wait_ge(small_in, 64)
            pe.wait_ge(pool_diff, 1)
            pe.wait_ge(lastu_sb, 1)
            for g in range(4):
                if g >= 2:
                    pe.wait_ge(poolT_sb, g - 1)
                mm(ps[:, 4 + g % 2, 0:TOK], pool_w_sb[:, g, :], diffT[:, g, :],
                   start=True, stop=True).then_inc(poolmm_ps, 1)
            pe.wait_ge(poolT_sb, 4)
            mix(0, pool_ks, False, True)
            attend(2)
            mix(1, pool_ks, True, False)
            mix(1, att_ks, False, True)
            turn_att(2)

            def rows_to_ps(t, banks):
                _, n, _ = tiles[t]
                pe.wait_ge(ln_done, NT + t + 1)
                for j in range(KT):
                    dst = ps[:, banks[j // 4], (j % 4) * P:(j % 4) * P + n] if t < 2 \
                        else ps[:, banks[0], j * n:(j + 1) * n]
                    last = tr(dst, rows[0:n, t, j:D:KT], ident[0:n, 0:n])
                    if t < 2 and j % 4 == 3:
                        last.then_inc(h1T_ps, 1)
                if t == 2:
                    last.then_inc(h1T_ps, 1)

            def route(t, copies):
                t0, n, _ = tiles[t]
                pe.wait_ge(h1T_sb, copies)
                for j in range(KT):
                    last = mm(ps[0:n, t // 2, t * NE:(t + 1) * NE], tokT[:, j, t0:t0 + n], w_router_sb[:, j, :],
                              start=(j == 0), stop=(j == KT - 1))
                return last

            rows_to_ps(0, (6, 7))
            mix(2, pool_ks, True, False)
            pe.wait_ge(attT_sb, 3)
            mix(2, att_ks, False, True)
            route(0, 2)
            rows_to_ps(1, (4, 5))
            keep_warm(4)
            route(1, 4).then_inc(router_ps, 1)
            keep_warm(4)
            rows_to_ps(2, (3,))
            keep_warm(4)
            pe.wait_ge(const_ready, 7)
            pe.wait_ge(gates_ready, 1)
            for t in range(2):
                for u in range(t + 1):
                    last = mm(ps[:, 4, t * NE:(t + 1) * NE], ones_b[:, :] if u < t else before[:, :],
                              chosen_b[:, u, :], start=(u == 0), stop=(u == t))
            last.then_inc(prefix_ps, 1)
            route(2, 5).then_inc(router_ps, 1)
            keep_warm(3)
            pe.wait_ge(pick_first, 1)
            for k in range(KT):
                for t in range(2):
                    last = mm(ps_x[:, k, :], rows[:, t, k:D:KT], pick[:, t, 0, :], start=(t == 0), stop=(t == 1))
                if k == 3:
                    pe.wait_ge(gates_ready, 2)
                    for u in range(NT):
                        mm(ps[:, 5, 0:NE], before[:, :] if u == 2 else ones_b[:, :], chosen_b[:, u, :],
                           start=(u == 0), stop=(u == 2))
                    for u in range(NT):
                        total = mm(ps[:, 5, NE:2 * NE], ones_b[:, :], chosen_b[:, u, :],
                                   start=(u == 0), stop=(u == 2))
                    total.then_inc(prefix_ps, 1)
            last.then_inc(x_first, 1)
            keep_warm(2)
            pe.wait_ge(pick_ready, 1)
            for k in range(KT):
                last = mm(ps[:, 3, k * BLK:(k + 1) * BLK], rows[:, 2, k:D:KT], pick[:, 2, 0, :],
                          start=True, stop=True)
            last.then_inc(x_gathered, 1)

            def gather(one, ready, want, done):
                pe.wait_ge(ready, want)
                for k in range(KT):
                    for t in range(NT):
                        last = mm(ps_x[:, k, :], rows[:, t, k:D:KT], one[:, t, 0, :],
                                  start=(t == 0), stop=(t == NT - 1))
                last.then_inc(done, 1)

            def up_products(x, e, free):
                for c in range(2):
                    for g in range(2):
                        a = c * F + g * 512
                        mm(ps_gu[g * BLK:(g + 1) * BLK, c, :], sel[:, :], bias_parts[:, a:a + 512],
                           start=True, stop=False)
                for k in range(KT):
                    second = isinstance(e, int) and e == 1 and k < 2
                    if k == 0 and second:
                        pe.wait_ge(early_in, 16)
                    elif k == 0 and not (isinstance(e, int) and e == 0):
                        pe.wait_ge(w_in_slot[0], 16 * e)
                    elif k % 2 == 0:
                        if free and isinstance(e, int) and e == NE - 1:
                            keep_warm(7, bank=2)
                        pe.wait_ge(w_in_slot[k // 2], 16 * (e + 1))
                    w = early_w1[:, k * 2 * F:(k + 1) * 2 * F] if second else w1_t[:, k]
                    for c in range(2):
                        for g in range(2):
                            a = c * F + g * 512
                            last = mm(ps_gu[g * BLK:(g + 1) * BLK, c, :], x[:, k, :], w[:, a:a + 512],
                                      start=False, stop=(k == KT - 1))
                    if free and k % 2 == 1 and k < KT - 1:
                        last.then_inc(slot_free[k // 2], 1)
                return last

            def turn_h():
                for c in range(4):
                    last = tr(ps_hT[:, c * P:(c + 1) * P], h_sb[:, c:512:4], ident[:, :])
                return last

            def down_products(e, h, free):
                if h == 0:
                    for g in range(2):
                        a = 2 * F + g * 512
                        mm(ps_y[g * BLK:(g + 1) * BLK, :], sel[:, :], bias_parts[:, a:a + 512],
                           start=True, stop=False)
                pe.wait_ge(w_in_slot[4 + h], 16 * (e + 1))
                for c in range(4):
                    for g in range(2):
                        last = mm(ps_y[g * BLK:(g + 1) * BLK, :], hT[:, c, h, :],
                                  w2_t[:, h, c, g * 512:(g + 1) * 512],
                                  start=False, stop=(h == 1 and c == 3))
                if free:
                    last.then_inc(slot_free[4 + h], 1)
                return last

            def turn_pick(src, dst, gates_of, done):
                for t in range(NT):
                    tr(dst[:, t * P:(t + 1) * P], src[:, t].rearrange("p h s -> p (h s)"), ident[:, :])
                for t in range(NT):
                    last = mm(dst[:, TOKP:TOKP + 1], src[:, t].rearrange("p h s -> p (h s)"),
                              gate_w[:, t, gates_of], start=(t == 0), stop=(t == NT - 1))
                last.then_inc(done, 1)

            def combine(t, done, dst=ps_c):
                for g in range(2):
                    last = mm(dst[:, g, :], giveT[:, t * P:(t + 1) * P], y_sb[:, g * 512:(g + 1) * 512],
                              start=True, stop=True)
                last.then_inc(done, 1)

            def x_combine(t, done):
                for g in range(2):
                    r = slice(g * BLK, (g + 1) * BLK)
                    last = mm(ps_c[:, g, :], x_giveT[r, t * P:(t + 1) * P], x_y[r, :], start=True, stop=True)
                last.then_inc(done, 1)

            pe.wait_ge(bias_ready, 1)
            pe.wait_ge(blocks_ready, 1)
            def expert(e, last=False):
                more = pe.value_load(blocks_i[0:1, 0, col(e)], min_val=0, max_val=LAST_BLK - 1)
                with pe.If(more > 0):
                    base = pe.value_load(blocks_i[0:1, 1, col(e)], min_val=0, max_val=NE * LAST_BLK)
                    with pe.Fori(0, more) as i:
                        b = base + i
                        pe.wait_ge(xT_ready, e + 1)
                        pe.wait_ge(y_ready, e + 1)
                        gather(x_pick, x_pick_ready, b + 1, x_x_gathered)
                        turn_pick(x_pick, x_ps_g, col(e), x_giveT_done)
                        pe.wait_ge(x_xT_ready, b + 1)
                        pe.wait_ge(sel_ready, e + 1)
                        up_products(x_xT, e, False).then_inc(x_gu_done, 1)
                        pe.wait_ge(x_giveT_ready, b + 1)
                        pe.wait_ge(x_h_ready, b + 1)
                        turn_h().then_inc(x_hT_done, 1)
                        pe.wait_ge(x_hT_ready, b + 1)
                        down_products(e, 0, False)
                        down_products(e, 1, False).then_inc(x_y_done, 1)
                        pe.wait_ge(x_y_ready, b + 1)
                        for t in range(NT):
                            x_combine(t, x_comb_done[t])
                            pe.wait_ge(x_acc_done[t], b + 1)
                pe.wait_ge(xT_ready, e + 1)
                pe.wait_ge(sel_ready, e + 1)
                up_products(xT, e, True).then_inc(slot_free[3], 1)
                if isinstance(e, int) and e == 0:
                    pe.wait_ge(gates_ready, 3)
                    turn_pick(pick, ps_g, slice(0, 1), giveT_done)
                pe.wait_ge(y_ready, e + 1)
                pe.wait_ge(giveT_ready, e + 1)
                combine(0, comb_done[0])
                if not last:
                    gather(pick, pick_ready, e + 2, x_gathered)
                else:
                    keep_warm(10, bank=2)
                pe.wait_ge(h_ready, e + 1)
                turn_h().then_inc(hT_done, 1)
                pe.wait_ge(acc_done[0], e + 1)
                combine(1, comb_done[1])
                pe.wait_ge(hT_ready, e + 1)
                down_products(e, 0, True)
                pe.wait_ge(acc_done[1], e + 1)
                combine(2, comb_done[2])
                down_products(e, 1, True)
                if not last:
                    pe.wait_ge(giveT_ready, e + 2)
                    turn_pick(pick, ps_g, col(e + 1), giveT_done)

            expert(0)
            expert(1)
            with pe.Fori(2, NE - 1) as e:
                expert(e)
            expert(NE - 1, last=True)
            pe.wait_ge(y_ready, NE + 1)
            pe.wait_ge(giveT_ready, NE + 1)
            for t in range(NT):
                combine(t, comb_done[t], dst=(ps_c, ps[:, 0:2, :], ps[:, 2:4, :])[t])

        @block.scalar
        def _(act):
            copy = nc.scalar.copy

            def sqrt_of(base, ts=range(NT)):
                for t in ts:
                    n = tiles[t][1]
                    act.wait_ge(var_ready, base + t + 1)
                    nc.scalar.activation(std[0:n, t:t + 1], veps[0:n, t:t + 1], ACT.Sqrt).then_inc(std_ready, 1)

            def tokT_copies(src, done, banks, parts=range(5)):
                for i in parts:
                    act.wait_ge(src, i + 1)
                    if i < 4:
                        t, q = i // 2, i % 2
                        copy(tokT[:, 4 * q:4 * q + 4, t * P:(t + 1) * P],
                             ps[:, banks[i], :].rearrange("p (j t) -> p j t", j=4)).then_inc(done, 1)
                    else:
                        copy(tokT[:, :, S:TOK],
                             ps[:, banks[i], 0:KT * TS].rearrange("p (j t) -> p j t", j=KT)).then_inc(done, 1)

            for t, (_, n, _) in enumerate(tiles):
                sqrt_of(0, (t,))
                act.wait_ge(norm_ready, t + 1)
                nc.scalar.activation(rows[0:n, t, :], rows[0:n, t, :], ACT.Identity, scale=rstd[0:n, t:t + 1],
                                     bias=shift[0:n, t:t + 1]).then_inc(normed, 1)
            act.wait_ge(ln0T_in, 32)
            act.wait_ge(tokT_ps, 5)
            for j in range(KT):
                last = nc.scalar.activation(tokT[:, j, S:TOK], ps[:, 4, j * TS:(j + 1) * TS], ACT.Identity,
                                            scale=ln0T[:, 0, j:j + 1], bias=ln0T[:, 1, j:j + 1])
            last.then_inc(tokT_sb, 1)

            def take(i):
                c0, w = order[i]
                bank = ps[:, proj_bank(i), :]
                act.wait_ge(proj_ps, i + 1)
                if i in (0, 5):
                    lo, raw = (kiT2, kwT) if i == 0 else (kT2, kvT)
                    for half in range(2):
                        r = slice(half * HEAD_DIM, (half + 1) * HEAD_DIM)
                        copy(lo[r, 0:S], bank[0:HEAD_DIM, 0:S])
                        copy(lo[r, S + PAST:S + PAST + TS], bank[0:HEAD_DIM, S:TOK])
                    copy(raw[0:w, :], bank[0:w, 0:TOK]).then_inc(proj_sb, 1)
                elif i < 5:
                    copy(qiT[:, i - 1, :], bank[:, 0:TOK]).then_inc(proj_sb, 1)
                elif i < 10:
                    copy(qT[:, i - 6, :], bank[:, 0:TOK]).then_inc(proj_sb, 1)
                else:
                    g = i - 10
                    copy(uext[:, g, POOL_PAST:U_S], bank[:, 0:S])
                    copy(uext[:, g, U_S + POOL_PAST:UW], bank[:, S:TOK]).then_inc(proj_sb, 1)

            for i in range(6):
                take(i)
            act.wait_ge(cacheT_ps, 1)
            for half in range(2):
                r = slice(half * HEAD_DIM, (half + 1) * HEAD_DIM)
                copy(kT2[r, S:S + PAST], ps[0:HEAD_DIM, 0, 0:PAST])
                last = copy(kiT2[r, S:S + PAST], ps[HEAD_DIM:P, 0, 0:PAST])
            last.then_inc(cacheT_sb, 1)
            act.wait_ge(kvrow_ps, 1)
            copy(kv_rows[:, 0:2, :], ps[:, 1, 0:2 * (P + KW)].rearrange("p (t n) -> p t n", t=2)).then_inc(kvrow_sb, 1)
            act.wait_ge(kvrow_ps, 2)
            copy(kv_rows[0:TS, 2, :], ps[0:TS, 2, 0:P + KW]).then_inc(kvrow_sb, 1)

            def relu_of(t):
                _, n, nk = tiles[t]
                for pair in range(4):
                    n_pair = 4 * t + pair
                    act.wait_ge(idx_ps, n_pair + 1)
                    if n_pair >= 2:
                        act.wait_ge(idx_used, n_pair - 1)
                    b = n_pair % 2
                    nc.scalar.activation(relu_sb[0:n, b, :, 0:nk], ps[0:n, 2 * b:2 * b + 2, 0:nk],
                                         ACT.Relu).then_inc(idx_relu, 1)

            relu_of(0)
            take(6)
            take(7)
            relu_of(1)
            take(8)
            take(9)
            relu_of(2)
            groups = [0]

            def exp_of(t):
                _, n, nk = tiles[t]
                act.wait_ge(max_ready, t + 1)
                for h in range(N_HEADS):
                    p = probs[0:n, h * nk:(h + 1) * nk]
                    last = nc.scalar.activation(p, p, ACT.Exp, bias=neg_max[0:n, t, h:h + 1],
                                                accum_out=row_sum[0:n, t, h:h + 1])
                last.then_inc(exp_done, 1)

            def probsT_copies(t):
                _, n, nk = tiles[t]
                if t >= 1:
                    act.wait_ge(pv_ps, t)
                for c in range(-(-nk // P)):
                    lw = min(P, nk - c * P)
                    for hg in range(2):
                        act.wait_ge(probsT_ps, groups[0] + 1)
                        at = (c * N_HEADS + 4 * hg) * n
                        copy(probsT[0:lw, at:at + 4 * n], ps[0:lw, 6 + groups[0] % 2, 0:4 * n])\
                            .then_inc(probsT_sb, 1)
                        groups[0] += 1

            def attT_copy(t):
                t0, n, _ = tiles[t]
                act.wait_ge(attT_ps, t + 1)
                copy(tokT[:, 0:4, t0:t0 + n],
                     ps[:, 3, 0:4 * n].rearrange("p (k t) -> p k t", k=4)).then_inc(attT_sb, 1)

            exp_of(0)
            take(10)
            take(11)
            probsT_copies(0)
            exp_of(1)
            take(12)
            take(13)
            act.wait_ge(stateT_ps, 1)
            copy(uext[:, :, U_S:U_S + POOL_PAST],
                 ps[:, 4, 0:4 * POOL_PAST].rearrange("p (g n) -> p g n", g=4)).then_inc(stateT_sb, 1)
            attT_copy(0)
            probsT_copies(1)
            exp_of(2)
            attT_copy(1)
            act.wait_ge(lastu_ps, 1)
            copy(last_u[:, :, :], ps[0:POOL_PAST, 4:6, :]).then_inc(lastu_sb, 1)
            probsT_copies(2)
            sqrt_of(NT, (0,))
            attT_copy(2)
            h1T_banks = (6, 7, 4, 5, 3)
            tokT_copies(h1T_ps, h1T_sb, h1T_banks, (0, 1))
            sqrt_of(NT, (1,))
            tokT_copies(h1T_ps, h1T_sb, h1T_banks, (2, 3))
            sqrt_of(NT, (2,))
            tokT_copies(h1T_ps, h1T_sb, h1T_banks, (4,))
            act.wait_ge(top_ready, 2)
            nc.scalar.activation(expo[:, :, :], shifted[:, :, :], ACT.Exp).then_inc(top_exp, 1)

            def gated_high(done):
                for g in range(2):
                    r = slice(g * BLK, (g + 1) * BLK)
                    nc.scalar.activation(y_sb[0:BLK, g * 512:(g + 1) * 512], ps_y[r, :], ACT.Copy,
                                         scale=gcol[r, :]).then_inc(done, 1)

            act.wait_ge(x_first, 1)
            copy(xT, ps_x).then_inc(x_first_sb, 1)
            act.wait_ge(blocks_ready, 1)
            def expert(e, last=False):
                more = act.value_load(blocks_i[0:1, 0, col(e)], min_val=0, max_val=LAST_BLK - 1)
                with act.If(more > 0):
                    base = act.value_load(blocks_i[0:1, 1, col(e)], min_val=0, max_val=NE * LAST_BLK)
                    with act.Fori(0, more) as i:
                        b = base + i
                        act.wait_ge(x_x_gathered, b + 1)
                        copy(x_xT, ps_x).then_inc(x_xT_ready, 1)
                        act.wait_ge(x_giveT_done, b + 1)
                        copy(x_giveT, x_ps_g[:, 0:TOKP])
                        copy(x_gcol[:, :], x_ps_g[:, TOKP:TOKP + 1]).then_inc(x_giveT_ready, 1)
                        act.wait_ge(x_gate_ready, b + 1)
                        nc.scalar.activation(sig_sb, g_sb, ACT.Sigmoid, scale=SWIGLU_ALPHA).then_inc(x_sig_ready, 1)
                        act.wait_ge(x_hT_done, b + 1)
                        copy(hT, ps_hT.rearrange("p (c h s) -> p c h s", c=4, h=2)).then_inc(x_hT_ready, 1)
                        act.wait_ge(x_y_done, b + 1)
                        act.wait_ge(x_giveT_ready, b + 1)
                        nc.scalar.activation(x_y, ps_y, ACT.Copy, scale=x_gcol[:, :]).then_inc(x_y_ready, 1)
                act.wait_ge(gate_ready, e + 1)
                nc.scalar.activation(sig_sb, g_sb, ACT.Sigmoid, scale=SWIGLU_ALPHA).then_inc(sig_ready, 1)
                if not last:
                    act.wait_ge(x_gathered, e + 2)
                    copy(xT, ps_x).then_inc(xT_ready, 1)
                act.wait_ge(hT_done, e + 1)
                copy(hT, ps_hT.rearrange("p (c h s) -> p c h s", c=4, h=2)).then_inc(hT_ready, 1)
                act.wait_ge(giveT_done, e + 1)
                act.wait_ge(comb_done[2], e + 1)
                copy(giveT[:, :], ps_g[:, 0:TOKP])
                copy(gcol[:, :], ps_g[:, TOKP:TOKP + 1]).then_inc(giveT_ready, 1)
                act.wait_ge(giveT_ready, e + 2)
                act.wait_ge(slot_free[5], e + 1)
                gated_high(y_high)

            expert(0)
            expert(1)
            with act.Fori(2, NE - 1) as e:
                expert(e)
            expert(NE - 1, last=True)
            for t, (_, n, _) in enumerate(tiles):
                sqrt_of(2 * NT, (t,))
                act.wait_ge(norm_ready, NT + t + 1)
                nc.scalar.activation(out_acc[0:n, t, :], out_acc[0:n, t, :], ACT.Identity, scale=rstd[0:n, t:t + 1],
                                     bias=shift[0:n, t:t + 1]).then_inc(normed, 1)
            for t in range(2):
                act.wait_ge(result[t], 1)
                act.dma_start(y_prompt[0, t * P:(t + 1) * P, :], out_acc[:, t, :]).then_inc(final_out, 16)
            act.wait_ge(result[2], 1)
            act.dma_start(y_sample[0], out_acc[0:TS, 2, :]).then_inc(final_out, 16)
            act.wait_ge(final_out, 48)

        @block.vector
        def _(dve):
            v = nc.vector
            step = [0]

            def link(ins):
                step[0] += 1
                ins.then_inc(dve_step, 1)
                dve.wait_ge(dve_step, step[0])

            def layer_norm(t, n, src, base):
                for q in range(2):
                    ins = v.bn_stats(stats[0:n, t, q, :], src[:, q * 512:(q + 1) * 512])
                link(ins)
                link(v.bn_aggr(moments[0:n, t, :], stats[0:n, t, :, :]))
                v.tensor_scalar(veps[0:n, t:t + 1], moments[0:n, t, 1:2], LN_EPS, None, ALU.add).then_inc(var_ready, 1)
                link(v.scalar_tensor_tensor(src, src, moments[0:n, t, 0:1], lnb[0:n, 0, :], ALU.subtract, ALU.mult))
                dve.wait_ge(std_ready, base + t + 1)
                link(v.reciprocal(rstd[0:n, t:t + 1], std[0:n, t:t + 1]))
                v.scalar_tensor_tensor(src, src, rstd[0:n, t:t + 1], lnb[0:n, 1, :], ALU.mult, ALU.add)\
                    .then_inc(ln_done, 1)

            def variance(t, n, src):
                for q in range(2):
                    ins = v.bn_stats(stats[0:n, t, q, :], src[:, q * 512:(q + 1) * 512])
                link(ins)
                link(v.bn_aggr(moments[0:n, t, :], stats[0:n, t, :, :]))
                v.tensor_scalar(veps[0:n, t:t + 1], moments[0:n, t, 1:2], LN_EPS, None, ALU.add).then_inc(var_ready, 1)

            def factors(t, n, base):
                dve.wait_ge(std_ready, base + t + 1)
                link(v.reciprocal(rstd[0:n, t:t + 1], std[0:n, t:t + 1]))
                v.scalar_tensor_tensor(shift[0:n, t:t + 1], moments[0:n, t, 0:1], -1.0, rstd[0:n, t:t + 1],
                                       ALU.mult, ALU.mult).then_inc(norm_ready, 1)

            for t, (_, n, _) in enumerate(tiles):
                dve.wait_ge(x_in[t], 16)
                variance(t, n, rows[0:n, t, :])
                factors(t, n, 0)
            dve.wait_ge(ln0T_in, 32)
            for i in range(4):
                dve.wait_ge(tokT_ps, i + 1)
                t, q = i // 2, i % 2
                for j in range(4 * q, 4 * q + 4):
                    ins = v.tensor_scalar(tokT[:, j, t * P:(t + 1) * P], ps[:, i, (j % 4) * P:(j % 4 + 1) * P],
                                          ln0T[:, 0, j:j + 1], ln0T[:, 1, j:j + 1], ALU.mult, ALU.add)
                ins.then_inc(tokT_sb_v, 1)

            dve.wait_ge(const_ready, 7)
            for g, w in enumerate(WINDOWS):
                ins = v.tensor_scalar(rcount[:, g, :], rcount[:, g, :], float(w), None, ALU.min)
            link(ins)
            link(v.reciprocal(rcount[:, :, :], rcount[:, :, :]))

            dve.wait_ge(bias_in, 6 * 16)
            for part in (1, 2):
                r = slice(0, (3 - part) * NE)
                link(v.tensor_copy(bias_round[r, :], bias_f[r, :]))
                ins = v.tensor_tensor(bias_f[r, :], bias_f[r, :], bias_round[r, :], ALU.subtract)
                if part == 1:
                    link(ins)
            ins.then_inc(bias_left, 1)

            dve.wait_ge(ln_in[0], 32)
            dve.wait_ge(normed, NT)
            dve.wait_ge(tokT_ps, 5)
            for t, (_, n, _) in enumerate(tiles):
                link(v.tensor_tensor(rows[0:n, t, :], rows[0:n, t, :], lnb[0:n, 0, :], ALU.mult))
                v.tensor_tensor(rows[0:n, t, :], rows[0:n, t, :], lnb[0:n, 1, :], ALU.add).then_inc(ln_done, 1)
            dve.wait_ge(ln_done, NT)

            dve.wait_ge(kvrow_sb, 2)
            for t, (_, n, _) in enumerate(tiles):
                ins = v.tensor_scalar(w_idx[0:n, t, :], kv_rows[0:n, t, P + HEAD_DIM:P + KW],
                                      N_HEADS ** -0.5 * HEAD_DIM ** -0.5, None, ALU.mult)
            link(ins)

            def index_scores(t):
                _, n, nk = tiles[t]
                sc = score[0:n, t, 0:nk]
                for pair in range(4):
                    n_pair = 4 * t + pair
                    dve.wait_ge(idx_relu, n_pair + 1)
                    for half in range(2):
                        r, w = relu_sb[0:n, n_pair % 2, half, 0:nk], w_idx[0:n, t, 2 * pair + half:2 * pair + half + 1]
                        if pair == 0 and half == 0:
                            link(v.tensor_scalar(sc, r, w, None, ALU.mult))
                        elif half == 0:
                            link(v.scalar_tensor_tensor(sc, r, w, sc, ALU.mult, ALU.add))
                        else:
                            v.scalar_tensor_tensor(sc, r, w, sc, ALU.mult, ALU.add).then_inc(idx_used, 1)
                            dve.wait_ge(idx_used, n_pair + 1)
                if t < 2:
                    link(v.memset(score[0:CHUNK, t, nk - CHUNK:nk], HIDDEN_KEY))

            def keep_top(t):
                _, n, nk = tiles[t]
                sc = score[0:n, t, 0:nk]
                assert topk[t] % 8 == 0
                for _ in range(topk[t] // 8):
                    link(v.max(max8[0:n, t, :], sc))
                    link(v.match_replace(sc, max8[0:n, t, :], sc, TAKEN))
                link(v.tensor_scalar(sc, sc, TAKEN / 2, HIDDEN_KEY, ALU.is_gt, ALU.mult))

            def mask_logits(t):
                _, n, nk = tiles[t]
                if t >= 1:
                    dve.wait_ge(probsT_ps, [2, 6][t - 1])
                for h in range(N_HEADS):
                    dve.wait_ge(qk_ps, N_HEADS * t + h + 1)
                    v.tensor_tensor_reduce(
                        out=probs[0:n, h * nk:(h + 1) * nk], in0=qk_bank(h)[0:n, 0:nk],
                        in1=score[0:n, t, 0:nk], scale=HEAD_DIM ** -0.5, scalar=TAKEN, op0=ALU.add, op1=ALU.max,
                        accum_out=row_max[0:n, t, h:h + 1]).then_inc(qk_used, 1)
                dve.wait_ge(qk_used, N_HEADS * (t + 1))
                v.tensor_scalar(neg_max[0:n, t, :], row_max[0:n, t, :], -1.0, None, ALU.mult).then_inc(max_ready, 1)

            def normalise(t):
                _, n, _ = tiles[t]
                dve.wait_ge(exp_done, t + 1)
                link(v.reciprocal(row_inv[0:n, t, :], row_sum[0:n, t, :]))
                dve.wait_ge(pv_ps, t + 1)
                if t >= 1:
                    dve.wait_ge(attT_ps, t)
                v.tensor_tensor(att_rows[0:n, :].rearrange("p (h d) -> p h d", h=N_HEADS),
                                ps[0:n, 3, :].rearrange("p (h d) -> p h d", h=N_HEADS),
                                row_inv[0:n, t, :].unsqueeze(2).broadcast_to([n, N_HEADS, HEAD_DIM]),
                                ALU.mult).then_inc(att_ready, 1)

            index_scores(0)
            keep_top(0)
            index_scores(1)
            keep_top(1)
            index_scores(2)
            mask_logits(0)
            keep_top(2)
            normalise(0)
            mask_logits(1)
            normalise(1)
            mask_logits(2)
            dve.wait_ge(pool_step, 4)
            dve.wait_ge(small_in, 64)
            for g, w in enumerate(WINDOWS):
                s = sums_a if g % 2 == 0 else sums_b
                link(v.tensor_tensor(s[:, g, POOL_PAST:POOL_PAST + 16], s[:, g, POOL_PAST:POOL_PAST + 16],
                                     rcount[:, g, :], ALU.mult))
                v.tensor_tensor(diffT[:, g, 0:16], s[:, g, POOL_PAST:POOL_PAST + 16],
                                uext[:, g, POOL_PAST:POOL_PAST + 16], ALU.subtract)
                v.scalar_tensor_tensor(diffT[:, g, 16:S], s[:, g, POOL_PAST + 16:U_S], 1.0 / w,
                                       uext[:, g, POOL_PAST + 16:U_S], ALU.mult, ALU.subtract)
                ins = v.scalar_tensor_tensor(diffT[:, g, S:TOK], s[:, g, U_S + POOL_PAST:UW], 1.0 / w,
                                             uext[:, g, U_S + POOL_PAST:UW], ALU.mult, ALU.subtract)
            ins.then_inc(pool_diff, 1)
            for g in range(4):
                dve.wait_ge(poolmm_ps, g + 1)
                v.tensor_scalar(tokT[:, 4 + g, :], ps[:, 4 + g % 2, 0:TOK], pool_scale_sb[:, g:g + 1], None,
                                ALU.mult).then_inc(poolT_sb, 1)

            def ln1(t):
                _, n, _ = tiles[t]
                dve.wait_ge(wo_ps, t + 1)
                if t < 2:
                    link(v.scalar_tensor_tensor(rows[:, t, :].rearrange("p (h n) -> p h n", h=2),
                                                rows[:, t, :].rearrange("p (h n) -> p h n", h=2), RESIDUAL,
                                                ps[:, 4 * t:4 * t + 2, :], ALU.mult, ALU.add))
                else:
                    for half in range(2):
                        r = rows[0:TS, 2, half * 512:(half + 1) * 512]
                        ins = v.scalar_tensor_tensor(r, r, RESIDUAL, ps[half * TS:(half + 1) * TS, 2, :],
                                                     ALU.mult, ALU.add)
                        link(ins)
                layer_norm(t, n, rows[0:n, t, :], NT)

            dve.wait_ge(ln_in[1], 32)
            ln1(0)
            normalise(2)
            ln1(1)
            ln1(2)

            v.memset(chosen[:, 2, :], 0.0)
            v.memset(chosen_b[:, 2, :], 0.0)
            ins = v.memset(gate_w[:, :, NE:NE + 1], 0.0)
            link(ins)
            link(v.memset(place[:, :, NE:NE + 1], -1.0))

            def choose(ts, n):
                tl = slice(ts[0], ts[-1] + 1)
                dve.wait_ge(router_ps, ts[0] // 2 + 1)
                at = ps[0:n, ts[0] // 2, ts[0] * NE:(ts[-1] + 1) * NE].rearrange("p (t e) -> p t e", t=len(ts))
                link(v.tensor_tensor(logits[0:n, tl, :], at,
                                     b_router_sb[0:n, :].unsqueeze(1).broadcast_to([n, len(ts), NE]), ALU.add))
                for t in ts:
                    ins = v.max(top8[:, t, :], logits[:, t, :])
                link(ins)
                v.tensor_tensor(shifted[:, tl, :], logits[:, tl, :],
                                top8[:, tl, 0:1].broadcast_to([P, len(ts), NE]), ALU.subtract).then_inc(top_ready, 1)
                link(v.memset(top8[:, tl, TOP_K:8], -TAKEN))
                for t in ts:
                    ins = v.match_replace(kept[:, t, :], top8[:, t, :], logits[:, t, :], TAKEN)
                link(ins)
                v.tensor_scalar(chosen_b[0:n, tl, :], kept[0:n, tl, :], TAKEN, None, ALU.is_equal)\
                    .then_inc(gates_ready, 1)
                link(v.tensor_scalar(chosen[0:n, tl, :], kept[0:n, tl, :], TAKEN, None, ALU.is_equal))

            def put(tl, n_tl, earlier):
                link(v.scalar_tensor_tensor(place[:, tl, 0:NE], earlier.rearrange("p (t e) -> p t e", t=n_tl), 1.0,
                                            chosen[:, tl, :], ALU.add, ALU.mult))
                link(v.tensor_scalar(place[:, tl, 0:NE], place[:, tl, 0:NE], -1.0, None, ALU.add))

            first_slots = iota_slot[:, 0:BLK]

            def one_hot(dst, at, slots, n_tiles=NT):
                return v.tensor_tensor(dst,
                                       slots.unsqueeze(1).unsqueeze(1).broadcast_to([P, n_tiles, 2, BLK]),
                                       at.unsqueeze(3).broadcast_to([P, n_tiles, 2, BLK]), ALU.is_equal)

            def select(e):
                v.tensor_copy(sel[:, :], same_exp[:, e].broadcast_to([3 * NE, BLK])).then_inc(sel_ready, 1)

            choose((0, 1), P)
            dve.wait_ge(gates_ready, 1)
            dve.wait_ge(prefix_ps, 1)
            put(slice(0, 2), 2, ps[:, 4, 0:2 * NE])
            one_hot(pick[:, 0:2], place[:, 0:2, 0:1], first_slots, 2).then_inc(pick_first, 1)
            choose((2,), TS)
            dve.wait_ge(gates_ready, 2)
            dve.wait_ge(prefix_ps, 2)
            put(slice(2, 3), 1, ps[:, 5, 0:NE])
            one_hot(pick[:, 2:3], place[:, 2:3, 0:1], first_slots, 1).then_inc(pick_ready, 1)
            select(slice(0, 1))
            count = ps[0:1, 5, NE:2 * NE]
            n_more, n_incl, n_excl = (blocks_f[:, i, :] for i in range(3))
            link(v.tensor_scalar(n_more, count, float(BLK), None, ALU.is_gt))
            for b in range(2, LAST_BLK):
                link(v.scalar_tensor_tensor(n_more, count, float(b * BLK), n_more, ALU.is_gt, ALU.add))
            link(v.tensor_tensor_scan(n_incl, n_more, n_more, 0.0, ALU.add, ALU.bypass))
            link(v.tensor_tensor(n_excl, n_incl, n_more, ALU.subtract))
            v.tensor_copy(blocks_i[:, 0, :], n_more)
            v.tensor_copy(blocks_i[:, 1, :], n_excl).then_inc(blocks_ready, 1)
            dve.wait_ge(x_first_sb, 1)
            dve.wait_ge(x_gathered, 1)
            v.tensor_tensor(xT, xT, ps[:, 3, :].rearrange("p (k s) -> p k s", k=KT), ALU.add).then_inc(xT_ready, 1)
            dve.wait_ge(top_exp, 1)
            link(v.tensor_tensor(weighed[:, :, :], expo[:, :, :], chosen[:, :, :], ALU.mult))
            link(v.tensor_reduce(top_s[:, :], weighed[:, :, :], AX, ALU.add))
            link(v.tensor_scalar(top_s[:, :], top_s[:, :], 1.0, None, ALU.max))
            link(v.reciprocal(top_r[:, :], top_s[:, :]))
            v.tensor_tensor(gate_w[:, :, 0:NE], weighed[:, :, :],
                            top_r[:, :].unsqueeze(2).broadcast_to([P, NT, NE]), ALU.mult).then_inc(gates_ready, 1)
            for t, (_, n, _) in enumerate(tiles):
                v.tensor_scalar(out_acc[0:n, t, :], rows[0:n, t, :], RESIDUAL, None, ALU.mult).then_inc(acc_init, 1)
            dve.wait_ge(acc_init, NT)
            v.tensor_scalar(giveT[:, :], rows[:, 0, 0:TOKP], 0.0, None, ALU.mult).then_inc(giveT_ready, 1)
            v.tensor_scalar(y_sb[:, :], rows[:, 0, :], 0.0, None, ALU.mult).then_inc(y_ready, 1)

            def gated_low(e):
                for g in range(2):
                    r = slice(g * BLK, (g + 1) * BLK)
                    dve.wait_ge(y_high, 2 * e + 1 + g)
                    ins = v.scalar_tensor_tensor(y_sb[BLK:P, g * 512:(g + 1) * 512], ps_y[r, :], gcol[r, :],
                                                 y_sb[0:BLK, g * 512:(g + 1) * 512].bitcast(F32),
                                                 ALU.mult, ALU.subtract)
                ins.then_inc(y_ready, 1)

            def swiglu(gu, gate, sig, up, prod, want, h_out):
                dve.wait_ge(gu, want)
                v.tensor_scalar(g_sb, ps_gu[:, 0, :], LIMIT, None, ALU.min).then_inc(gate, 1)
                v.tensor_scalar(u_sb, ps_gu[:, 1, :], LIMIT, -LIMIT, ALU.min, ALU.max).then_inc(up, 1)
                dve.wait_ge(gate, want)
                dve.wait_ge(up, want)
                v.scalar_tensor_tensor(u_sb, u_sb, 1.0, g_sb, ALU.add, ALU.mult).then_inc(prod, 1)
                dve.wait_ge(prod, want)
                dve.wait_ge(sig, want)
                v.tensor_tensor(h_sb, u_sb, sig_sb, ALU.mult).then_inc(h_out, 1)

            def accumulate(t, comb, want, done, src=ps_c):
                _, n, _ = tiles[t]
                dve.wait_ge(comb, want)
                acc = out_acc[0:n, t, :].rearrange("p (h n) -> p h n", h=2)
                v.tensor_tensor(acc, acc, src[0:n, :, :], ALU.add).then_inc(done, 1)

            dve.wait_ge(blocks_ready, 1)
            def expert(e, last=False):
                more = dve.value_load(blocks_i[0:1, 0, col(e)], min_val=0, max_val=LAST_BLK - 1)
                with dve.If(more > 0):
                    base = dve.value_load(blocks_i[0:1, 1, col(e)], min_val=0, max_val=NE * LAST_BLK)
                    with dve.Fori(0, more) as i:
                        b = base + i
                        slots = iota_slot[:, bass.ds((i + 1) * BLK, BLK)]
                        one_hot(x_pick, place[:, :, col(e)], slots).then_inc(x_pick_ready, 1)
                        swiglu(x_gu_done, x_gate_ready, x_sig_ready, x_up_ready, x_prod_ready, b + 1, x_h_ready)
                        for t in range(NT):
                            accumulate(t, x_comb_done[t], b + 1, x_acc_done[t])
                if not last:
                    dve.wait_ge(giveT_done, e + 1)
                    one_hot(pick, place[:, :, col(e + 1)], first_slots).then_inc(pick_ready, 1)
                swiglu(slot_free[3], gate_ready, sig_ready, up_ready, prod_ready, e + 1, h_ready)
                accumulate(0, comb_done[0], e + 1, acc_done[0])
                accumulate(1, comb_done[1], e + 1, acc_done[1])
                if not last:
                    dve.wait_ge(slot_free[4], e + 1)
                    select(col(e + 1))
                accumulate(2, comb_done[2], e + 1, acc_done[2])
                gated_low(e)

            expert(0)
            expert(1)
            with dve.Fori(2, NE - 1) as e:
                expert(e)
            expert(NE - 1, last=True)
            dve.wait_ge(ln_in[2], 32)

            def sum_up(t):
                n = tiles[t][1]
                accumulate(t, comb_done[t], NE + 1, acc_done[t], src=(ps_c, ps[:, 0:2, :], ps[:, 2:4, :])[t])
                dve.wait_ge(acc_done[t], NE + 1)
                variance(t, n, out_acc[0:n, t, :])

            def gain(t, done):
                n = tiles[t][1]
                dve.wait_ge(normed, NT + t + 1)
                row = out_acc[0:n, t, :]
                v.tensor_tensor(row, row, lnb[0:n, 0, :], ALU.mult).then_inc(done, 1)

            sum_up(0)
            sum_up(1)
            factors(0, P, 2 * NT)
            sum_up(2)
            factors(1, P, 2 * NT)
            gain(0, gained)
            factors(2, TS, 2 * NT)
            gain(1, gained)
            gain(2, gained_last)
            dve.wait_ge(gained_last, 1)
            row = out_acc[0:TS, 2, :]
            v.tensor_tensor(row, row, lnb[0:TS, 1, :], ALU.add).then_inc(result[2], 1)


_INS = ['x_prompt', 'x_sample', 'cache_k', 'cache_v', 'cache_kidx', 'state_pool', 'ln0_g', 'ln0_b', 'w_in', 'w_o',
        'pool_w', 'pool_scale', 'ln1_g', 'ln1_b', 'w_router', 'b_router', 'w1', 'b1', 'w2', 'b2', 'ln2_g', 'ln2_b']
_OUTS = [(1, 256, 1024), (1, 32, 1024), (1, 1, 256, 64), (1, 1, 256, 64), (1, 1, 256, 64), (1, 1, 15, 512),
         (1, 1, 32, 64), (1, 1, 32, 64), (1, 1, 32, 64), (1, 1, 15, 512)]


def kernel(**inputs):
    import numpy as _np
    import concourse.bacc as _bacc
    from concourse import mybir as _mybir
    from concourse.bass_utils import run_bass_kernel_spmd as _run

    nc = _bacc.Bacc("TRN2", target_bir_lowering=False, num_devices=1)
    arrays, ins, outs = {}, [], []
    for name in _INS:
        a = _np.ascontiguousarray(inputs[name])
        arrays[f"in_{name}_dram"] = a
        ins.append(nc.dram_tensor(f"in_{name}_dram", a.shape, _mybir.dt.from_np(a.dtype), kind="ExternalInput").ap())
    for i, shape in enumerate(_OUTS):
        outs.append(nc.dram_tensor(f"out_{i}_dram", shape, _mybir.dt.float32, kind="ExternalOutput").ap())
    encoder_kernel(nc, ins, outs)
    r = _run(nc, [arrays], core_ids=[0])
    return tuple(r.results[0][f"out_{i}_dram"] for i in range(len(_OUTS)))
```
